# Optimizing a Trainium2 kernel written in Bass

```python
import jax, jax.numpy as jnp
from jax import lax
import numpy as np

D_MODEL = 1024
BATCH = 1
SEQ = 4096
DEPTH = 1

CHUNK = 64
MEM_LEN = 256
EPS = 1e-6
NEG_INF = -1e30

GLA_HEADS = 4
GLA_DK = 64
GLA_DV = 128
GLA_LR = 16
GLA_TAU = 16.0
GLA_KW = GLA_HEADS * GLA_DK
GLA_W = GLA_HEADS * GLA_DV

SWA_HEADS = 8
SWA_KV_HEADS = 2
SWA_HD = 64
WINDOW = 128
WIN_CHUNKS = WINDOW // CHUNK
ROPE_DIM = SWA_HD // 4
ROPE_THETA = 500000.0
SWA_W = SWA_HEADS * SWA_HD
SWA_KVW = SWA_KV_HEADS * SWA_HD

XA_HEADS = 4
XA_HD = 64
XA_W = XA_HEADS * XA_HD

D_MIX = GLA_W + SWA_W + XA_W

SPLITS = (GLA_KW, GLA_KW, GLA_W, GLA_W, GLA_LR,
          SWA_W, SWA_KVW, SWA_KVW, SWA_W,
          XA_W, XA_W)
D_IN = sum(SPLITS)

kernel_name = "hymba_gla_swa_sink_memxattn_block"

def rms_norm(x, g):
    xf = x.astype(jnp.float32)
    y = xf * lax.rsqrt(jnp.mean(xf * xf, axis=-1, keepdims=True) + EPS)
    return (y * g.astype(jnp.float32)).astype(x.dtype)

def partial_rope(x, pos):
    half = ROPE_DIM // 2
    inv = 1.0 / (ROPE_THETA ** (jnp.arange(half, dtype=jnp.float32) / half))
    ang = pos.astype(jnp.float32)[..., None] * inv
    c = jnp.cos(ang)[:, :, None, :]
    s = jnp.sin(ang)[:, :, None, :]
    xf = x.astype(jnp.float32)
    x1, x2, rest = xf[..., :half], xf[..., half:ROPE_DIM], xf[..., ROPE_DIM:]
    out = jnp.concatenate([x1 * c - x2 * s, x2 * c + x1 * s, rest], axis=-1)
    return out.astype(x.dtype)

def gla_chunk_causal(q, k, v, log_a):
    B, S, H, dk = q.shape
    dv = v.shape[-1]
    n = S // CHUNK
    rs = lambda t: t.reshape(B, n, CHUNK, H, t.shape[-1]).astype(jnp.float32)
    q, k, v, la = rs(q), rs(k), rs(v), rs(log_a)
    b = jnp.cumsum(la, axis=2)
    b_end = b[:, :, -1]
    k_dec = k * jnp.exp(b_end[:, :, None] - b)
    att = jnp.einsum('bnthk,bnshk->bnhts', q, k_dec)
    intra = jnp.einsum('bnhts,bnshv->bnthv', att, v)
    u = jnp.einsum('bnshk,bnshv->bnhkv', k_dec, v)
    g_end = jnp.exp(b_end)

    def step(state, xs):
        g_c, u_c = xs
        return g_c[..., None] * state + u_c, state

    s0 = jnp.zeros((B, H, dk, dv), jnp.float32)
    _, s_prev = lax.scan(step, s0, (jnp.moveaxis(g_end, 1, 0), jnp.moveaxis(u, 1, 0)))
    inter = jnp.einsum('bnthk,nbhkv->bnthv', q * g_end[:, :, None], s_prev)
    return (intra + inter).reshape(B, S, H, dv)

def swa_with_sinks(q, k, v, sink):
    B, S, Hq, hd = q.shape
    Hkv = k.shape[2]
    G = Hq // Hkv
    n = S // CHUNK
    qb = q.reshape(B, n, CHUNK, Hkv, G, hd)

    def window(t):
        tb = t.reshape(B, n, CHUNK, Hkv, hd)
        tp = jnp.pad(tb, ((0, 0), (WIN_CHUNKS - 1, 0), (0, 0), (0, 0), (0, 0)))
        return jnp.concatenate([tp[:, i:i + n] for i in range(WIN_CHUNKS)], axis=2)

    kw, vw = window(k), window(v)
    key_chunk = (jnp.arange(n)[:, None] - (WIN_CHUNKS - 1)
                 + (jnp.arange(WINDOW) // CHUNK)[None, :])
    valid = key_chunk >= 0
    s = jnp.einsum('bnqhgd,bnkhd->bnhgqk', qb, kw,
                   preferred_element_type=jnp.float32) * (hd ** -0.5)
    s = jnp.where(valid[None, :, None, None, None, :], s, NEG_INF)
    sk = sink.astype(jnp.float32).reshape(1, 1, Hkv, G, 1, 1)
    m = jnp.maximum(jnp.max(s, axis=-1, keepdims=True), sk)
    p = jnp.exp(s - m)
    p = p / (jnp.sum(p, axis=-1, keepdims=True) + jnp.exp(sk - m))
    o = jnp.einsum('bnhgqk,bnkhd->bnqhgd', p.astype(v.dtype), vw)
    return o.reshape(B, S, Hq, hd)

def memory_cross_attention(q, mem, g_mem, w_mem_kv):
    B, M, _ = mem.shape
    kv = rms_norm(mem, g_mem) @ w_mem_kv
    k, v = jnp.split(kv, 2, axis=-1)
    k = k.reshape(B, M, XA_HEADS, XA_HD)
    v = v.reshape(B, M, XA_HEADS, XA_HD)
    s = jnp.einsum('bshd,bmhd->bhsm', q, k,
                   preferred_element_type=jnp.float32) * (XA_HD ** -0.5)
    p = jax.nn.softmax(s, axis=-1).astype(v.dtype)
    return jnp.einsum('bhsm,bmhd->bshd', p, v)

def setup_inputs(seed: int = 0) -> dict:
    key = jax.random.key(seed)
    ks = jax.random.split(key, 13)
    f32 = jnp.float32
    nrm = lambda k, shp: jax.random.normal(k, shp, f32)
    x = nrm(ks[0], (BATCH, SEQ, D_MODEL))
    mem = nrm(ks[1], (BATCH, MEM_LEN, D_MODEL))
    offset = jax.random.randint(ks[2], (BATCH, 1), 0, 4096, dtype=jnp.int32)
    positions = offset + jnp.arange(SEQ, dtype=jnp.int32)[None, :]
    g_norm = 1.0 + 0.02 * nrm(ks[3], (DEPTH, D_MODEL))
    w_in = nrm(ks[4], (DEPTH, D_MODEL, D_IN)) * (D_MODEL ** -0.5)
    w_a2 = nrm(ks[5], (DEPTH, GLA_LR, GLA_KW)) * (GLA_LR ** -0.5)
    b_a = 0.1 * nrm(ks[6], (DEPTH, GLA_KW))
    g_gla = 1.0 + 0.02 * nrm(ks[7], (DEPTH, GLA_DV))
    sinks = 0.5 * nrm(ks[8], (DEPTH, SWA_HEADS))
    g_mem = 1.0 + 0.02 * nrm(ks[9], (DEPTH, D_MODEL))
    w_mem_kv = nrm(ks[10], (DEPTH, D_MODEL, 2 * XA_W)) * (D_MODEL ** -0.5)
    w_out = nrm(ks[11], (DEPTH, D_MIX, D_MODEL)) * (D_MIX ** -0.5)
    g_final = 1.0 + 0.02 * nrm(ks[12], (D_MODEL,))
    return {"x": x, "mem": mem, "positions": positions, "g_norm": g_norm,
            "w_in": w_in, "w_a2": w_a2, "b_a": b_a, "g_gla": g_gla,
            "sinks": sinks, "g_mem": g_mem, "w_mem_kv": w_mem_kv,
            "w_out": w_out, "g_final": g_final}

def reference(x, mem, positions, g_norm, w_in, w_a2, b_a, g_gla, sinks,
              g_mem, w_mem_kv, w_out, g_final):
    B, S, _ = x.shape
    split_idx = np.cumsum(SPLITS)[:-1].tolist()
    for l in range(DEPTH):
        h = rms_norm(x, g_norm[l])
        proj = h @ w_in[l]
        (gq, gk, gv, gz, g_lr, sq, sk, sv, sz, xq, xz) = jnp.split(proj, split_idx, axis=-1)

        log_a = jax.nn.log_sigmoid((g_lr @ w_a2[l] + b_a[l]).astype(jnp.float32)) / GLA_TAU
        o_g = gla_chunk_causal(
            (gq * (GLA_DK ** -0.5)).reshape(B, S, GLA_HEADS, GLA_DK),
            gk.reshape(B, S, GLA_HEADS, GLA_DK),
            gv.reshape(B, S, GLA_HEADS, GLA_DV),
            log_a.reshape(B, S, GLA_HEADS, GLA_DK)).astype(x.dtype)
        o_g = rms_norm(o_g, g_gla[l]).reshape(B, S, GLA_W) * jax.nn.silu(gz)

        q_s = partial_rope(sq.reshape(B, S, SWA_HEADS, SWA_HD), positions)
        k_s = partial_rope(sk.reshape(B, S, SWA_KV_HEADS, SWA_HD), positions)
        o_s = swa_with_sinks(q_s, k_s, sv.reshape(B, S, SWA_KV_HEADS, SWA_HD), sinks[l])
        o_s = o_s.reshape(B, S, SWA_W) * jax.nn.silu(sz)

        o_x = memory_cross_attention(xq.reshape(B, S, XA_HEADS, XA_HD), mem, g_mem[l], w_mem_kv[l])
        o_x = o_x.reshape(B, S, XA_W) * jax.nn.silu(xz)

        x = x + jnp.concatenate([o_g, o_s, o_x], axis=-1) @ w_out[l]
    return rms_norm(x, g_final)


_drawn_inputs = setup_inputs


def setup_inputs(seed=0):
    import zlib

    import numpy as np

    out = dict(_drawn_inputs(seed))
    spreads = {}
    factors = {'g_norm': 4.075,
     'b_a': 3.458,
     'g_gla': 7.617,
     'sinks': 8.0,
     'g_mem': 8.0,
     'g_final': 2.887}
    for name, (base, spread) in spreads.items():
        noise = np.random.default_rng([zlib.crc32(name.encode()), seed]).standard_normal(out[name].shape)
        drawn = base * np.exp(spread * noise) if base else spread * noise
        out[name] = __import__('jax').numpy.asarray(drawn.astype(out[name].dtype))
    for name, factor in factors.items():
        out[name] = (out[name] * factor).astype(out[name].dtype)
    return out
```

```python
from contextlib import ExitStack

import numpy as np

import concourse.bass as bass
from concourse import mybir

F32 = mybir.dt.float32
F16 = mybir.dt.float16
I32 = mybir.dt.int32
ALU = mybir.AluOpType
ACT = mybir.ActivationFunctionType
AX = mybir.AxisListType.X

P = 128
SEQ = 4096
D = 1024
KD = D // P
MEM = 256
MB = MEM // P
CHUNK = 64
EPS = 1e-6
TILES = SEQ // P
NEG = -1e30

GLA_H, GLA_DK, GLA_DV, GLA_LR, GLA_TAU = 4, 64, 128, 16, 16.0
GLA_KW, GLA_W = GLA_H * GLA_DK, GLA_H * GLA_DV
SWA_H, SWA_KV, HD = 8, 2, 64
SWA_W, SWA_KVW = SWA_H * HD, SWA_KV * HD
XA_H = 4
XA_W = XA_H * HD
D_MIX = GLA_W + SWA_W + XA_W
KM = D_MIX // P
ROPE_HALF = HD // 8
ROPE_THETA = 500000.0
SCALE = HD ** -0.5

_names = ("gq", "gk", "gv", "gz", "lr", "sq", "sk", "sv", "sz", "xq", "xz")
_widths = (GLA_KW, GLA_KW, GLA_W, GLA_W, GLA_LR, SWA_W, SWA_KVW, SWA_KVW, SWA_W, XA_W, XA_W)
_starts = dict(zip(_names, np.cumsum((0,) + _widths[:-1]).tolist()))
_width = dict(zip(_names, _widths))
GROUPS = (("sk", "sv", "lr"), ("sq",), ("gq", "gk"), ("xq", "xz"), ("gv",), ("gz",), ("sz",))
KVL, SQ, GQK, XQZ, GV, GZ, SZ = range(len(GROUPS))
NG = len(GROUPS)
GCOLS = [sum(_width[n] for n in g) for g in GROUPS]
GOFF = [KD * c for c in np.cumsum([0] + GCOLS[:-1]).tolist()]
W_WORDS = KD * sum(GCOLS)

X_UP = 1024.0
W_UP = 2.0 ** 14
M_UP = 2.0 ** 14
EXPONENT = 0x7F800000


def two_pi_parts(scale, bits, count):
    left, parts = 2.0 * np.pi * scale, []
    for _ in range(count):
        lsb = 2.0 ** (np.floor(np.log2(left)) - bits + 1)
        parts.append(float(np.floor(left / lsb) * lsb))
        left -= parts[-1]
    return parts


class Tile:

    def __init__(self, m, p):
        self.m, self.p = m, p

    def moved(self, k):
        n = self.p + k
        return Tile(self.m + n // 2, n % 2)

    def index(self):
        return self.m * 2 + self.p

    def done(self, per=1, lag=0):
        return self.m * (2 * per) + per * (self.p + 1 - lag)

    def done_alike(self, per=16):
        return self.m * per + per


def wait(eng, sem, value):
    if isinstance(value, int) and value <= 0:
        return
    eng.wait_ge(sem, value)


def build_kernel(nc, x, mem, pos, g_norm, w_groups, w_a2, b_a, g_gla, sinks, g_mem, w_mem, w_out, g_final, out):
    ctx = ExitStack()
    with ctx:
        def sb(name, shape, dt=F32):
            return ctx.enter_context(nc.sbuf_tensor(name, shape, dt))

        def sem(name):
            return ctx.enter_context(nc.semaphore(name))

        mix_dram = nc.dram_tensor("mix_rows", [SEQ, D_MIX], F32, kind="Internal").ap()

        W = sb("W", [P, W_WORDS])
        scratch = sb("scratch", [P, 8448])
        x_in = sb("x_in", [P, 2, D])
        x_hi = sb("x_hi", [P, D], F16)
        x_lo = sb("x_lo", [P, D], F16)
        hT_hi = sb("hT_hi", [P, 2, D], F16)
        hT_lo = sb("hT_lo", [P, 2, D], F16)
        qkv = sb("qkv", [P, 2, SWA_W + 2 * SWA_KVW + GLA_LR])
        q_pad = sb("q_pad", [P, SWA_H, 2, HD])
        k_win = sb("k_win", [P, 2, SWA_KV, 2, HD])
        v_win = sb("v_win", [P, 2, SWA_KVW])
        kT = sb("kT", [P, SWA_KV, P])
        gqk = sb("gqk", [P, 2, 2 * GLA_KW])
        xq = sb("xq", [P, XA_W])
        xqT = sb("xqT", [P, 2, P])
        gv = sb("gv", [P, GLA_W])
        gates = sb("gates", [P, 2, D_MIX])
        tanh_z = sb("tanh_z", [P, 512])
        lrT = sb("lrT", [32, P])
        wa2 = sb("wa2", [32, GLA_KW])
        la = sb("la", [P, GLA_KW])
        la_e = sb("la_e", [P, GLA_KW])
        decay = sb("decay", [P, GLA_KW])
        state = sb("state", [P, 2, 2, GLA_DV])
        memT_k = sb("memT_k", [P, XA_H, MEM])
        mem_v = sb("mem_v", [P, MB, XA_W])
        ident = sb("ident", [P, P])
        ident16 = sb("ident16", [P, P], F16)
        later = sb("later", [P, P])
        halves = sb("halves", [P, 2])
        rope_t = sb("rope_t", [P, 4, SWA_H + SWA_KV, ROPE_HALF])
        cos_sin = sb("cos_sin", [P, TILES, 2, ROPE_HALF])
        cs = sb("cs", [P, 2, ROPE_HALF])
        small = sb("small", [P, 160])

        used = [0]

        def column(n):
            used[0] += n
            assert used[0] <= 160
            return small[:, used[0] - n:used[0]]

        gn, gm, gg = column(KD), column(KD), column(1)
        minus_half = column(4)
        unscale, unscale_half = column(NG), column(NG)
        w_max, w_max1, w_all, w_pow, w_rec = column(KM), column(1), column(1), column(1), column(1)
        w_scale = column(KM)
        x_ss, x_ms, x_rs = column(1), column(1), column(1)
        s_mx, s_m, s_diff, s_sink, s_den, s_den2, s_rden = (column(SWA_H) for _ in range(7))
        c_mx, c_den, c_rden = (column(XA_H) for _ in range(3))
        g_end = column(4)
        o_ss, o_ms, o_rs, o_rc = (column(GLA_H) for _ in range(4))
        m_amax, m_pow, m_rec, m_scale = (column(1) for _ in range(4))
        m_un, m_un_now = column(2), column(2)
        w_out_un = column(1)
        sink_b = sb("sink_b", [P, SWA_H])

        def room(at, n, *shape):
            v = scratch[:, at:at + n]
            names = "abcd"[:len(shape)]
            return v.rearrange(f"p ({' '.join(names)}) -> p {' '.join(names)}", **dict(zip(names, shape)))

        probs = room(0, 1024, SWA_H, P)
        probsT = room(1024, 1024, SWA_H, P)
        xprobs = room(2048, 1024, XA_H, MEM)
        xprobsT = room(3072, 1024, XA_H * MB, P)
        k_dec = room(4096, 1024, 2, 2, 2, P)
        qT_pad = room(5120, 1024, SWA_H, P)
        gqT = room(6144, 1024, 2, 2, 2, P)
        mix = scratch[:, 7168:8448]
        raw = [scratch[:, 0:4096], scratch[:, 4096:8192]]

        def w_hi(g):
            n = KD * GCOLS[g]
            return W[:, GOFF[g]:GOFF[g] + n // 2].bitcast(F16).rearrange("p (k c) -> p k c", k=KD)

        def w_lo(g):
            n = KD * GCOLS[g]
            return W[:, GOFF[g] + n // 2:GOFF[g] + n].bitcast(F16).rearrange("p (k c) -> p k c", k=KD)

        mem_w = W[:, GOFF[SZ]:GOFF[SZ] + KD * 2 * XA_W].rearrange("p (k c) -> p k c", k=KD)
        mem_in = W[:, GOFF[GZ]:GOFF[GZ] + 2 * D].rearrange("p (b d) -> p b d", b=MB)
        memT = W[:, GOFF[GZ] + 2 * D:GOFF[GZ] + 4 * D].rearrange("p (k m) -> p k m", k=KD)
        wo_raw = W[:, GOFF[SQ]:GOFF[SQ] + KM * D].rearrange("p (k c) -> p k c", k=KM)
        wo_hi = W[:, GOFF[GV]:GOFF[GV] + KM * D // 2].bitcast(F16).rearrange("p (k c) -> p k c", k=KM)
        wo_lo = W[:, GOFF[GV] + KM * D // 2:GOFF[GV] + KM * D].bitcast(F16).rearrange("p (k c) -> p k c", k=KM)
        assert GOFF[SQ] + KM * D <= GOFF[GV] and GOFF[GV] + KM * D <= W_WORDS
        m_in = [scratch[:, b * D_MIX:(b + 1) * D_MIX] for b in range(2)]
        m_hi = scratch[:, 2560:3200].bitcast(F16)
        m_lo = scratch[:, 3200:3840].bitcast(F16)
        mT_hi = [scratch[:, 3840 + 640 * b:4480 + 640 * b].bitcast(F16) for b in range(2)]
        mT_lo = [scratch[:, 5120 + 640 * b:5760 + 640 * b].bitcast(F16) for b in range(2)]
        y = scratch[:, 6400:7424]
        g_fin = scratch[:, 7424:8448]

        def bank(name):
            return ctx.enter_context(nc.psum_tensor(name, [P, 512], F32))

        proj = [bank("proj0"), bank("proj1")]
        turn = [bank("turn0"), bank("turn1")]
        score = [bank("score0"), bank("score1")]
        decay_ps = bank("decay_ps")
        kv_ps = bank("kv_ps")

        sem_names = """ mem_in_s memw_in wout_in gfin_in small_in
            set_up_steps b_chain b_un_now id_zero id_set  later_one later_cut misc_set pads_set pads2_set     ang_done
            ang_abs sin_done cos_done 
            mem_sq mem_ms mem_rs mem_scaled mem_T mem_T_out memk_ps memk_out memv_ps memv_out
              wmax1 wall_s     wscale2_s   w_hi_s w_lo_s
            x_ss_s x_ms_s x_rs_s x_hi_s x_lo_s xT_hi_ps xT_lo_ps hT_hi_s hT_lo_s
            kvl_out sq_out gqk_out tanh_s xz_out xq_out gv_out gz_out sz_out
            cs_s rope_t_s rope_s q_pad_s k_win_s v_win_s
            kT_ps qTa_ps qTb_ps gqT_ps kT_s lrT_s qTa_s qTb_s gqT_s xqT_s
            lr_ps la_abs la_exp la_ln la_s decay_cum decay_s g_end_s k_dec_s
            s_ps s_mx_s s_m_s s_d_s s_diff_s s_exp_s s_sink_s s_den_s s_den2_s s_rden_s s_rdc_s s_gate_s
            x_ps x_mx_s x_d_s x_exp_s x_den_s x_rden_s x_rdc_s x_gate_s
            pTa_ps pTb_ps pTa_s pTb_s xTa_ps xTb_ps xTa_s xTb_s
            kv_done state_s os_ps og_ps ox_ps o_ss_s o_ms_s o_rs_s o_rc_s mix_s mix_out
               wo_cols      b_scale b_un b_hi b_lo bT_hi bT_lo bT_hi_s bT_lo_s
            y_ps0 y_ps1 y_res0 y_res1 y_ss y_ms y_rs y_fin y_out state0"""
        s = {n: sem(n) for n in sem_names.split()}
        assert len(s) == len(sem_names.split())
        w_raw_in = [sem("w_raw_in_even"), sem("w_raw_in_odd")]
        x_in_s = [sem("x_in_even"), sem("x_in_odd")]
        xr_in_s = [sem("xr_in_even"), sem("xr_in_odd")]
        m_in_s = [sem("m_in_even"), sem("m_in_odd")]
        proj_ps = [sem(f"proj_ps{g}") for g in range(NG)]

        def split_through(eng, g):
            eng.wait_ge(s["w_hi_s"], KD * (g + 1))
            eng.wait_ge(s["w_lo_s"], KD * (g + 1))

        block = ctx.enter_context(nc.Block())

        def iterations(eng, body):
            body(Tile(0, 0), project=True, attend=False)
            body(Tile(0, 1), project=True, attend=True, first=True)
            with eng.Fori(1, TILES // 2 - 1) as m:
                body(Tile(m, 0), project=True, attend=True)
                body(Tile(m, 1), project=True, attend=True)
            body(Tile(TILES // 2 - 1, 0), project=True, attend=True)
            body(Tile(TILES // 2 - 1, 1), project=True, attend=True, last=True)
            body(Tile(TILES // 2, 0), project=False, attend=True, last=True)

        def out_iterations(eng, body):
            body(Tile(0, 0), 2)
            body(Tile(0, 1), 2)
            with eng.Fori(1, TILES // 2 - 1) as m:
                body(Tile(m, 0), 2)
                body(Tile(m, 1), 2)
            body(Tile(TILES // 2 - 1, 0), 1)
            body(Tile(TILES // 2 - 1, 1), 0)

        last_reader = {KVL: "kvl_out", SQ: "sq_out", GQK: "gqk_out", XQZ: "xq_out", GV: "gv_out", GZ: "gz_out",
                       SZ: "sz_out"}
        proj_bank = lambda t, g: proj[(t.p + g) % 2]

        @block.sync
        def _(sp):
            sp.dma_start(mem_in, mem.rearrange("(b p) d -> p b d", p=P)).then_inc(s["mem_in_s"], 16)
            sp.dma_start(mem_w, w_mem).then_inc(s["memw_in"], 16)
            sp.dma_start(x_in[:, 0, :], x[0:P, :]).then_inc(x_in_s[0], 16)
            for g in range(NG):
                if g >= 2:
                    split_through(sp, g - 2)
                sp.dma_start(raw[g % 2][:, 0:KD * GCOLS[g]], w_groups[g]).then_inc(w_raw_in[g % 2], 16)
                if g == 0:
                    sp.dma_start(x_in[:, 1, :], x[P:2 * P, :]).then_inc(x_in_s[1], 16)

            def body(n, project, attend, first=False, last=False):
                if project and not last:
                    nxt = n.moved(2)
                    row = sp.snap(nxt.index() * P) if not isinstance(n.m, int) else nxt.index() * P
                    if not (isinstance(n.m, int) and nxt.index() >= TILES):
                        wait(sp, s["x_hi_s"], n.done())
                        sp.wait_ge(s["x_lo_s"], n.done())
                        sp.dma_start(x_in[:, n.p, :], x[bass.ds(row, P), :]).then_inc(x_in_s[n.p], 16)
                if last and project:
                    for g in (SQ, GQK, XQZ):
                        sp.wait_ge(proj_ps[g], TILES)
                    sp.dma_start(wo_raw, w_out).then_inc(s["wout_in"], 16)
                if attend:
                    t = n.moved(-1)
                    row = sp.snap(t.index() * P) if not isinstance(n.m, int) else t.index() * P
                    sp.wait_ge(s["mix_s"], t.done(6))
                    sp.dma_start(mix_dram[bass.ds(row, P), :], mix).then_inc(s["mix_out"], 16)

            iterations(sp, body)

            sp.wait_ge(s["mix_out"], 16 * TILES)
            sp.dma_start(m_in[0], mix_dram[0:P, :]).then_inc(m_in_s[0], 16)
            sp.dma_start(x_in[:, 0, :], x[0:P, :]).then_inc(xr_in_s[0], 16)
            sp.dma_start(m_in[1], mix_dram[P:2 * P, :]).then_inc(m_in_s[1], 16)
            sp.dma_start(x_in[:, 1, :], x[P:2 * P, :]).then_inc(xr_in_s[1], 16)
            sp.dma_start(g_fin, g_final.partition_broadcast(P)).then_inc(s["gfin_in"], 16)

            def out_body(b, more):
                fixed = isinstance(b.m, int)
                nxt = b.moved(2)
                row = b.index() * P if fixed else sp.snap(b.index() * P)
                row2 = nxt.index() * P if fixed else sp.snap(nxt.index() * P)
                if not (fixed and nxt.index() >= TILES):
                    sp.wait_ge(s["b_hi"], b.done())
                    sp.wait_ge(s["b_lo"], b.done())
                    sp.dma_start(m_in[b.p], mix_dram[bass.ds(row2, P), :]).then_inc(m_in_s[b.p], 16)
                    sp.wait_ge(s["y_res0"], b.done())
                    sp.wait_ge(s["y_res1"], b.done())
                    sp.dma_start(x_in[:, b.p, :], x[bass.ds(row2, P), :]).then_inc(xr_in_s[b.p], 16)
                sp.wait_ge(s["y_fin"], b.done())
                sp.dma_start(out[bass.ds(row, P), :], y).then_inc(s["y_out"], 16)

            out_iterations(sp, out_body)
            sp.wait_ge(s["y_out"], 16 * TILES)

        @block.gpsimd
        def _(pool):
            g = nc.gpsimd
            g.memset(ident[:], 0.0).then_inc(s["id_zero"], 1)
            g.memset(later[:], 1.0 / GLA_TAU).then_inc(s["later_one"], 1)
            g.memset(minus_half, -0.5).then_inc(s["misc_set"], 1)
            g.memset(lrT[:], 1.0).then_inc(s["misc_set"], 1)
            g.memset(halves[:], 0.0).then_inc(s["misc_set"], 1)
            g.memset(q_pad[:], 0.0).then_inc(s["misc_set"], 1)
            g.memset(k_win[:], 0.0).then_inc(s["misc_set"], 1)
            g.memset(v_win[:], 0.0).then_inc(s["misc_set"], 1)
            g.memset(state[:], 0.0).then_inc(s["misc_set"], 1)
            g.memset(memT_k[:], 0.0).then_inc(s["misc_set"], 1)
            pool.wait_ge(s["misc_set"], 8)
            g.memset(halves[0:CHUNK, 0:1], 1.0 / GLA_TAU).then_inc(s["pads_set"], 1)
            g.memset(halves[CHUNK:P, 1:2], 1.0 / GLA_TAU).then_inc(s["pads_set"], 1)
            pool.wait_ge(s["pads_set"], 2)
            pool.wait_ge(s["id_zero"], 1)
            g.affine_select(out=ident[:], in_=ident[:], compare_op=ALU.not_equal, fill=1.0, base=0,
                            pattern=[[-1, P]], channel_multiplier=1).then_inc(s["id_set"], 1)
            pool.wait_ge(s["later_one"], 1)
            g.affine_select(out=later[:], in_=later[:], compare_op=ALU.is_gt, fill=0.0, base=0,
                            pattern=[[-1, P]], channel_multiplier=1).then_inc(s["later_cut"], 1)
            pool.wait_ge(s["later_cut"], 1)
            g.memset(later[CHUNK:P, 0:CHUNK], 0.0).then_inc(s["pads_set"], 1)
            pool.wait_ge(s["pads_set"], 3)
            pool.wait_ge(s["id_set"], 1)
            g.tensor_copy(ident16[:], ident[:]).then_inc(s["id_set"], 1)

            for b in range(MB):
                pool.wait_ge(s["mem_ms"], b + 1)
                g.tensor_tensor(m_rec[:, :] if b else m_pow[:, :], m_scale[:, :] if b else m_amax[:, :],
                                minus_half[:, 0:1], ALU.pow).then_inc(s["mem_rs"], 1)

            def row_pow(t):
                pool.wait_ge(s["x_ms_s"], t.done())
                wait(pool, s["x_hi_s"], t.done(lag=1))
                wait(pool, s["x_lo_s"], t.done(lag=1))
                g.tensor_tensor(x_rs, x_ms, minus_half[:, 0:1], ALU.pow).then_inc(s["x_rs_s"], 1)

            def all_max(k):
                pool.wait_ge(s["wmax1"], k + 1)
                g.partition_all_reduce(w_all, w_max1, P, bass.bass_isa.ReduceOp.max).then_inc(s["wall_s"], 1)

            row_pow(Tile(0, 0))
            def body(n, project, attend, first=False, last=False):
                t = n.moved(-1)
                tp = t.p
                if not attend:
                    for k in range(GQK + 3):
                        all_max(k)
                if project:
                    heads = qkv[:, n.p, 0:SWA_W + SWA_KVW].rearrange("p (h d) -> p h d", d=HD)
                    x1, x2 = heads[:, :, 0:ROPE_HALF], heads[:, :, ROPE_HALF:2 * ROPE_HALF]
                    shape = [P, SWA_H + SWA_KV, ROPE_HALF]
                    c = cs[:, 0:1, :].to_broadcast(shape)
                    sn = cs[:, 1:2, :].to_broadcast(shape)
                    pool.wait_ge(s["cs_s"], n.done())
                    pool.wait_ge(s["kvl_out"], n.done())
                    pool.wait_ge(s["sq_out"], n.done())
                    for i, (a, b) in enumerate(((x1, c), (x2, sn), (x2, c), (x1, sn))):
                        g.tensor_tensor(rope_t[:, i], a, b, ALU.mult).then_inc(s["rope_t_s"], 1)
                    pool.wait_ge(s["rope_t_s"], n.done(4))
                    g.tensor_tensor(x1, rope_t[:, 0], rope_t[:, 1], ALU.subtract).then_inc(s["rope_s"], 1)
                    g.tensor_tensor(x2, rope_t[:, 2], rope_t[:, 3], ALU.add).then_inc(s["rope_s"], 1)
                    if not (last and project):
                        row_pow(n.moved(1))
                if not attend:
                    for k in range(GQK + 3, NG):
                        all_max(k)
                    split_through(pool, NG - 1)
                    g.memset(k_dec, 0.0).then_inc(s["pads2_set"], 1)
                    g.memset(gqT, 0.0).then_inc(s["pads2_set"], 1)
                if attend:
                    pool.wait_ge(s["s_rden_s"], t.done())
                    g.tensor_tensor(s_den, s_rden, unscale_half[:, SZ:SZ + 1].to_broadcast([P, SWA_H]), ALU.mult)\
                        .then_inc(s["s_rdc_s"], 1)
                    sg = gates[:, tp, GLA_W:GLA_W + SWA_W].rearrange("p (h d) -> p h d", d=HD)
                    pool.wait_ge(s["s_rdc_s"], t.done())
                    g.tensor_tensor(sg, sg, s_den.unsqueeze(2).to_broadcast([P, SWA_H, HD]), ALU.mult)\
                        .then_inc(s["s_gate_s"], 1)
                    pool.wait_ge(s["x_rden_s"], t.done())
                    g.tensor_tensor(c_den, c_rden, unscale_half[:, XQZ:XQZ + 1].to_broadcast([P, XA_H]), ALU.mult)\
                        .then_inc(s["x_rdc_s"], 1)
                    xg = gates[:, tp, GLA_W + SWA_W:D_MIX].rearrange("p (h d) -> p h d", d=HD)
                    pool.wait_ge(s["x_rdc_s"], t.done())
                    g.tensor_tensor(xg, xg, c_den.unsqueeze(2).to_broadcast([P, XA_H, HD]), ALU.mult)\
                        .then_inc(s["x_gate_s"], 1)
                    pool.wait_ge(s["o_ms_s"], t.done())
                    g.tensor_tensor(o_rs, o_ms, minus_half, ALU.pow).then_inc(s["o_rs_s"], 1)
                    pool.wait_ge(s["o_rs_s"], t.done())
                    g.tensor_tensor(o_rc, o_rs, unscale_half[:, GZ:GZ + 1].to_broadcast([P, GLA_H]), ALU.mult)\
                        .then_inc(s["o_rc_s"], 1)

            iterations(pool, body)
            all_max(NG)

            def out_body(b, more):
                pool.wait_ge(s["y_ms"], b.done())
                g.tensor_tensor(x_rs, x_ms, minus_half[:, 0:1], ALU.pow).then_inc(s["y_rs"], 1)

            out_iterations(pool, out_body)

        @block.scalar
        def _(act):
            a = nc.scalar
            for dst, src in ((gn, g_norm), (gm, g_mem), (gg, g_gla)):
                act.dma_start(dst, src).then_inc(s["small_in"], 16)
            act.dma_start(la_e[:, 0:TILES].bitcast(I32), pos).then_inc(s["small_in"], 16)
            act.dma_start(wa2[0:GLA_LR, :], w_a2).then_inc(s["small_in"], 16)
            act.dma_start(wa2[GLA_LR:GLA_LR + 1, :], b_a).then_inc(s["small_in"], 16)
            act.dma_start(sink_b[:], sinks.partition_broadcast(P)).then_inc(s["small_in"], 16)

            act.wait_ge(s["mem_in_s"], 16)
            for b in range(MB):
                a.activation((x_hi, x_lo)[b][:], mem_in[:, b, :], ACT.Square,
                             accum_out=(s_mx if b == 0 else s_m)[:, 0:1]).then_inc(s["mem_sq"], 1)
            for b in range(MB):
                act.wait_ge(s["mem_rs"], b + 1)
                a.activation(mem_in[:, b, :], mem_in[:, b, :], ACT.Copy, scale=(m_rec if b else m_pow))\
                    .then_inc(s["mem_scaled"], 1)

            def x_square(t):
                act.wait_ge(x_in_s[t.p], t.done_alike())
                wait(act, s["x_ms_s"], t.done(lag=1))
                wait(act, s["xT_hi_ps"], t.done(lag=1))
                a.activation(x_hi[:], x_in[:, t.p, :], ACT.Square, accum_out=x_ss).then_inc(s["x_ss_s"], 1)

            def x_high(t):
                act.wait_ge(s["x_rs_s"], t.done())
                act.wait_ge(s["x_ss_s"], t.done())
                a.activation(x_hi[:], x_in[:, t.p, :], ACT.Copy, scale=x_rs).then_inc(s["x_hi_s"], 1)

            def hT_high(t):
                act.wait_ge(s["xT_hi_ps"], t.done())
                wait(act, proj_ps[SZ], t.done(lag=2))
                a.activation(hT_hi[:, t.p, :], turn[0][:].bitcast(F16), ACT.Copy).then_inc(s["hT_hi_s"], 1)

            act.wait_ge(s["mem_scaled"], 2)
            x_square(Tile(0, 0))
            act.wait_ge(s["ang_done"], 1)
            a.activation(cos_sin[:, :, 1, :], cos_sin[:, :, 1, :], ACT.Sin).then_inc(s["sin_done"], 1)
            act.wait_ge(s["ang_abs"], 2)
            a.activation(cos_sin[:, :, 0, :], cos_sin[:, :, 0, :], ACT.Sin).then_inc(s["cos_done"], 1)
            x_high(Tile(0, 0))
            hT_high(Tile(0, 0))

            for j in range(2):
                act.wait_ge(s["memk_ps"], j + 1)
                for b in range(2):
                    rows = slice(b * HD, (b + 1) * HD)
                    act.wait_ge(s["misc_set"], 8)
                    a.activation(memT_k[rows, 2 * j + b, :], score[j][rows, 0:MEM], ACT.Copy)\
                        .then_inc(s["memk_out"], 1)
            for b in range(MB):
                act.wait_ge(s["memv_ps"], b + 1)
                a.activation(mem_v[:, b, :], score[b][:, 256:256 + XA_W], ACT.Copy).then_inc(s["memv_out"], 1)

            def split_high(g):
                act.wait_ge(s["wscale2_s"], g + 1)
                if g == GZ:
                    act.wait_ge(s["memk_ps"], 2)
                    act.wait_ge(s["memv_ps"], 2)
                r = raw[g % 2][:, 0:KD * GCOLS[g]].rearrange("p (k c) -> p k c", k=KD)
                for k in range(KD):
                    a.activation(w_hi(g)[:, k, :], r[:, k, :], ACT.Copy, scale=w_scale[:, k:k + 1])\
                        .then_inc(s["w_hi_s"], 1)

            def project_out(g, n):
                if g in (SQ,):
                    return
                act.wait_ge(proj_ps[g], n.done())
                ps = proj_bank(n, g)
                if g == KVL:
                    a.activation(qkv[:, n.p, SWA_W:], ps[:, 0:GCOLS[g]], ACT.Copy, scale=unscale[:, g:g + 1])\
                        .then_inc(s["kvl_out"], 1)
                elif g == GQK:
                    a.activation(gqk[:, n.p, :], ps[:], ACT.Copy, scale=unscale[:, g:g + 1])\
                        .then_inc(s["gqk_out"], 1)
                elif g == GV:
                    a.activation(gv[:], ps[:], ACT.Copy, scale=unscale[:, g:g + 1]).then_inc(s["gv_out"], 1)
                else:
                    cols = slice(XA_W, 2 * XA_W) if g == XQZ else slice(0, 512)
                    width = cols.stop - cols.start
                    before = {XQZ: ("sz_out", 1), GZ: ("xz_out", 0), SZ: ("gz_out", 0)}[g]
                    wait(act, s[before[0]], n.done(lag=before[1]))
                    if g == XQZ:
                        wait(act, s["o_ss_s"], n.done(4, lag=2))
                    a.activation(tanh_z[:, 0:width], ps[:, cols], ACT.Tanh, scale=unscale_half[:, g:g + 1])\
                        .then_inc(s["tanh_s"], 1)

            def pad_queries(n):
                act.wait_ge(s["rope_s"], n.done(2))
                act.wait_ge(s["misc_set"], 8)
                wait(act, s["qTa_ps"], n.done(lag=1))
                wait(act, s["qTb_ps"], n.done(lag=1))
                q = qkv[:, n.p, 0:SWA_W].rearrange("p (h d) -> p h d", d=HD)
                for c in range(2):
                    rows = slice(c * CHUNK, (c + 1) * CHUNK)
                    a.activation(q_pad[rows, :, c, :], q[rows], ACT.Copy).then_inc(s["q_pad_s"], 1)

            def body(n, project, attend, first=False, last=False):
                t = n.moved(-1)
                lagged = project and not attend
                if lagged:
                    x_square(n.moved(1))
                    for g in range(NG):
                        split_high(g)
                        if g >= 2:
                            project_out(g - 2, n)
                            if g - 2 == GQK:
                                pad_queries(n)
                                x_high(n.moved(1))
                    project_out(NG - 2, n)
                    project_out(NG - 1, n)
                    hT_high(n.moved(1))
                    return
                more = project and not (last and project)
                if project:
                    project_out(KVL, n)
                act.wait_ge(s["qTa_ps"], t.done())
                wait(act, s["s_ps"], t.done(lag=1))
                if first:
                    split_through(act, NG - 1)
                a.activation(qT_pad[:, 0:4, :], turn[1][:], ACT.Copy).then_inc(s["qTa_s"], 1)
                if more:
                    x_square(n.moved(1))
                act.wait_ge(s["qTb_ps"], t.done())
                a.activation(qT_pad[:, 4:8, :], turn[0][:], ACT.Copy).then_inc(s["qTb_s"], 1)
                act.wait_ge(s["lr_ps"], t.done())
                wait(act, s["la_s"], t.done(lag=1))
                a.activation(la_e[:], decay_ps[:, 0:GLA_KW], ACT.Abs).then_inc(s["la_abs"], 1)
                act.wait_ge(s["la_abs"], t.done())
                a.activation(la_e[:], la_e[:], ACT.Exp, scale=-1.0).then_inc(s["la_exp"], 1)
                act.wait_ge(s["la_exp"], t.done())
                a.activation(la_e[:], la_e[:], ACT.Ln, bias=1.0).then_inc(s["la_ln"], 1)
                if project:
                    project_out(GQK, n)
                    pad_queries(n)
                if more:
                    x_high(n.moved(1))
                act.wait_ge(s["s_d_s"], t.done(2))
                a.activation(probs, probs, ACT.Exp).then_inc(s["s_exp_s"], 1)
                act.wait_ge(s["s_diff_s"], t.done())
                a.activation(s_sink, s_diff, ACT.Exp).then_inc(s["s_sink_s"], 1)
                if project:
                    project_out(XQZ, n)
                act.wait_ge(s["decay_cum"], t.done())
                wait(act, s["k_dec_s"], t.done(2, lag=1))
                a.activation(decay[:], decay_ps[:, 0:GLA_KW], ACT.Exp).then_inc(s["decay_s"], 1)
                wait(act, s["state_s"], t.done(4, lag=1))
                a.activation(g_end, decay_ps[:, GLA_KW:GLA_KW + 4], ACT.Exp).then_inc(s["g_end_s"], 1)
                if more:
                    hT_high(n.moved(1))
                act.wait_ge(s["x_d_s"], t.done(2))
                a.activation(xprobs, xprobs, ACT.Exp, scale=SCALE).then_inc(s["x_exp_s"], 1)
                if project:
                    act.wait_ge(s["kv_done"], t.done())
                    project_out(GV, n)
                act.wait_ge(s["pTa_ps"], t.done())
                wait(act, s["os_ps"], t.done(lag=1))
                a.activation(probsT[:, 0:4, :], turn[0][:], ACT.Copy).then_inc(s["pTa_s"], 1)
                if project:
                    project_out(GZ, n)
                act.wait_ge(s["xTb_ps"], t.done())
                wait(act, s["ox_ps"], t.done(lag=1))
                a.activation(xprobsT[:, 4:8, :], turn[1][:], ACT.Copy).then_inc(s["xTb_s"], 1)
                if project:
                    project_out(SZ, n)
                act.wait_ge(s["og_ps"], t.done())
                wait(act, s["o_ms_s"], t.done(lag=1))
                act.wait_ge(s["sz_out"], n.done() if project else TILES)
                for h in range(GLA_H):
                    a.activation(tanh_z[:, h * GLA_DV:(h + 1) * GLA_DV], score[0][:, h * GLA_DV:(h + 1) * GLA_DV], ACT.Square,
                                 accum_out=o_ss[:, h:h + 1]).then_inc(s["o_ss_s"], 1)

            iterations(act, body)

            act.wait_ge(s["wo_cols"], 2)
            for g in (GV, GZ, SZ):
                act.wait_ge(proj_ps[g], TILES)
            for k in range(KM):
                a.activation(wo_hi[:, k, :], wo_raw[:, k, :], ACT.Copy, scale=w_scale[:, k:k + 1])\
                    .then_inc(s["w_hi_s"], 1)

            def mix_high(b):
                act.wait_ge(s["b_scale"], b.done())
                act.wait_ge(m_in_s[b.p], b.done_alike())
                wait(act, s["bT_hi"], b.done(lag=1))
                a.activation(m_hi, m_in[b.p], ACT.Copy, scale=m_scale).then_inc(s["b_hi"], 1)

            def mixT_high(b):
                act.wait_ge(s["bT_hi"], b.done())
                wait(act, s["y_ps1"], b.done(lag=2))
                a.activation(mT_hi[b.p][:, 0:D], turn[0][:].bitcast(F16), ACT.Copy).then_inc(s["bT_hi_s"], 1)
                a.activation(mT_hi[b.p][:, D:D_MIX], turn[1][:].bitcast(F16)[:, 0:D_MIX - D], ACT.Copy)\
                    .then_inc(s["bT_hi_s"], 1)

            mix_high(Tile(0, 0))
            mixT_high(Tile(0, 0))
            mix_high(Tile(0, 1))

            def out_body(b, more):
                if more:
                    mixT_high(b.moved(1))
                if more == 2:
                    mix_high(b.moved(2))
                act.wait_ge(s["y_res0"], b.done())
                act.wait_ge(s["y_res1"], b.done())
                a.activation(gates[:, 0, 0:D], y, ACT.Square, accum_out=x_ss).then_inc(s["y_ss"], 1)

            out_iterations(act, out_body)

        @block.vector
        def _(dve):
            v = nc.vector

            dve.wait_ge(s["small_in"], 16 * 7)
            steps = [0]

            def step(ins):
                steps[0] += 1
                ins.then_inc(s["set_up_steps"], 1)
                dve.wait_ge(s["set_up_steps"], steps[0])

            posf = la[:, 0:TILES]
            ang = cos_sin[:, :, 1, :]
            turns_f = gates[:, 0, 0:TILES * ROPE_HALF].rearrange("p (t j) -> p t j", j=ROPE_HALF)
            turns_i = gates[:, 1, 0:TILES * ROPE_HALF].bitcast(I32).rearrange("p (t j) -> p t j", j=ROPE_HALF)
            step(v.tensor_copy(posf, la_e[:, 0:TILES].bitcast(I32)))
            inv = np.float32(1.0) / np.power(np.float32(ROPE_THETA),
                                             np.arange(ROPE_HALF, dtype=np.float32) / np.float32(ROPE_HALF))
            for j in range(ROPE_HALF):
                step(v.tensor_scalar(ang[:, :, j:j + 1], posf.unsqueeze(2), float(inv[j]), None, ALU.mult))
            for scale, bits, count in ((4096.0, 7, 6), (1.0, 11, 4)):
                step(v.tensor_scalar(turns_i, ang, float(1.0 / (2.0 * np.pi * scale)), None, ALU.mult))
                step(v.tensor_copy(turns_f, turns_i))
                for part in two_pi_parts(scale, bits, count):
                    step(v.scalar_tensor_tensor(out=ang, in0=turns_f, scalar=-part, in1=ang, op0=ALU.mult,
                                                op1=ALU.add))
            step(v.tensor_scalar(ang, ang, float(np.float32(3.1415925)), float(np.float32(-3.1415925)),
                                 ALU.min, ALU.max))
            step(v.tensor_scalar(turns_f, ang, -1.0, None, ALU.mult))
            v.tensor_tensor(cos_sin[:, :, 0, :], turns_f, ang, ALU.max).then_inc(s["ang_abs"], 1)
            dve.wait_ge(s["ang_abs"], 1)
            v.tensor_scalar(cos_sin[:, :, 0, :], cos_sin[:, :, 0, :], -1.0, float(np.pi / 2), ALU.mult, ALU.add)\
                .then_inc(s["ang_abs"], 1)
            dve.wait_ge(s["ang_abs"], 2)
            v.tensor_copy(turns_f, ang).then_inc(s["ang_done"], 1)

            for b in range(MB):
                dve.wait_ge(s["mem_sq"], b + 1)
                v.tensor_scalar(m_scale if b else m_amax, (s_mx if b == 0 else s_m)[:, 0:1], 1.0 / D, EPS,
                                ALU.mult, ALU.add).then_inc(s["mem_ms"], 1)

            def x_mean(t):
                dve.wait_ge(s["x_ss_s"], t.done())
                wait(dve, s["x_rs_s"], t.done(lag=1))
                v.tensor_scalar(x_ms, x_ss, 1.0 / D / X_UP ** 2, EPS / X_UP ** 2, ALU.mult, ALU.add)\
                    .then_inc(s["x_ms_s"], 1)

            def x_low(t):
                dve.wait_ge(s["x_rs_s"], t.done())
                dve.wait_ge(s["x_hi_s"], t.done())
                wait(dve, s["xT_lo_ps"], t.done(lag=1))
                v.scalar_tensor_tensor(out=x_lo[:], in0=x_in[:, t.p, :], scalar=x_rs, in1=x_hi[:], op0=ALU.mult,
                                       op1=ALU.subtract).then_inc(s["x_lo_s"], 1)

            def hT_low(t):
                dve.wait_ge(s["xT_lo_ps"], t.done())
                wait(dve, proj_ps[SZ], t.done(lag=2))
                v.tensor_copy(hT_lo[:, t.p, :], turn[1][:].bitcast(F16)).then_inc(s["hT_lo_s"], 1)

            x_mean(Tile(0, 0))
            x_low(Tile(0, 0))
            for k in range(KD):
                for b in range(MB):
                    i = k * MB + b
                    dve.wait_ge(s["mem_T"], i // 4 + 1)
                    bk = (turn + score)[(i // 4) % 4]
                    v.tensor_scalar(memT[:, k, b * P:(b + 1) * P], bk[:, (i % 4) * P:(i % 4 + 1) * P],
                                    gm[:, k:k + 1], None, ALU.mult).then_inc(s["mem_T_out"], 1)
            hT_low(Tile(0, 0))

            def power_scale(k):
                dve.wait_ge(s["wall_s"], k + 1)
                step(v.tensor_scalar(w_all, w_all, 1e-20, None, ALU.max))
                step(v.tensor_scalar(w_pow.bitcast(I32), w_all.bitcast(I32), EXPONENT, None, ALU.bitwise_and))
                step(v.reciprocal(w_rec, w_pow))

            def split_low(g):
                r = raw[g % 2][:, 0:KD * GCOLS[g]].rearrange("p (k c) -> p k c", k=KD)
                dve.wait_ge(w_raw_in[g % 2], 16 * (g // 2 + 1))
                step(v.tensor_reduce(w_max[:, 0:KD], r, AX, ALU.max, apply_absolute_value=True))
                step(v.tensor_tensor(w_max[:, 0:KD], w_max[:, 0:KD], gn, ALU.mult))
                v.tensor_reduce(w_max1, w_max[:, 0:KD], AX, ALU.max, apply_absolute_value=True)\
                    .then_inc(s["wmax1"], 1)
                power_scale(g)
                if g:
                    dve.wait_ge(s["w_hi_s"], KD * g)
                step(v.tensor_scalar(unscale[:, g:g + 1], w_pow, 1.0 / W_UP / X_UP, None, ALU.mult))
                step(v.tensor_scalar(unscale_half[:, g:g + 1], w_pow, 0.5 / W_UP / X_UP, None, ALU.mult))
                v.tensor_scalar(w_scale[:, 0:KD], gn, w_rec, W_UP, ALU.mult, ALU.mult).then_inc(s["wscale2_s"], 1)
                dve.wait_ge(s["wscale2_s"], g + 1)
                for k in range(KD):
                    dve.wait_ge(s["w_hi_s"], KD * g + k + 1)
                    v.scalar_tensor_tensor(out=w_lo(g)[:, k, :], in0=r[:, k, :], scalar=w_scale[:, k:k + 1],
                                           in1=w_hi(g)[:, k, :], op0=ALU.mult, op1=ALU.subtract)\
                        .then_inc(s["w_lo_s"], 1)

            def project_out(g, n):
                ps = proj_bank(n, g)
                if g == SQ:
                    dve.wait_ge(proj_ps[g], n.done())
                    v.tensor_scalar(qkv[:, n.p, 0:SWA_W], ps[:], unscale[:, g:g + 1], None, ALU.mult)\
                        .then_inc(s["sq_out"], 1)
                elif g in (XQZ, GZ, SZ):
                    dve.wait_ge(s["tanh_s"], n.done(3) - {XQZ: 2, GZ: 1, SZ: 0}[g])
                    cols, at, name = {XQZ: (slice(XA_W, 2 * XA_W), GLA_W + SWA_W, "xz_out"),
                                      GZ: (slice(0, 512), 0, "gz_out"), SZ: (slice(0, 512), GLA_W, "sz_out")}[g]
                    width = cols.stop - cols.start
                    v.scalar_tensor_tensor(out=gates[:, n.p, at:at + width], in0=tanh_z[:, 0:width], scalar=1.0,
                                           in1=ps[:, cols], op0=ALU.add, op1=ALU.mult).then_inc(s[name], 1)
                    if g == XQZ:
                        wait(dve, s["gqT_ps"], n.done(lag=1))
                        v.tensor_scalar(xq[:], ps[:, 0:XA_W], unscale[:, g:g + 1], None, ALU.mult)\
                            .then_inc(s["xq_out"], 1)

            def tile_cos_sin(n):
                wait(dve, s["rope_t_s"], n.done(4, lag=1))
                v.tensor_scalar(cs[:], cos_sin[:, bass.ds(n.index(), 1)], 1.0, None, ALU.mult)\
                    .then_inc(s["cs_s"], 1)

            def pad_keys(n):
                dve.wait_ge(s["rope_s"], n.done(2))
                dve.wait_ge(s["misc_set"], 8)
                wait(dve, s["kT_ps"], n.done(lag=1))
                k = qkv[:, n.p, SWA_W:SWA_W + SWA_KVW].rearrange("p (h d) -> p h d", d=HD)
                v.tensor_copy(k_win[:, n.p, :, 1, :], k).then_inc(s["k_win_s"], 1)
                v.tensor_copy(k_win[0:CHUNK, n.p, :, 0, :], k[0:CHUNK]).then_inc(s["k_win_s"], 1)
                v.tensor_copy(k_win[CHUNK:P, 1 - n.p, :, 0, :], k[CHUNK:P]).then_inc(s["k_win_s"], 1)

            def pad_values(n):
                wait(dve, s["os_ps"], n.done(lag=1))
                dve.wait_ge(s["kvl_out"], n.done())
                dve.wait_ge(s["misc_set"], 8)
                val = qkv[:, n.p, SWA_W + SWA_KVW:SWA_W + 2 * SWA_KVW]
                v.tensor_copy(v_win[0:CHUNK, n.p, :], val[0:CHUNK]).then_inc(s["v_win_s"], 1)
                v.tensor_copy(v_win[CHUNK:P, 1 - n.p, :], val[CHUNK:P]).then_inc(s["v_win_s"], 1)

            def body(n, project, attend, first=False, last=False):
                t = n.moved(-1)
                tp = t.p
                if not attend:
                    dve.wait_ge(s["cos_done"], 1)
                    dve.wait_ge(s["sin_done"], 1)
                    tile_cos_sin(n)
                    x_mean(n.moved(1))
                    for g in range(NG):
                        split_low(g)
                        if g >= 2:
                            project_out(g - 2, n)
                            if g - 2 == GQK:
                                pad_keys(n)
                                x_low(n.moved(1))
                    project_out(NG - 2, n)
                    project_out(NG - 1, n)
                    hT_low(n.moved(1))
                    pad_values(n)
                    return
                more = project and not (last and project)
                if project:
                    tile_cos_sin(n)
                dve.wait_ge(s["kT_ps"], t.done())
                wait(dve, s["s_ps"], t.done(lag=1))
                v.tensor_copy(kT[:].rearrange("p a b -> p (a b)"), turn[0][:, 0:2 * P]).then_inc(s["kT_s"], 1)
                wait(dve, s["lr_ps"], t.done(lag=1))
                v.tensor_copy(lrT[0:GLA_LR, :], turn[0][0:GLA_LR, 2 * P:3 * P]).then_inc(s["lrT_s"], 1)
                if project:
                    project_out(SQ, n)
                dve.wait_ge(s["gqT_ps"], t.done())
                wait(dve, s["og_ps"], t.done(lag=1))
                if first:
                    dve.wait_ge(s["pads2_set"], 2)
                for b in range(2):
                    rows = slice(b * GLA_DK, (b + 1) * GLA_DK)
                    v.tensor_scalar(gqT[rows, :, b].rearrange("p a c (h t) -> p a (c h) t", h=2)[:, :, 0:4:3],
                                    turn[1][rows, 0:2 * P].rearrange("p (a c t) -> p a c t", a=2, c=2),
                                    GLA_DK ** -0.5, None, ALU.mult).then_inc(s["gqT_s"], 1)
                wait(dve, s["x_ps"], t.done(lag=1))
                v.tensor_copy(xqT[:].rearrange("p a b -> p (a b)"), turn[1][:, 2 * P:4 * P]).then_inc(s["xqT_s"], 1)
                if more:
                    x_mean(n.moved(1))
                dve.wait_ge(s["la_ln"], t.done())
                wait(dve, s["decay_cum"], t.done(lag=1))
                v.scalar_tensor_tensor(out=la[:], in0=decay_ps[:, 0:GLA_KW], scalar=0.0, in1=la_e[:], op0=ALU.min,
                                       op1=ALU.subtract).then_inc(s["la_s"], 1)
                if project:
                    pad_keys(n)
                dve.wait_ge(s["s_ps"], t.done())
                if first:
                    for b in range(2):
                        v.memset(score[b][0:CHUNK, :].rearrange("p (h k) -> p h k", h=4)[:, :, CHUNK:P], NEG)\
                            .then_inc(s["state0"], 1)
                    dve.wait_ge(s["state0"], 2)
                for b in range(2):
                    v.tensor_reduce(s_mx[:, 4 * b:4 * b + 4], score[b][:].rearrange("p (h k) -> p h k", h=4), AX,
                                    ALU.max).then_inc(s["s_mx_s"], 1)
                dve.wait_ge(s["s_mx_s"], t.done(2))
                v.scalar_tensor_tensor(out=s_m, in0=s_mx, scalar=SCALE, in1=sink_b[:], op0=ALU.mult, op1=ALU.max)\
                    .then_inc(s["s_m_s"], 1)
                dve.wait_ge(s["s_m_s"], t.done())
                wait(dve, s["pTa_ps"], t.done(lag=1))
                wait(dve, s["pTb_ps"], t.done(lag=1))
                for b in range(2):
                    v.scalar_tensor_tensor(out=probs[:, 4 * b:4 * b + 4, :],
                                           in0=score[b][:].rearrange("p (h k) -> p h k", h=4), scalar=SCALE,
                                           in1=s_m[:, 4 * b:4 * b + 4].unsqueeze(2).to_broadcast([P, 4, P]),
                                           op0=ALU.mult, op1=ALU.subtract).then_inc(s["s_d_s"], 1)
                wait(dve, s["s_sink_s"], t.done(lag=1))
                v.tensor_tensor(s_diff, sink_b[:], s_m, ALU.subtract).then_inc(s["s_diff_s"], 1)
                if more:
                    x_low(n.moved(1))
                dve.wait_ge(s["s_exp_s"], t.done())
                wait(dve, s["s_gate_s"], t.done(lag=1))
                v.tensor_reduce(s_den2, probs, AX, ALU.add).then_inc(s["s_den_s"], 1)
                dve.wait_ge(s["s_den_s"], t.done())
                dve.wait_ge(s["s_sink_s"], t.done())
                v.tensor_tensor(s_den2, s_den2, s_sink, ALU.add).then_inc(s["s_den2_s"], 1)
                dve.wait_ge(s["s_den2_s"], t.done())
                if project:
                    project_out(XQZ, n)
                if more:
                    hT_low(n.moved(1))
                dve.wait_ge(s["decay_s"], t.done())
                dve.wait_ge(s["gqk_out"], t.done())
                wait(dve, s["kv_done"], t.done(lag=1))
                for c in range(2):
                    rows = slice(c * CHUNK, (c + 1) * CHUNK)
                    v.tensor_tensor(
                        k_dec[rows, c].rearrange("p a b (h d) -> p a (b h) d", h=2)[:, :, 0:4:3],
                        gqk[rows, tp, GLA_KW:2 * GLA_KW].rearrange("p (a b d) -> p a b d", a=2, b=2),
                        decay[rows].rearrange("p (a b d) -> p a b d", a=2, b=2), ALU.mult)\
                        .then_inc(s["k_dec_s"], 1)
                dve.wait_ge(s["x_ps"], t.done())
                for b in range(2):
                    v.tensor_reduce(c_mx[:, 2 * b:2 * b + 2], score[b][:].rearrange("p (h k) -> p h k", h=2), AX,
                                    ALU.max).then_inc(s["x_mx_s"], 1)
                dve.wait_ge(s["x_mx_s"], t.done(2))
                wait(dve, s["xTa_ps"], t.done(lag=1))
                wait(dve, s["xTb_ps"], t.done(lag=1))
                for b in range(2):
                    v.tensor_tensor(xprobs[:, 2 * b:2 * b + 2, :], score[b][:].rearrange("p (h k) -> p h k", h=2),
                                    c_mx[:, 2 * b:2 * b + 2].unsqueeze(2).to_broadcast([P, 2, MEM]),
                                    ALU.subtract).then_inc(s["x_d_s"], 1)
                v.reciprocal(s_rden, s_den2).then_inc(s["s_rden_s"], 1)
                dve.wait_ge(s["pTb_ps"], t.done())
                wait(dve, s["os_ps"], t.done(lag=1))
                v.tensor_copy(probsT[:, 4:8, :].rearrange("p a b -> p (a b)"), turn[1][:]).then_inc(s["pTb_s"], 1)
                dve.wait_ge(s["kv_done"], t.done())
                dve.wait_ge(s["g_end_s"], t.done())
                wait(dve, s["og_ps"], t.done(lag=1))
                for c in range(2):
                    for j in range(2):
                        if c or not first:
                            dve.wait_ge(s["state_s"], (t.done(4) - 2) if c else t.done(4, lag=1))
                        v.scalar_tensor_tensor(out=state[:, c, j, :], in0=state[:, 1 - c, j, :],
                                               scalar=g_end[:, 2 * j + c:2 * j + c + 1],
                                               in1=kv_ps[:, (2 * c + j) * GLA_DV:(2 * c + j + 1) * GLA_DV],
                                               op0=ALU.mult, op1=ALU.add).then_inc(s["state_s"], 1)
                dve.wait_ge(s["x_exp_s"], t.done())
                wait(dve, s["x_gate_s"], t.done(lag=1))
                v.tensor_reduce(c_mx, xprobs, AX, ALU.add).then_inc(s["x_den_s"], 1)
                dve.wait_ge(s["x_den_s"], t.done())
                v.reciprocal(c_rden, c_mx).then_inc(s["x_rden_s"], 1)
                if project:
                    project_out(GZ, n)
                dve.wait_ge(s["xTa_ps"], t.done())
                wait(dve, s["ox_ps"], t.done(lag=1))
                v.tensor_copy(xprobsT[:, 0:4, :].rearrange("p a b -> p (a b)"), turn[0][:]).then_inc(s["xTa_s"], 1)
                if project:
                    project_out(SZ, n)
                wait(dve, s["mix_out"], t.done(16, lag=1))
                dve.wait_ge(s["os_ps"], t.done())
                dve.wait_ge(s["s_gate_s"], t.done())
                v.tensor_tensor(mix[:, GLA_W:GLA_W + SWA_W], score[1][:], gates[:, tp, GLA_W:GLA_W + SWA_W],
                                ALU.mult).then_inc(s["mix_s"], 1)
                dve.wait_ge(s["o_ss_s"], t.done(4))
                wait(dve, s["o_rs_s"], t.done(lag=1))
                v.tensor_scalar(o_ms, o_ss, 1.0 / GLA_DV, EPS, ALU.mult, ALU.add).then_inc(s["o_ms_s"], 1)
                dve.wait_ge(s["ox_ps"], t.done())
                dve.wait_ge(s["x_gate_s"], t.done())
                v.tensor_tensor(mix[:, GLA_W + SWA_W:D_MIX], decay_ps[:, 0:XA_W], gates[:, tp, GLA_W + SWA_W:D_MIX],
                                ALU.mult).then_inc(s["mix_s"], 1)
                dve.wait_ge(s["o_rc_s"], t.done())
                for h in range(GLA_H):
                    cols = slice(h * GLA_DV, (h + 1) * GLA_DV)
                    v.scalar_tensor_tensor(out=mix[:, cols], in0=score[0][:, cols], scalar=o_rc[:, h:h + 1],
                                           in1=gates[:, tp, cols], op0=ALU.mult, op1=ALU.mult)\
                        .then_inc(s["mix_s"], 1)
                if project:
                    pad_values(n)

            iterations(dve, body)

            dve.wait_ge(s["wout_in"], 16)
            step(v.tensor_reduce(w_max, wo_raw, AX, ALU.max, apply_absolute_value=True))
            step(v.tensor_scalar(w_max[:, 0:GLA_H], w_max[:, 0:GLA_H], gg, None, ALU.mult))
            v.tensor_reduce(w_max1, w_max, AX, ALU.max, apply_absolute_value=True).then_inc(s["wmax1"], 1)
            power_scale(NG)
            v.tensor_scalar(w_scale[:, 0:KM], minus_half[:, 0:1].to_broadcast([P, KM]), w_rec, -2.0 * W_UP,
                            ALU.mult, ALU.mult).then_inc(s["wo_cols"], 1)
            dve.wait_ge(s["wo_cols"], 1)
            v.tensor_scalar(w_scale[:, 0:GLA_H], w_scale[:, 0:GLA_H], gg, None, ALU.mult).then_inc(s["wo_cols"], 1)
            step(v.tensor_scalar(w_out_un, w_pow, 1.0 / W_UP / M_UP, None, ALU.mult))
            dve.wait_ge(s["wo_cols"], 2)

            def mix_low(b):
                dve.wait_ge(m_in_s[b.p], b.done_alike())
                wait(dve, s["b_hi"], b.done(lag=1))
                wait(dve, s["b_lo"], b.done(lag=1))
                v.tensor_reduce(m_amax, m_in[b.p], AX, ALU.max, apply_absolute_value=True).then_inc(s["b_chain"], 1)
                dve.wait_ge(s["b_chain"], b.done(4) - 3)
                v.tensor_scalar(m_amax, m_amax, 1e-20, None, ALU.max).then_inc(s["b_chain"], 1)
                dve.wait_ge(s["b_chain"], b.done(4) - 2)
                v.tensor_scalar(m_pow.bitcast(I32), m_amax.bitcast(I32), EXPONENT, None, ALU.bitwise_and)\
                    .then_inc(s["b_chain"], 1)
                dve.wait_ge(s["b_chain"], b.done(4) - 1)
                v.reciprocal(m_rec, m_pow).then_inc(s["b_chain"], 1)
                dve.wait_ge(s["b_chain"], b.done(4))
                v.tensor_scalar(m_scale, m_rec, M_UP, None, ALU.mult).then_inc(s["b_scale"], 1)
                wait(dve, s["b_un_now"], b.done(lag=2))
                v.tensor_scalar(m_un[:, b.p:b.p + 1], m_pow, w_out_un, None, ALU.mult).then_inc(s["b_un"], 1)
                dve.wait_ge(s["b_hi"], b.done())
                wait(dve, s["bT_lo"], b.done(lag=1))
                v.scalar_tensor_tensor(out=m_lo, in0=m_in[b.p], scalar=m_scale, in1=m_hi, op0=ALU.mult,
                                       op1=ALU.subtract).then_inc(s["b_lo"], 1)

            def mixT_low(b):
                dve.wait_ge(s["bT_lo"], b.done())
                wait(dve, s["y_ps1"], b.done(lag=2))
                v.tensor_copy(mT_lo[b.p][:, 0:D], score[0][:].bitcast(F16)).then_inc(s["bT_lo_s"], 1)
                v.tensor_copy(mT_lo[b.p][:, D:D_MIX], score[1][:].bitcast(F16)[:, 0:D_MIX - D])\
                    .then_inc(s["bT_lo_s"], 1)

            for k in range(KM):
                dve.wait_ge(s["w_hi_s"], KD * NG + k + 1)
                v.scalar_tensor_tensor(out=wo_lo[:, k, :], in0=wo_raw[:, k, :], scalar=w_scale[:, k:k + 1],
                                       in1=wo_hi[:, k, :], op0=ALU.mult, op1=ALU.subtract).then_inc(s["w_lo_s"], 1)
            mix_low(Tile(0, 0))
            mixT_low(Tile(0, 0))
            mix_low(Tile(0, 1))

            def out_body(b, more):
                un = m_un_now[:, b.p:b.p + 1]
                dve.wait_ge(s["b_un"], b.done())
                v.tensor_copy(un, m_un[:, b.p:b.p + 1]).then_inc(s["b_un_now"], 1)
                dve.wait_ge(s["b_un_now"], b.done())
                dve.wait_ge(xr_in_s[b.p], b.done_alike())
                wait(dve, s["y_out"], b.done(16, lag=1))
                for h in range(2):
                    dve.wait_ge(s[f"y_ps{h}"], b.done())
                    ps = (proj if h == 0 else (decay_ps, kv_ps))[b.p]
                    cols = slice(h * 512, (h + 1) * 512)
                    v.scalar_tensor_tensor(out=y[:, cols], in0=ps[:], scalar=un, in1=x_in[:, b.p, cols],
                                           op0=ALU.mult, op1=ALU.add).then_inc(s[f"y_res{h}"], 1)
                    if more and h == 0:
                        mixT_low(b.moved(1))
                    if more == 2 and h == 0:
                        mix_low(b.moved(2))
                dve.wait_ge(s["y_ss"], b.done())
                v.tensor_scalar(x_ms, x_ss, 1.0 / D, EPS, ALU.mult, ALU.add).then_inc(s["y_ms"], 1)
                dve.wait_ge(s["y_rs"], b.done())
                if not isinstance(b.m, int) or b.index() < 2:
                    dve.wait_ge(s["gfin_in"], 16)
                v.scalar_tensor_tensor(out=y, in0=y, scalar=x_rs, in1=g_fin, op0=ALU.mult, op1=ALU.mult)\
                    .then_inc(s["y_fin"], 1)

            out_iterations(dve, out_body)

        @block.tensor
        def _(pe):
            t_ = nc.tensor

            def mm(o, l, r, first, last):
                return t_.matmul(o, lhsT=l, rhs=r, start=first, stop=last)

            def x_turn(t):
                for half, bk, ready, done in ((x_hi, turn[0], "x_hi_s", "xT_hi_ps"), (x_lo, turn[1], "x_lo_s", "xT_lo_ps")):
                    pe.wait_ge(s[ready], t.done())
                    for k in range(KD):
                        i = t_.transpose(bk[:].bitcast(F16)[:, k * P:(k + 1) * P], half[:, k * P:(k + 1) * P], ident16[:])
                    i.then_inc(s[done], 1)

            def project(g, n):
                pe.wait_ge(s["hT_hi_s"], n.done())
                pe.wait_ge(s["hT_lo_s"], n.done())
                ps = proj_bank(n, g)[:, 0:GCOLS[g]]
                two_back = (g - 2) % NG
                wait(pe, s[last_reader[two_back]], n.done(lag=1 if g < 2 else 0))
                for k in range(KD):
                    hi = hT_hi[:, n.p, k * P:(k + 1) * P]
                    lo = hT_lo[:, n.p, k * P:(k + 1) * P]
                    mm(ps, hi, w_hi(g)[:, k, :], k == 0, False)
                    mm(ps, hi, w_lo(g)[:, k, :], False, False)
                    i = mm(ps, lo, w_hi(g)[:, k, :], False, k == KD - 1)
                i.then_inc(proj_ps[g], 1)

            pe.wait_ge(s["id_set"], 2)
            pe.wait_ge(s["mem_scaled"], 2)
            for k in range(KD):
                for b in range(MB):
                    i = k * MB + b
                    bk = (turn + score)[(i // 4) % 4]
                    ins = t_.transpose(bk[:, (i % 4) * P:(i % 4 + 1) * P], mem_in[:, b, k * P:(k + 1) * P], ident[:])
                    if i % 4 == 3:
                        ins.then_inc(s["mem_T"], 1)
            pe.wait_ge(s["mem_T_out"], KD * MB)
            x_turn(Tile(0, 0))
            pe.wait_ge(s["memw_in"], 16)
            for j in range(2):
                for k in range(KD):
                    ins = mm(score[j][:, 0:MEM], mem_w[:, k, j * P:(j + 1) * P], memT[:, k, :], k == 0, k == KD - 1)
                ins.then_inc(s["memk_ps"], 1)
            pe.wait_ge(s["memk_out"], 4)
            for b in range(MB):
                for k in range(KD):
                    ins = mm(score[b][:, 256:256 + XA_W], memT[:, k, b * P:(b + 1) * P],
                             mem_w[:, k, XA_W:2 * XA_W], k == 0, k == KD - 1)
                ins.then_inc(s["memv_ps"], 1)

            def body(n, project_, attend, first=False, last=False):
                t = n.moved(-1)
                tp = t.p
                more = project_ and not (last and project_)
                if not attend:
                    for g in range(NG):
                        split_through(pe, g)
                        project(g, n)
                        if g == GV:
                            x_turn(n.moved(1))
                    return
                if project_:
                    project(KVL, n)
                if first:
                    pe.wait_ge(s["hT_hi_s"], 2)
                    pe.wait_ge(s["hT_lo_s"], 2)
                    pe.wait_ge(s["memv_out"], 2)
                pe.wait_ge(s["k_win_s"], t.done(3))
                pe.wait_ge(s["kvl_out"], t.done())
                wait(pe, s["xTa_s"], t.done(lag=1))
                for h in range(SWA_KV):
                    i = t_.transpose(turn[0][:, h * P:(h + 1) * P],
                                     k_win[:, tp, h].rearrange("p a b -> p (a b)"), ident[:])
                i = t_.transpose(turn[0][0:GLA_LR, 2 * P:3 * P], qkv[:, tp, SWA_W + 2 * SWA_KVW:], ident[:])
                i.then_inc(s["kT_ps"], 1)
                pe.wait_ge(s["q_pad_s"], t.done(2))
                wait(pe, s["xTb_s"], t.done(lag=1))
                for h in range(4):
                    i = t_.transpose(turn[1][:, h * P:(h + 1) * P], q_pad[:, h].rearrange("p a b -> p (a b)"), ident[:])
                i.then_inc(s["qTa_ps"], 1)
                if project_:
                    project(SQ, n)
                pe.wait_ge(s["kT_s"], t.done())
                pe.wait_ge(s["lrT_s"], t.done())
                for h in range(4):
                    i = t_.transpose(turn[0][:, h * P:(h + 1) * P], q_pad[:, 4 + h].rearrange("p a b -> p (a b)"),
                                     ident[:])
                i.then_inc(s["qTb_ps"], 1)
                pe.wait_ge(s["qTa_s"], t.done())
                pe.wait_ge(s["gqk_out"], t.done())
                pe.wait_ge(s["xq_out"], t.done())
                for j in range(2):
                    t_.transpose(turn[1][:, j * P:(j + 1) * P], gqk[:, tp, j * P:(j + 1) * P], ident[:])
                for j in range(2):
                    i = t_.transpose(turn[1][:, (2 + j) * P:(3 + j) * P], xq[:, j * P:(j + 1) * P], ident[:])
                i.then_inc(s["gqT_ps"], 1)
                wait(pe, s["mix_s"], t.done(6, lag=1))
                mm(decay_ps[:, 0:GLA_KW], lrT[0:GLA_LR + 1, :], wa2[0:GLA_LR + 1, :], True, True)\
                    .then_inc(s["lr_ps"], 1)
                if project_:
                    project(GQK, n)
                pe.wait_ge(s["qTb_s"], t.done())
                for h in range(SWA_H):
                    i = mm(score[h // 4][:, (h % 4) * P:(h % 4 + 1) * P], qT_pad[:, h, :],
                           kT[:, h // (SWA_H // SWA_KV), :], True, True)
                i.then_inc(s["s_ps"], 1)
                if project_:
                    project(XQZ, n)
                pe.wait_ge(s["la_s"], t.done())
                mm(decay_ps[:, 0:GLA_KW], later[:], la[:], True, True)
                for j in range(2):
                    i = mm(decay_ps[:, GLA_KW + 2 * j:GLA_KW + 2 * j + 2], la[:, j * P:(j + 1) * P], halves[:],
                           True, True)
                i.then_inc(s["decay_cum"], 1)
                pe.wait_ge(s["s_d_s"], t.done(2))
                pe.wait_ge(s["xqT_s"], t.done())
                for h in range(XA_H):
                    i = mm(score[h // 2][:, (h % 2) * MEM:(h % 2 + 1) * MEM], xqT[:, h // 2, :], memT_k[:, h, :],
                           True, True)
                i.then_inc(s["x_ps"], 1)
                if more:
                    pe.wait_ge(s["gqT_s"], t.done(2))
                    x_turn(n.moved(1))
                if project_:
                    project(GV, n)
                if more:
                    pe.wait_ge(s["hT_hi_s"], n.done(lag=-1))
                    pe.wait_ge(s["hT_lo_s"], n.done(lag=-1))
                pe.wait_ge(s["gqT_s"], t.done(2))
                pe.wait_ge(s["s_exp_s"], t.done())
                for half, done in ((0, "pTa_ps"), (1, "pTb_ps")):
                    for h in range(4):
                        i = t_.transpose(turn[half][:, h * P:(h + 1) * P], probs[:, 4 * half + h, :], ident[:])
                    i.then_inc(s[done], 1)
                pe.wait_ge(s["k_dec_s"], t.done(2))
                if not project_ or first:
                    pe.wait_ge(s["gv_out"], t.done())
                wait(pe, s["state_s"], t.done(4, lag=1))
                for c in range(2):
                    for j in range(2):
                        for b in range(2):
                            h = 2 * j + b
                            i = mm(kv_ps[:, (2 * c + j) * GLA_DV:(2 * c + j + 1) * GLA_DV], k_dec[:, c, j, b, :],
                                   gv[:, h * GLA_DV:(h + 1) * GLA_DV], b == 0, b == 1)
                i.then_inc(s["kv_done"], 1)
                if project_:
                    project(GZ, n)
                pe.wait_ge(s["x_exp_s"], t.done())
                pe.wait_ge(s["pTa_s"], t.done())
                pe.wait_ge(s["pTb_s"], t.done())
                for half, done in ((0, "xTa_ps"), (1, "xTb_ps")):
                    for i4 in range(4):
                        h, b = 2 * half + i4 // MB, i4 % MB
                        i = t_.transpose(turn[half][:, i4 * P:(i4 + 1) * P], xprobs[:, h, b * P:(b + 1) * P], ident[:])
                    i.then_inc(s[done], 1)
                pe.wait_ge(s["v_win_s"], t.done(2))
                for h in range(SWA_H):
                    kv = slice((h // 4) * HD, (h // 4 + 1) * HD)
                    mm(score[1][0:CHUNK, h * HD:(h + 1) * HD], probsT[:, h, 0:CHUNK], v_win[:, tp, kv], True, True)
                    i = mm(score[1][CHUNK:P, h * HD:(h + 1) * HD], probsT[:, h, CHUNK:P],
                           qkv[:, tp, SWA_W + SWA_KVW + kv.start:SWA_W + SWA_KVW + kv.stop], True, True)
                i.then_inc(s["os_ps"], 1)
                if project_:
                    project(SZ, n)
                pe.wait_ge(s["state_s"], t.done(4))
                for h in range(GLA_H):
                    for c in range(2):
                        i = mm(score[0][:, h * GLA_DV:(h + 1) * GLA_DV], gqT[:, h // 2, h % 2, c, :],
                               state[:, c, h // 2, :], c == 0, c == 1)
                i.then_inc(s["og_ps"], 1)
                pe.wait_ge(s["xTa_s"], t.done())
                pe.wait_ge(s["xTb_s"], t.done())
                pe.wait_ge(s["g_end_s"], t.done())
                for h in range(XA_H):
                    for b in range(MB):
                        i = mm(decay_ps[:, h * HD:(h + 1) * HD], xprobsT[:, h * MB + b, :],
                               mem_v[:, b, h * HD:(h + 1) * HD], b == 0, b == MB - 1)
                i.then_inc(s["ox_ps"], 1)

            iterations(pe, lambda n, project, attend, first=False, last=False:
                       body(n, project, attend, first, last))

            def mix_turn(b):
                for half, banks, ready, done, free in ((m_hi, turn, "b_hi", "bT_hi", "bT_hi_s"),
                                                       (m_lo, score, "b_lo", "bT_lo", "bT_lo_s")):
                    pe.wait_ge(s[ready], b.done())
                    wait(pe, s[free], b.done(2, lag=1))
                    for k in range(KM):
                        i = t_.transpose(banks[k // 8][:].bitcast(F16)[:, (k % 8) * P:(k % 8 + 1) * P],
                                         half[:, k * P:(k + 1) * P], ident16[:])
                    i.then_inc(s[done], 1)

            pe.wait_ge(s["mix_s"], 6 * TILES)
            mix_turn(Tile(0, 0))
            pe.wait_ge(s["w_hi_s"], KD * NG + KM)
            pe.wait_ge(s["w_lo_s"], KD * NG + KM)

            def out_body(b, more):
                pe.wait_ge(s["bT_hi_s"], b.done(2))
                pe.wait_ge(s["bT_lo_s"], b.done(2))
                for h in range(2):
                    ps = (proj if h == 0 else (decay_ps, kv_ps))[b.p]
                    wait(pe, s[f"y_res{h}"], b.done(lag=2))
                    cols = slice(h * 512, (h + 1) * 512)
                    for k in range(KM):
                        hi = mT_hi[b.p][:, k * P:(k + 1) * P]
                        lo = mT_lo[b.p][:, k * P:(k + 1) * P]
                        mm(ps[:], hi, wo_hi[:, k, cols], k == 0, False)
                        mm(ps[:], hi, wo_lo[:, k, cols], False, False)
                        i = mm(ps[:], lo, wo_hi[:, k, cols], False, k == KM - 1)
                    i.then_inc(s[f"y_ps{h}"], 1)
                    if h == 0 and more:
                        mix_turn(b.moved(1))

            out_iterations(pe, out_body)


_OUT = (1, SEQ, D)


def kernel(**inputs):
    import numpy as _np
    import concourse.bacc as _bacc
    from concourse import mybir as _mybir
    from concourse.bass_utils import run_bass_kernel_spmd as _run

    c = _np.ascontiguousarray
    rows = lambda a, k: c(_np.asarray(a).reshape(k, P, -1).transpose(1, 0, 2))
    w_in = _np.asarray(inputs["w_in"])[0]
    arrays = {
        "x": c(_np.asarray(inputs["x"])[0]),
        "mem": c(_np.asarray(inputs["mem"])[0]),
        "pos": c(_np.asarray(inputs["positions"])[0].reshape(TILES, P).T),
        "g_norm": c(_np.asarray(inputs["g_norm"]).reshape(KD, P).T),
        "w_a2": c(_np.asarray(inputs["w_a2"])[0]),
        "b_a": c(_np.asarray(inputs["b_a"])),
        "g_gla": c(_np.asarray(inputs["g_gla"]).reshape(GLA_DV, 1)),
        "sinks": c(_np.asarray(inputs["sinks"])[0]),
        "g_mem": c(_np.asarray(inputs["g_mem"]).reshape(KD, P).T),
        "w_mem": rows(inputs["w_mem_kv"], KD),
        "w_out": rows(inputs["w_out"], KM),
        "g_final": c(_np.asarray(inputs["g_final"])),
    }
    for i, names in enumerate(GROUPS):
        cols = _np.concatenate([w_in[:, _starts[n]:_starts[n] + _width[n]] for n in names], axis=1)
        arrays[f"w_group{i}"] = rows(cols, KD).reshape(P, -1)
    nc = _bacc.Bacc("TRN2", target_bir_lowering=False, num_devices=1, dynamic_dma_scratch_size=4096)
    args = {n: nc.dram_tensor(n, a.shape, _mybir.dt.from_np(a.dtype), kind="ExternalInput").ap()
            for n, a in arrays.items()}
    out = nc.dram_tensor("out", (SEQ, D), F32, kind="ExternalOutput").ap()
    build_kernel(nc, args["x"], args["mem"], args["pos"], args["g_norm"],
                 [args[f"w_group{i}"] for i in range(NG)], args["w_a2"], args["b_a"], args["g_gla"],
                 args["sinks"], args["g_mem"], args["w_mem"], args["w_out"], args["g_final"], out)
    r = _run(nc, [arrays], core_ids=[0])
    return r.results[0]["out"].reshape(_OUT)
```

```python
from contextlib import ExitStack

import numpy as np

import concourse.bass as bass
from concourse import mybir

F32 = mybir.dt.float32
F16 = mybir.dt.float16
I32 = mybir.dt.int32
ALU = mybir.AluOpType
ACT = mybir.ActivationFunctionType
AX = mybir.AxisListType.X

P = 128
SEQ = 4096
D = 1024
KD = D // P
MEM = 256
MB = MEM // P
CHUNK = 64
EPS = 1e-6
TILES = SEQ // P
NEG = -1e30

GLA_H, GLA_DK, GLA_DV, GLA_LR, GLA_TAU = 4, 64, 128, 16, 16.0
GLA_KW, GLA_W = GLA_H * GLA_DK, GLA_H * GLA_DV
SWA_H, SWA_KV, HD = 8, 2, 64
SWA_W, SWA_KVW = SWA_H * HD, SWA_KV * HD
XA_H = 4
XA_W = XA_H * HD
D_MIX = GLA_W + SWA_W + XA_W
KM = D_MIX // P
ROPE_HALF = HD // 8
ROPE_THETA = 500000.0
SCALE = HD ** -0.5

_names = ("gq", "gk", "gv", "gz", "lr", "sq", "sk", "sv", "sz", "xq", "xz")
_widths = (GLA_KW, GLA_KW, GLA_W, GLA_W, GLA_LR, SWA_W, SWA_KVW, SWA_KVW, SWA_W, XA_W, XA_W)
_starts = dict(zip(_names, np.cumsum((0,) + _widths[:-1]).tolist()))
_width = dict(zip(_names, _widths))
GROUPS = (("sk", "sv", "lr"), ("sq",), ("gq", "gk"), ("xq", "xz"), ("gv",), ("gz",), ("sz",))
KVL, SQ, GQK, XQZ, GV, GZ, SZ = range(len(GROUPS))
NG = len(GROUPS)
GCOLS = [sum(_width[n] for n in g) for g in GROUPS]
GOFF = [KD * c for c in np.cumsum([0] + GCOLS[:-1]).tolist()]
W_WORDS = KD * sum(GCOLS)

X_UP = 1024.0
W_UP = 2.0 ** 14
M_UP = 2.0 ** 14
PROB_UP, V_UP = 2.0 ** 14, 2.0 ** 14
EXPONENT = 0x7F800000
HIGH_A = 5


def two_pi_parts(scale, bits, count):
    left, parts = 2.0 * np.pi * scale, []
    for _ in range(count):
        lsb = 2.0 ** (np.floor(np.log2(left)) - bits + 1)
        parts.append(float(np.floor(left / lsb) * lsb))
        left -= parts[-1]
    return parts


class Tile:

    def __init__(self, m, p):
        self.m, self.p = m, p

    def moved(self, k):
        n = self.p + k
        return Tile(self.m + n // 2, n % 2)

    def index(self):
        return self.m * 2 + self.p

    def done(self, per=1, lag=0):
        return self.m * (2 * per) + per * (self.p + 1 - lag)

    def done_alike(self, per=16):
        return self.m * per + per


def wait(eng, sem, value):
    if isinstance(value, int) and value <= 0:
        return
    eng.wait_ge(sem, value)


def build_kernel(nc, x, mem, pos, g_norm, w_groups, w_a2, b_a, g_gla, sinks, g_mem, w_mem, w_out, g_final, out):
    ctx = ExitStack()
    with ctx:
        def sb(name, shape, dt=F32):
            return ctx.enter_context(nc.sbuf_tensor(name, shape, dt))

        def sem(name):
            return ctx.enter_context(nc.semaphore(name))

        mix_dram = nc.dram_tensor("mix_rows", [SEQ, D_MIX], F32, kind="Internal").ap()

        W = sb("W", [P, W_WORDS])
        scratch = sb("scratch", [P, 8448])
        x_in = sb("x_in", [P, 2, D])
        x_hi = sb("x_hi", [P, D], F16)
        x_lo = sb("x_lo", [P, D], F16)
        hT_hi = sb("hT_hi", [P, 2, D], F16)
        hT_lo = sb("hT_lo", [P, 2, D], F16)
        qkv = sb("qkv", [P, 2, SWA_W + 2 * SWA_KVW + GLA_LR])
        q_pad = sb("q_pad", [P, SWA_H, 2, HD])
        k_win = sb("k_win", [P, 2, SWA_KV, 2, HD])
        v_win = sb("v_win", [P, 2, SWA_KVW])
        kT = sb("kT", [P, SWA_KV, P])
        gqk = sb("gqk", [P, 2, 2 * GLA_KW])
        xq = sb("xq", [P, XA_W])
        xqT = sb("xqT", [P, 2, P])
        gv = sb("gv", [P, GLA_W])
        gates = sb("gates", [P, 2, D_MIX])
        tanh_z = sb("tanh_z", [P, 512])
        lrT = sb("lrT", [32, P])
        wa2 = sb("wa2", [32, GLA_KW])
        la = sb("la", [P, GLA_KW])
        la_e = sb("la_e", [P, GLA_KW])
        decay = sb("decay", [P, GLA_KW])
        state = sb("state", [P, 2, 2, GLA_DV])
        memT_k = sb("memT_k", [P, XA_H // 2, MEM])
        mem_v = sb("mem_v", [P, MB, XA_W])
        mem_v_hi = sb("mem_v_hi", [P, MB, XA_W], F16)
        mem_v_lo = sb("mem_v_lo", [P, MB, XA_W], F16)
        ident = sb("ident", [P, P])
        ident16 = sb("ident16", [P, P], F16)
        later = sb("later", [P, P])
        halves = sb("halves", [P, 2])
        rope_t = sb("rope_t", [P, 4, SWA_H + SWA_KV, ROPE_HALF])
        cos_sin = sb("cos_sin", [P, TILES, 2, ROPE_HALF])
        cs = sb("cs", [P, 2, ROPE_HALF])
        small = sb("small", [P, 224])

        used = [0]

        def column(n):
            used[0] += n
            assert used[0] <= 224
            return small[:, used[0] - n:used[0]]

        gn, gm, gg = column(KD), column(KD), column(1)
        minus_half = column(4)
        unscale, unscale_half = column(NG), column(NG)
        w_max, w_max1, w_pow, w_rec = column(KM), column(1), column(1), column(1)
        g_top, tiny, w_sum, w_bound, w_all = column(1), column(1), column(NG), column(NG), column(NG + 2)
        w_scale = column(2 * KD)
        x_ss, x_ms, x_rs = column(1), column(1), column(1)
        s_mx, s_m, s_diff, s_sink, s_den, s_den2, s_rden = (column(SWA_H) for _ in range(7))
        c_mx, c_den, c_rden = (column(XA_H) for _ in range(3))
        g_end = column(4)
        o_ss, o_ms, o_rs, o_rc = (column(GLA_H) for _ in range(4))
        m_amax, m_pow, m_rec, m_scale = (column(1) for _ in range(4))
        m_un, m_un_now = column(2), column(2)
        w_out_un = column(1)
        v_scale, v_unscale, xa_unscale = (column(1) for _ in range(3))
        sink_b = sb("sink_b", [P, SWA_H])

        def room(at, n, *shape):
            v = scratch[:, at:at + n]
            names = "abcd"[:len(shape)]
            return v.rearrange(f"p ({' '.join(names)}) -> p {' '.join(names)}", **dict(zip(names, shape)))

        probs = room(0, 1024, SWA_H, P)
        probsT = room(1024, 1024, SWA_H, P)
        xprobs = room(2048, 1024, XA_H, MEM)
        xprobsT_hi, xprobsT_lo = (scratch[:, at:at + 512].bitcast(F16).rearrange("p (a b) -> p a b", b=P)
                                  for at in (3072, 3584))
        k_dec = scratch[:, 4096:4096 + GLA_KW]
        qT_pad = room(5120, 1024, SWA_H, P)
        gqT = room(6144, GLA_KW, 2, P)
        mix = scratch[:, 7168:8448]
        raw_rooms = (scratch[:, 0:4096], scratch[:, 4096:8192], W[:, GOFF[GV]:GOFF[GV] + 4096],
                     W[:, GOFF[SZ]:GOFF[SZ] + 4096])
        RAW = {KVL: (0, 1), SQ: (1, 1), GQK: (2, 1), XQZ: (0, 2), GV: (1, 2), GZ: (3, 1), SZ: (0, 3)}

        def raw(g):
            return raw_rooms[RAW[g][0]][:, 0:KD * GCOLS[g]].rearrange("p (k c) -> p k c", k=KD)

        def block_scale(g, k):
            return w_scale[:, (g % 2) * KD + k:(g % 2) * KD + k + 1]

        def wait_raw(eng, g):
            eng.wait_ge(w_raw_in[RAW[g][0]], 16 * RAW[g][1])

        def gla_out(h):
            return gla_banks[h % 2][:, (h // 2) * GLA_DV:(h // 2 + 1) * GLA_DV]

        def w_hi(g):
            n = KD * GCOLS[g]
            return W[:, GOFF[g]:GOFF[g] + n // 2].bitcast(F16).rearrange("p (k c) -> p k c", k=KD)

        def w_lo(g):
            n = KD * GCOLS[g]
            return W[:, GOFF[g] + n // 2:GOFF[g] + n].bitcast(F16).rearrange("p (k c) -> p k c", k=KD)

        mem_w = W[:, GOFF[SZ]:GOFF[SZ] + KD * 2 * XA_W].rearrange("p (k c) -> p k c", k=KD)
        mem_in = W[:, GOFF[GZ]:GOFF[GZ] + 2 * D].rearrange("p (b d) -> p b d", b=MB)
        memT = W[:, GOFF[GZ] + 2 * D:GOFF[GZ] + 4 * D].rearrange("p (k m) -> p k m", k=KD)
        wo_raw = W[:, GOFF[SQ]:GOFF[SQ] + KM * D].rearrange("p (k c) -> p k c", k=KM)
        wo_halves = W[:, GOFF[GV]:GOFF[GV] + KM * D].bitcast(F16).rearrange("p (k a c) -> p k a c", k=KM, a=2)
        wo_hi, wo_lo = wo_halves[:, :, 0, :], wo_halves[:, :, 1, :]
        assert GOFF[SQ] + KM * D + 3 * D_MIX // 2 <= GOFF[GV] and GOFF[GV] + KM * D + 3 * D_MIX // 2 <= W_WORDS

        def words(buffer, at, n=D_MIX // 2):
            return buffer[:, at:at + n]

        left_a, left_b = GOFF[SQ] + KM * D, GOFF[GV] + KM * D
        m_in = [words(W, left_b, D_MIX), words(W, GOFF[KVL], D_MIX)]
        m_hi = words(W, left_b + D_MIX).bitcast(F16)
        m_lo = words(W, left_a).bitcast(F16)
        mT_hi = [words(W, left_a + D_MIX // 2).bitcast(F16), words(scratch, 0).bitcast(F16)]
        mT_lo = [words(W, left_a + D_MIX).bitcast(F16), words(scratch, D_MIX // 2).bitcast(F16)]
        y = words(scratch, D_MIX, D)
        g_fin = words(scratch, D_MIX + D, D)
        WO_SUM = 2
        wo_junk = W[:, GOFF[KVL]:GOFF[KVL] + WO_SUM * D].rearrange("p (k c) -> p k c", k=WO_SUM)
        WO_ROOMS = ((SQ, 0, 4), (GQK, 4, 8), (XQZ, 8, KM))

        def bank(name):
            return ctx.enter_context(nc.psum_tensor(name, [P, 512], F32))

        proj = [bank("proj0"), bank("proj1")]
        turn = [bank("turn0"), bank("turn1")]
        score = [bank("score0"), bank("score1")]
        decay_ps = bank("decay_ps")
        kv_ps = bank("kv_ps")

        gla_banks = (score[0], kv_ps)
        kv_banks = (kv_ps[:, 0:2 * GLA_DV], decay_ps[:, 2 * GLA_DV:4 * GLA_DV])
        xa_order = [h for b in range(2) for h in range(b, XA_H, 2)]
        mem_banks = (score[0], score[1], decay_ps, kv_ps)

        sem_names = """ mem_in_s memw_in gfin_in small_in
            set_up_steps b_chain b_un_now id_set misc_set pads_set
            ang_done ang_abs cos_done
            mem_sq mem_ms mem_rs mem_scaled mem_T mem_T_out memk_ps memk_out memv_ps memv_out v_split_s
            g_top_s w_sum_s w_bound_s wmax1 wall_s wscale2_s w_hi_s w_hi2_s w_lo_s unscale_s
            x_ss_s x_ms_s x_rs_s x_hi_s x_lo_s xT_hi_ps xT_lo_ps hT_hi_s hT_lo_s
            kvl_out sq_out gqk_out tanh_s xz_out xq_out gv_out gz_out sz_out
            cs_s rope_t_s rope_s q_pad_s k_win_s v_win_s
            kT_ps qTa_ps qTb_ps gqT_ps kT_s lrT_s qTa_s qTb_s gqT_s xqT_s
            lr_ps la_abs la_exp la_ln la_s decay_cum decay_s g_end_s k_dec_s
            s_ps s_mx_s s_m_s s_d_s s_diff_s s_exp_s s_sink_s s_den_s s_den2_s s_rden_s s_rdc_s s_gate_s
            x_ps x_mx_s x_d_s x_exp_s x_den_s x_rden_s x_rdc_s x_gate_s
            pTa_ps pTb_ps pTa_s pTb_s xTa_ps xTb_ps xTa_s xTb_s xT_hi_out
            kv_done state_s os_ps og_ps ox_ps o_ss_s o_ms_s o_rs_s o_rc_s mix_s mix_out
            wo_cols b_scale b_un b_hi b_lo bT_hi bT_lo bT_hi_s bT_lo_s
            y_ps0 y_ps1 y_res0 y_res1 y_ss y_ms y_rs y_fin y_out state0"""
        s = {n: sem(n) for n in sem_names.split()}
        assert len(s) == len(sem_names.split())
        w_raw_in = [sem(f"w_raw_in{r}") for r in range(4)]
        x_in_s = [sem("x_in_even"), sem("x_in_odd")]
        xr_in_s = [sem("xr_in_even"), sem("xr_in_odd")]
        m_in_s = [sem("m_in_even"), sem("m_in_odd")]
        wout_in = [sem(f"wout_in{part}") for part in range(3)]
        proj_ps = [sem(f"proj_ps{g}") for g in range(NG)]

        def split_through(eng, g):
            eng.wait_ge(s["w_lo_s"], KD * (g + 1))

        block = ctx.enter_context(nc.Block())

        def iterations(eng, body):
            body(Tile(0, 0), project=True, attend=False)
            body(Tile(0, 1), project=True, attend=True, first=True)
            with eng.Fori(1, TILES // 2 - 1) as m:
                body(Tile(m, 0), project=True, attend=True)
                body(Tile(m, 1), project=True, attend=True)
            body(Tile(TILES // 2 - 1, 0), project=True, attend=True)
            body(Tile(TILES // 2 - 1, 1), project=True, attend=True, last=True)
            body(Tile(TILES // 2, 0), project=False, attend=True, last=True)

        def out_iterations(eng, body):
            body(Tile(0, 0), 2)
            body(Tile(0, 1), 2)
            with eng.Fori(1, TILES // 2 - 1) as m:
                body(Tile(m, 0), 2)
                body(Tile(m, 1), 2)
            body(Tile(TILES // 2 - 1, 0), 1)
            body(Tile(TILES // 2 - 1, 1), 0)

        last_reader = {KVL: "kvl_out", SQ: "sq_out", GQK: "gqk_out", XQZ: "xq_out", GV: "gv_out", GZ: "gz_out",
                       SZ: "sz_out"}
        proj_bank = lambda t, g: proj[(t.p + g) % 2]

        @block.sync
        def _(sp):
            def raw_load(g):
                sp.dma_start(raw_rooms[RAW[g][0]][:, 0:KD * GCOLS[g]], w_groups[g]).then_inc(w_raw_in[RAW[g][0]], 16)

            for dst, src in ((la_e[:, 0:TILES].bitcast(I32), pos), (gn, g_norm), (gm, g_mem), (gg, g_gla),
                             (wa2[0:GLA_LR, :], w_a2), (wa2[GLA_LR:GLA_LR + 1, :], b_a),
                             (sink_b[:], sinks.partition_broadcast(P))):
                sp.dma_start(dst, src).then_inc(s["small_in"], 16)
            sp.dma_start(x_in[:, 0, :], x[0:P, :]).then_inc(x_in_s[0], 16)
            raw_load(KVL)
            sp.dma_start(mem_in, mem.rearrange("(b p) d -> p b d", p=P)).then_inc(s["mem_in_s"], 16)
            raw_load(SQ)
            sp.dma_start(mem_w, w_mem).then_inc(s["memw_in"], 16)
            raw_load(GQK)
            sp.dma_start(x_in[:, 1, :], x[P:2 * P, :]).then_inc(x_in_s[1], 16)
            for g in (XQZ, GV):
                split_through(sp, g - 3)
                raw_load(g)
            sp.wait_ge(s["memv_ps"], MB)
            raw_load(GZ)
            split_through(sp, XQZ)
            raw_load(SZ)

            def body(n, project, attend, first=False, last=False):
                if project and not last:
                    nxt = n.moved(2)
                    row = sp.snap(nxt.index() * P) if not isinstance(n.m, int) else nxt.index() * P
                    if not (isinstance(n.m, int) and nxt.index() >= TILES):
                        wait(sp, s["x_hi_s"], n.done())
                        sp.wait_ge(s["x_lo_s"], n.done())
                        sp.dma_start(x_in[:, n.p, :], x[bass.ds(row, P), :]).then_inc(x_in_s[n.p], 16)
                if last and project:
                    for part, (g, k0, k1) in enumerate(WO_ROOMS):
                        sp.wait_ge(proj_ps[g], TILES)
                        sp.dma_start(wo_raw[:, k0:k1, :], w_out[:, k0:k1, :]).then_inc(wout_in[part], 16)
                if last and not project:
                    sp.wait_ge(s["mix_out"], 16 * 2)
                    sp.wait_ge(proj_ps[SZ], TILES)
                    sp.dma_start(m_in[0], mix_dram[0:P, :]).then_inc(m_in_s[0], 16)
                    sp.wait_ge(s["x_hi_s"], TILES)
                    sp.wait_ge(s["x_lo_s"], TILES)
                    sp.dma_start(x_in[:, 0, :], x[0:P, :]).then_inc(xr_in_s[0], 16)
                    sp.wait_ge(s["w_sum_s"], NG + KM // WO_SUM)
                    sp.dma_start(m_in[1], mix_dram[P:2 * P, :]).then_inc(m_in_s[1], 16)
                    sp.dma_start(x_in[:, 1, :], x[P:2 * P, :]).then_inc(xr_in_s[1], 16)
                if attend:
                    t = n.moved(-1)
                    row = sp.snap(t.index() * P) if not isinstance(n.m, int) else t.index() * P
                    sp.wait_ge(s["mix_s"], t.done(6))
                    sp.dma_start(mix_dram[bass.ds(row, P), :], mix).then_inc(s["mix_out"], 16)

            iterations(sp, body)

            sp.wait_ge(s["mix_out"], 16 * TILES)
            sp.dma_start(g_fin, g_final.partition_broadcast(P)).then_inc(s["gfin_in"], 16)

            def out_body(b, more):
                fixed = isinstance(b.m, int)
                nxt = b.moved(2)
                row = b.index() * P if fixed else sp.snap(b.index() * P)
                row2 = nxt.index() * P if fixed else sp.snap(nxt.index() * P)
                if not (fixed and nxt.index() >= TILES):
                    sp.wait_ge(s["b_hi"], b.done())
                    sp.wait_ge(s["b_lo"], b.done())
                    sp.dma_start(m_in[b.p], mix_dram[bass.ds(row2, P), :]).then_inc(m_in_s[b.p], 16)
                    sp.wait_ge(s["y_res0"], b.done())
                    sp.wait_ge(s["y_res1"], b.done())
                    sp.dma_start(x_in[:, b.p, :], x[bass.ds(row2, P), :]).then_inc(xr_in_s[b.p], 16)
                sp.wait_ge(s["y_fin"], b.done())
                sp.dma_start(out[bass.ds(row, P), :], y).then_inc(s["y_out"], 16)

            out_iterations(sp, out_body)
            sp.wait_ge(s["y_out"], 16 * TILES)

        @block.gpsimd
        def _(pool):
            g = nc.gpsimd
            g.memset(ident[:], 0.0).then_inc(s["misc_set"], 1)
            g.memset(later[:], 1.0 / GLA_TAU).then_inc(s["misc_set"], 1)
            g.memset(minus_half, -0.5).then_inc(s["misc_set"], 1)
            g.memset(tiny, 1e-20).then_inc(s["misc_set"], 1)
            g.memset(lrT[:], 1.0).then_inc(s["misc_set"], 1)
            g.memset(halves[:], 0.0).then_inc(s["misc_set"], 1)
            g.memset(q_pad[:], 0.0).then_inc(s["misc_set"], 1)
            g.memset(k_win[:], 0.0).then_inc(s["misc_set"], 1)
            g.memset(v_win[:], 0.0).then_inc(s["misc_set"], 1)
            g.memset(state[:], 0.0).then_inc(s["misc_set"], 1)
            pool.wait_ge(s["misc_set"], 10)
            g.memset(halves[0:CHUNK, 0:1], 1.0 / GLA_TAU).then_inc(s["pads_set"], 1)
            g.memset(halves[CHUNK:P, 1:2], 1.0 / GLA_TAU).then_inc(s["pads_set"], 1)
            pool.wait_ge(s["pads_set"], 2)
            g.affine_select(out=ident[:], in_=ident[:], compare_op=ALU.not_equal, fill=1.0, base=0,
                            pattern=[[-1, P]], channel_multiplier=1).then_inc(s["id_set"], 1)
            g.affine_select(out=later[:], in_=later[:], compare_op=ALU.is_gt, fill=0.0, base=0,
                            pattern=[[-1, P]], channel_multiplier=1).then_inc(s["pads_set"], 1)
            pool.wait_ge(s["pads_set"], 3)
            g.memset(later[CHUNK:P, 0:CHUNK], 0.0).then_inc(s["pads_set"], 1)
            pool.wait_ge(s["pads_set"], 4)
            pool.wait_ge(s["id_set"], 1)
            g.tensor_copy(ident16[:], ident[:]).then_inc(s["id_set"], 1)

            def memory_pow(b):
                pool.wait_ge(s["mem_ms"], b + 1)
                g.tensor_tensor(m_rec[:, :] if b else m_pow[:, :], m_scale[:, :] if b else m_amax[:, :],
                                minus_half[:, 0:1], ALU.pow).then_inc(s["mem_rs"], 1)

            def row_pow(t):
                pool.wait_ge(s["x_ms_s"], t.done())
                wait(pool, s["x_hi_s"], t.done(lag=1))
                wait(pool, s["x_lo_s"], t.done(lag=1))
                g.tensor_tensor(x_rs, x_ms, minus_half[:, 0:1], ALU.pow).then_inc(s["x_rs_s"], 1)

            def all_bound(k):
                pool.wait_ge(s["w_sum_s"], k + 1)
                pool.wait_ge(s["g_top_s"], 1)
                b = w_bound[:, k:k + 1]
                g.tensor_tensor(b, w_sum[:, k:k + 1], g_top, ALU.mult).then_inc(s["w_bound_s"], 1)
                pool.wait_ge(s["w_bound_s"], 2 * k + 1)
                g.tensor_tensor(b, b, tiny, ALU.add).then_inc(s["w_bound_s"], 1)
                pool.wait_ge(s["w_bound_s"], 2 * k + 2)
                g.partition_all_reduce(w_all[:, k:k + 1], b, P, bass.bass_isa.ReduceOp.max).then_inc(s["wall_s"], 1)

            def all_max(k):
                pool.wait_ge(s["wmax1"], k + 1)
                g.partition_all_reduce(w_all[:, NG + k:NG + k + 1], w_max1, P, bass.bass_isa.ReduceOp.max)\
                    .then_inc(s["wall_s"], 1)

            row_pow(Tile(0, 0))
            all_bound(0)
            for b in range(MB):
                memory_pow(b)

            def body(n, project, attend, first=False, last=False):
                t = n.moved(-1)
                tp = t.p
                if not attend:
                    for k in range(1, GQK + 3):
                        all_bound(k)
                if project:
                    heads = qkv[:, n.p, 0:SWA_W + SWA_KVW].rearrange("p (h d) -> p h d", d=HD)
                    x1, x2 = heads[:, :, 0:ROPE_HALF], heads[:, :, ROPE_HALF:2 * ROPE_HALF]
                    shape = [P, SWA_H + SWA_KV, ROPE_HALF]
                    c = cs[:, 0:1, :].to_broadcast(shape)
                    sn = cs[:, 1:2, :].to_broadcast(shape)
                    pool.wait_ge(s["cs_s"], n.done())
                    pool.wait_ge(s["kvl_out"], n.done())
                    pool.wait_ge(s["sq_out"], n.done())
                    for i, (a, b) in enumerate(((x1, c), (x2, sn), (x2, c), (x1, sn))):
                        g.tensor_tensor(rope_t[:, i], a, b, ALU.mult).then_inc(s["rope_t_s"], 1)
                    pool.wait_ge(s["rope_t_s"], n.done(4))
                    g.tensor_tensor(x1, rope_t[:, 0], rope_t[:, 1], ALU.subtract).then_inc(s["rope_s"], 1)
                    g.tensor_tensor(x2, rope_t[:, 2], rope_t[:, 3], ALU.add).then_inc(s["rope_s"], 1)
                    if not (last and project):
                        row_pow(n.moved(1))
                if not attend:
                    for k in range(GQK + 3, NG):
                        all_bound(k)
                if not attend:
                    all_max(0)
                if attend:
                    pool.wait_ge(s["s_rden_s"], t.done())
                    g.tensor_tensor(s_den, s_rden, unscale_half[:, SZ:SZ + 1].to_broadcast([P, SWA_H]), ALU.mult)\
                        .then_inc(s["s_rdc_s"], 1)
                    sg = gates[:, tp, GLA_W:GLA_W + SWA_W].rearrange("p (h d) -> p h d", d=HD)
                    pool.wait_ge(s["s_rdc_s"], t.done())
                    g.tensor_tensor(sg, sg, s_den.unsqueeze(2).to_broadcast([P, SWA_H, HD]), ALU.mult)\
                        .then_inc(s["s_gate_s"], 1)
                    pool.wait_ge(s["x_rden_s"], t.done())
                    g.tensor_tensor(c_den, c_rden, xa_unscale.to_broadcast([P, XA_H]), ALU.mult)\
                        .then_inc(s["x_rdc_s"], 1)
                    xg = gates[:, tp, GLA_W + SWA_W:D_MIX].rearrange("p (j b d) -> p b j d", b=2, d=HD)
                    by_head = c_den.rearrange("p (b j) -> p b j", b=2).unsqueeze(3)
                    pool.wait_ge(s["x_rdc_s"], t.done())
                    g.tensor_tensor(xg, xg, by_head.to_broadcast([P, 2, XA_H // 2, HD]), ALU.mult)\
                        .then_inc(s["x_gate_s"], 1)
                    if last and project:
                        all_max(1)
                    pool.wait_ge(s["o_ms_s"], t.done())
                    g.tensor_tensor(o_rs, o_ms, minus_half, ALU.pow).then_inc(s["o_rs_s"], 1)
                    pool.wait_ge(s["o_rs_s"], t.done())
                    g.tensor_tensor(o_rc, o_rs, unscale_half[:, GZ:GZ + 1].to_broadcast([P, GLA_H]), ALU.mult)\
                        .then_inc(s["o_rc_s"], 1)

            iterations(pool, body)
            def out_body(b, more):
                pool.wait_ge(s["y_ms"], b.done())
                g.tensor_tensor(x_rs, x_ms, minus_half[:, 0:1], ALU.pow).then_inc(s["y_rs"], 1)

            out_iterations(pool, out_body)

        @block.scalar
        def _(act):
            a = nc.scalar
            def x_square(t):
                act.wait_ge(x_in_s[t.p], t.done_alike())
                wait(act, s["x_ms_s"], t.done(lag=1))
                wait(act, s["xT_hi_ps"], t.done(lag=1))
                a.activation(x_hi[:], x_in[:, t.p, :], ACT.Square, accum_out=x_ss).then_inc(s["x_ss_s"], 1)

            def x_high(t):
                act.wait_ge(s["x_rs_s"], t.done())
                act.wait_ge(s["x_ss_s"], t.done())
                a.activation(x_hi[:], x_in[:, t.p, :], ACT.Copy, scale=x_rs).then_inc(s["x_hi_s"], 1)

            def hT_high(t):
                act.wait_ge(s["xT_hi_ps"], t.done())
                wait(act, proj_ps[SZ], t.done(lag=2))
                a.activation(hT_hi[:, t.p, :], turn[0][:].bitcast(F16), ACT.Copy).then_inc(s["hT_hi_s"], 1)

            def memory_keys():
                for j in range(2):
                    act.wait_ge(s["memk_ps"], j + 1)
                    a.activation(memT_k[:, j, :], score[j][:, 0:MEM], ACT.Copy).then_inc(s["memk_out"], 1)

            def memory_values():
                for b in range(MB):
                    act.wait_ge(s["memv_ps"], b + 1)
                    a.activation(mem_v[:, b, :], score[b][:, 256:256 + XA_W], ACT.Copy).then_inc(s["memv_out"], 1)

            def magnitudes(g):
                wait_raw(act, g)
                if g < GV:
                    junk = W[:, GOFF[g]:GOFF[g] + KD * GCOLS[g]]
                elif g < SZ:
                    junk = W[:, GOFF[GZ]:GOFF[GZ] + KD * GCOLS[GZ]]
                    act.wait_ge(s["memv_ps"], MB)
                    act.wait_ge(s["w_sum_s"], g)
                else:
                    junk = raw_rooms[1]
                    split_through(act, GV)
                a.activation(junk[:, 0:KD * GCOLS[g]], raw_rooms[RAW[g][0]][:, 0:KD * GCOLS[g]], ACT.Abs,
                             accum_out=w_sum[:, g:g + 1]).then_inc(s["w_sum_s"], 1)

            def split_high(g):
                if XQZ <= g < SZ:
                    magnitudes(g + 1)
                act.wait_ge(s["wscale2_s"], g + 1)
                if g == SZ:
                    split_through(act, GZ)
                for k in range(HIGH_A):
                    a.activation(w_hi(g)[:, k, :], raw(g)[:, k, :], ACT.Copy, scale=block_scale(g, k))\
                        .then_inc(s["w_hi_s"], 1)
                if g == KVL:
                    hT_high(Tile(0, 0))
                if g < XQZ:
                    magnitudes(g + 1)

            x_square(Tile(0, 0))
            magnitudes(KVL)
            act.wait_ge(s["mem_in_s"], 16)
            for b in range(MB):
                a.activation((hT_hi, hT_lo)[b][:, 1, :], mem_in[:, b, :], ACT.Square,
                             accum_out=(s_mx if b == 0 else s_m)[:, 0:1]).then_inc(s["mem_sq"], 1)
            x_high(Tile(0, 0))

            def project_out(g, n):
                if g in (SQ,):
                    return
                act.wait_ge(proj_ps[g], n.done())
                ps = proj_bank(n, g)
                if g == KVL:
                    a.activation(qkv[:, n.p, SWA_W:], ps[:, 0:GCOLS[g]], ACT.Copy, scale=unscale[:, g:g + 1])\
                        .then_inc(s["kvl_out"], 1)
                elif g == GQK:
                    a.activation(gqk[:, n.p, :], ps[:], ACT.Copy, scale=unscale[:, g:g + 1])\
                        .then_inc(s["gqk_out"], 1)
                elif g == GV:
                    a.activation(gv[:], ps[:], ACT.Copy, scale=unscale[:, g:g + 1]).then_inc(s["gv_out"], 1)
                else:
                    cols = slice(XA_W, 2 * XA_W) if g == XQZ else slice(0, 512)
                    width = cols.stop - cols.start
                    before = {XQZ: ("sz_out", 1), GZ: ("xz_out", 0), SZ: ("gz_out", 0)}[g]
                    wait(act, s[before[0]], n.done(lag=before[1]))
                    if g == XQZ:
                        wait(act, s["o_ss_s"], n.done(4, lag=2))
                    a.activation(tanh_z[:, 0:width], ps[:, cols], ACT.Tanh, scale=unscale_half[:, g:g + 1])\
                        .then_inc(s["tanh_s"], 1)

            def pad_queries(n):
                act.wait_ge(s["rope_s"], n.done(2))
                act.wait_ge(s["misc_set"], 10)
                wait(act, s["qTa_ps"], n.done(lag=1))
                wait(act, s["qTb_ps"], n.done(lag=1))
                q = qkv[:, n.p, 0:SWA_W].rearrange("p (h d) -> p h d", d=HD)
                for c in range(2):
                    rows = slice(c * CHUNK, (c + 1) * CHUNK)
                    a.activation(q_pad[rows, :, c, :], q[rows], ACT.Copy).then_inc(s["q_pad_s"], 1)

            def out_sums(i):
                act.wait_ge(wout_in[i * WO_SUM // 4], 16)
                if i:
                    act.wait_ge(s["w_sum_s"], NG + i)
                a.activation(wo_junk, wo_raw[:, i * WO_SUM:(i + 1) * WO_SUM, :], ACT.Abs,
                             scale=gg if i * WO_SUM < GLA_H else 1.0, accum_out=w_max[:, i:i + 1])\
                    .then_inc(s["w_sum_s"], 1)

            def out_high(k0, k1):
                act.wait_ge(s["wo_cols"], 2)
                act.wait_ge(proj_ps[(GV, GZ, SZ)[k0 // 4]], TILES)
                for k in range(k0, k1):
                    a.activation(wo_hi[:, k, :], wo_raw[:, k, :], ACT.Copy, scale=w_scale[:, k:k + 1])\
                        .then_inc(s["w_hi_s"], 1)

            def mix_high(b):
                act.wait_ge(s["b_scale"], b.done())
                act.wait_ge(m_in_s[b.p], b.done_alike())
                wait(act, s["bT_hi"], b.done(lag=1))
                a.activation(m_hi, m_in[b.p], ACT.Copy, scale=m_scale).then_inc(s["b_hi"], 1)

            def mixT_high(b):
                act.wait_ge(s["bT_hi"], b.done())
                wait(act, s["y_ps1"], b.done(lag=2))
                a.activation(mT_hi[b.p][:, 0:D], turn[0][:].bitcast(F16), ACT.Copy).then_inc(s["bT_hi_s"], 1)
                a.activation(mT_hi[b.p][:, D:D_MIX], turn[1][:].bitcast(F16)[:, 0:D_MIX - D], ACT.Copy)\
                    .then_inc(s["bT_hi_s"], 1)

            def body(n, project, attend, first=False, last=False):
                t = n.moved(-1)
                lagged = project and not attend
                if lagged:
                    for g in range(NG):
                        split_high(g)
                        if g == KVL:
                            act.wait_ge(s["ang_done"], 1)
                            a.activation(cos_sin[:, :, 1, :], cos_sin[:, :, 1, :], ACT.Sin)
                            a.activation(cos_sin[:, :, 0, :], cos_sin[:, :, 0, :], ACT.Sin).then_inc(s["cos_done"], 1)
                        if g == SQ:
                            memory_keys()
                        if g == GQK:
                            x_square(n.moved(1))
                        if g == XQZ:
                            memory_values()
                        if g >= 2:
                            project_out(g - 2, n)
                            if g - 2 == GQK:
                                pad_queries(n)
                                x_high(n.moved(1))
                    project_out(NG - 2, n)
                    project_out(NG - 1, n)
                    hT_high(n.moved(1))
                    return
                more = project and not (last and project)
                ending, ended = last and project, last and not project
                if project:
                    project_out(KVL, n)
                act.wait_ge(s["qTa_ps"], t.done())
                wait(act, s["s_ps"], t.done(lag=1))
                if first:
                    split_through(act, NG - 1)
                a.activation(qT_pad[:, 0:4, :], turn[1][:], ACT.Copy).then_inc(s["qTa_s"], 1)
                if ended:
                    out_high(4, 7)
                if more:
                    x_square(n.moved(1))
                act.wait_ge(s["qTb_ps"], t.done())
                a.activation(qT_pad[:, 4:8, :], turn[0][:], ACT.Copy).then_inc(s["qTb_s"], 1)
                if ended:
                    out_high(7, 8)
                act.wait_ge(s["lr_ps"], t.done())
                wait(act, s["la_s"], t.done(lag=1))
                a.activation(la_e[:], decay_ps[:, 0:GLA_KW], ACT.Abs).then_inc(s["la_abs"], 1)
                act.wait_ge(s["la_abs"], t.done())
                a.activation(la_e[:], la_e[:], ACT.Exp, scale=-1.0).then_inc(s["la_exp"], 1)
                act.wait_ge(s["la_exp"], t.done())
                a.activation(la_e[:], la_e[:], ACT.Ln, bias=1.0).then_inc(s["la_ln"], 1)
                if ended:
                    out_high(8, KM)
                if project:
                    project_out(GQK, n)
                    pad_queries(n)
                if more:
                    x_high(n.moved(1))
                act.wait_ge(s["s_d_s"], t.done(2))
                a.activation(probs, probs, ACT.Exp).then_inc(s["s_exp_s"], 1)
                act.wait_ge(s["s_diff_s"], t.done())
                a.activation(s_sink, s_diff, ACT.Exp).then_inc(s["s_sink_s"], 1)
                if project:
                    project_out(XQZ, n)
                act.wait_ge(s["decay_cum"], t.done())
                wait(act, s["k_dec_s"], t.done(lag=1))
                a.activation(decay[:], decay_ps[:, 0:GLA_KW], ACT.Exp).then_inc(s["decay_s"], 1)
                wait(act, s["state_s"], t.done(4, lag=1))
                a.activation(g_end, kv_ps[:, GLA_KW:GLA_KW + 4], ACT.Exp).then_inc(s["g_end_s"], 1)
                if ending:
                    out_sums(0)
                    out_sums(1)
                if more:
                    hT_high(n.moved(1))
                act.wait_ge(s["x_d_s"], t.done(2))
                a.activation(xprobs, xprobs, ACT.Exp, scale=SCALE).then_inc(s["x_exp_s"], 1)
                if project:
                    act.wait_ge(s["kv_done"], t.done())
                    project_out(GV, n)
                if ending:
                    out_sums(2)
                    out_sums(3)
                act.wait_ge(s["pTa_ps"], t.done())
                wait(act, s["os_ps"], t.done(lag=1))
                a.activation(probsT[:, 0:4, :], turn[0][:], ACT.Copy).then_inc(s["pTa_s"], 1)
                if project:
                    project_out(GZ, n)
                if ending:
                    out_sums(4)
                wait(act, s["ox_ps"], t.done(lag=1))
                for half in range(2):
                    act.wait_ge(s[("xTa_ps", "xTb_ps")[half]], t.done())
                    a.activation(xprobsT_hi[:, 4 * half:4 * half + 4, :], turn[half][:], ACT.Copy, scale=PROB_UP)\
                        .then_inc(s["xT_hi_out"], 1)
                if ending:
                    out_high(0, 4)
                if ended:
                    mix_high(Tile(0, 0))
                if project:
                    project_out(SZ, n)
                act.wait_ge(s["og_ps"], t.done())
                wait(act, s["o_ms_s"], t.done(lag=1))
                act.wait_ge(s["sz_out"], n.done() if project else TILES)
                for h in range(GLA_H):
                    a.activation(tanh_z[:, h * GLA_DV:(h + 1) * GLA_DV], gla_out(h), ACT.Square,
                                 accum_out=o_ss[:, h:h + 1]).then_inc(s["o_ss_s"], 1)

            iterations(act, body)

            mixT_high(Tile(0, 0))
            mix_high(Tile(0, 1))

            def out_body(b, more):
                if more:
                    mixT_high(b.moved(1))
                if more == 2:
                    mix_high(b.moved(2))
                act.wait_ge(s["y_res0"], b.done())
                act.wait_ge(s["y_res1"], b.done())
                a.activation(gates[:, 0, 0:D], y, ACT.Square, accum_out=x_ss).then_inc(s["y_ss"], 1)

            out_iterations(act, out_body)

        @block.vector
        def _(dve):
            v = nc.vector

            def x_mean(t):
                dve.wait_ge(s["x_ss_s"], t.done())
                wait(dve, s["x_rs_s"], t.done(lag=1))
                v.tensor_scalar(x_ms, x_ss, 1.0 / D / X_UP ** 2, EPS / X_UP ** 2, ALU.mult, ALU.add)\
                    .then_inc(s["x_ms_s"], 1)

            dve.wait_ge(s["small_in"], 16 * 7)
            steps = [0]

            def step(ins):
                steps[0] += 1
                ins.then_inc(s["set_up_steps"], 1)
                dve.wait_ge(s["set_up_steps"], steps[0])

            posf = la[:, 0:TILES]
            ang = cos_sin[:, :, 1, :]
            turns_f = gates[:, 0, 0:TILES * ROPE_HALF].rearrange("p (t j) -> p t j", j=ROPE_HALF)
            turns_i = gates[:, 1, 0:TILES * ROPE_HALF].bitcast(I32).rearrange("p (t j) -> p t j", j=ROPE_HALF)
            step(v.tensor_copy(posf, la_e[:, 0:TILES].bitcast(I32)))
            inv = np.float32(1.0) / np.power(np.float32(ROPE_THETA),
                                             np.arange(ROPE_HALF, dtype=np.float32) / np.float32(ROPE_HALF))
            for j in range(ROPE_HALF):
                step(v.tensor_scalar(ang[:, :, j:j + 1], posf.unsqueeze(2), float(inv[j]), None, ALU.mult))
            step(v.tensor_reduce(w_max1, gn, AX, ALU.max, apply_absolute_value=True))
            v.tensor_copy(g_top, w_max1).then_inc(s["g_top_s"], 1)
            for scale, bits, count in ((4096.0, 7, 6), (1.0, 11, 4)):
                step(v.tensor_scalar(turns_i, ang, float(1.0 / (2.0 * np.pi * scale)), None, ALU.mult))
                step(v.tensor_copy(turns_f, turns_i))
                for part in two_pi_parts(scale, bits, count):
                    step(v.scalar_tensor_tensor(out=ang, in0=turns_f, scalar=-part, in1=ang, op0=ALU.mult,
                                                op1=ALU.add))
                if scale > 1.0:
                    x_mean(Tile(0, 0))
            step(v.tensor_scalar(ang, ang, float(np.float32(3.1415925)), float(np.float32(-3.1415925)),
                                 ALU.min, ALU.max))
            step(v.tensor_scalar(turns_f, ang, -1.0, None, ALU.mult))
            v.tensor_tensor(cos_sin[:, :, 0, :], turns_f, ang, ALU.max).then_inc(s["ang_abs"], 1)
            dve.wait_ge(s["ang_abs"], 1)
            v.tensor_scalar(cos_sin[:, :, 0, :], cos_sin[:, :, 0, :], -1.0, float(np.pi / 2), ALU.mult, ALU.add)\
                .then_inc(s["ang_abs"], 1)
            dve.wait_ge(s["ang_abs"], 2)
            v.tensor_copy(turns_f, ang).then_inc(s["ang_done"], 1)

            def x_low(t):
                dve.wait_ge(s["x_rs_s"], t.done())
                dve.wait_ge(s["x_hi_s"], t.done())
                wait(dve, s["xT_lo_ps"], t.done(lag=1))
                v.scalar_tensor_tensor(out=x_lo[:], in0=x_in[:, t.p, :], scalar=x_rs, in1=x_hi[:], op0=ALU.mult,
                                       op1=ALU.subtract).then_inc(s["x_lo_s"], 1)

            def hT_low(t):
                dve.wait_ge(s["xT_lo_ps"], t.done())
                wait(dve, proj_ps[SZ], t.done(lag=2))
                v.tensor_copy(hT_lo[:, t.p, :], turn[1][:].bitcast(F16)).then_inc(s["hT_lo_s"], 1)

            def power_scale(k):
                dve.wait_ge(s["wall_s"], k + 1)
                step(v.tensor_scalar(w_pow.bitcast(I32), w_all[:, k:k + 1].bitcast(I32), EXPONENT, None, ALU.bitwise_and))
                step(v.reciprocal(w_rec, w_pow))

            def group_scale(g):
                power_scale(g)
                v.tensor_scalar(w_scale[:, (g % 2) * KD:(g % 2 + 1) * KD], gn, w_rec, W_UP, ALU.mult, ALU.mult).then_inc(s["wscale2_s"], 1)
                v.tensor_scalar(unscale[:, g:g + 1], w_pow, 1.0 / W_UP / X_UP, None, ALU.mult)\
                    .then_inc(s["unscale_s"], 1)
                v.tensor_scalar(unscale_half[:, g:g + 1], w_pow, 0.5 / W_UP / X_UP, None, ALU.mult)\
                    .then_inc(s["unscale_s"], 1)

            def split_low(g):
                dve.wait_ge(s["wscale2_s"], g + 1)
                dve.wait_ge(s["unscale_s"], 2 * (g + 1))
                wait_raw(dve, g)
                for k in range(HIGH_A, KD):
                    v.tensor_scalar(w_hi(g)[:, k, :], raw(g)[:, k, :], block_scale(g, k), None, ALU.mult)\
                        .then_inc(s["w_hi2_s"], 1)
                for k in range(KD):
                    if k < HIGH_A:
                        dve.wait_ge(s["w_hi_s"], HIGH_A * g + k + 1)
                    else:
                        dve.wait_ge(s["w_hi2_s"], (KD - HIGH_A) * g + k + 1 - HIGH_A)
                    v.scalar_tensor_tensor(out=w_lo(g)[:, k, :], in0=raw(g)[:, k, :], scalar=block_scale(g, k),
                                           in1=w_hi(g)[:, k, :], op0=ALU.mult, op1=ALU.subtract)\
                        .then_inc(s["w_lo_s"], 1)
                    if g + 1 < NG and k == (5 if g >= XQZ else KD - 1):
                        group_scale(g + 1)

            def memory_rows():
                for b in range(MB):
                    dve.wait_ge(s["mem_rs"], b + 1)
                    v.tensor_scalar(mem_in[:, b, :], mem_in[:, b, :], m_rec if b else m_pow, None, ALU.mult)\
                        .then_inc(s["mem_scaled"], 1)

            def split_memory_values():
                dve.wait_ge(s["wall_s"], NG + 1)
                step(v.tensor_scalar(w_all[:, NG:NG + 1], w_all[:, NG:NG + 1], 1e-20, None, ALU.max))
                power_scale(NG)
                step(v.tensor_scalar(v_scale, w_rec, V_UP, None, ALU.mult))
                step(v.tensor_scalar(v_unscale, w_pow, 1.0 / V_UP / PROB_UP, None, ALU.mult))
                step(v.tensor_scalar(xa_unscale, unscale_half[:, XQZ:XQZ + 1], v_unscale, None, ALU.mult))
                v.tensor_scalar(mem_v_hi[:], mem_v[:], v_scale, None, ALU.mult).then_inc(s["v_split_s"], 1)
                dve.wait_ge(s["v_split_s"], 1)
                v.scalar_tensor_tensor(out=mem_v_lo[:], in0=mem_v[:], scalar=v_scale, in1=mem_v_hi[:], op0=ALU.mult,
                                       op1=ALU.subtract).then_inc(s["v_split_s"], 1)

            def memory_turned():
                for k in range(KD):
                    dve.wait_ge(s["mem_T"], k // 2 + 1)
                    v.tensor_scalar(memT[:, k, :], mem_banks[k // 2][:, (k % 2) * MEM:(k % 2 + 1) * MEM],
                                    gm[:, k:k + 1], None, ALU.mult).then_inc(s["mem_T_out"], 1)

            group_scale(KVL)
            for b in range(MB):
                dve.wait_ge(s["mem_sq"], b + 1)
                v.tensor_scalar(m_scale if b else m_amax, (s_mx if b == 0 else s_m)[:, 0:1], 1.0 / D, EPS,
                                ALU.mult, ALU.add).then_inc(s["mem_ms"], 1)
            x_low(Tile(0, 0))
            hT_low(Tile(0, 0))
            memory_rows()

            def project_out(g, n):
                ps = proj_bank(n, g)
                if g == SQ:
                    dve.wait_ge(proj_ps[g], n.done())
                    v.tensor_scalar(qkv[:, n.p, 0:SWA_W], ps[:], unscale[:, g:g + 1], None, ALU.mult)\
                        .then_inc(s["sq_out"], 1)
                elif g in (XQZ, GZ, SZ):
                    dve.wait_ge(s["tanh_s"], n.done(3) - {XQZ: 2, GZ: 1, SZ: 0}[g])
                    cols, at, name = {XQZ: (slice(XA_W, 2 * XA_W), GLA_W + SWA_W, "xz_out"),
                                      GZ: (slice(0, 512), 0, "gz_out"), SZ: (slice(0, 512), GLA_W, "sz_out")}[g]
                    width = cols.stop - cols.start
                    v.scalar_tensor_tensor(out=gates[:, n.p, at:at + width], in0=tanh_z[:, 0:width], scalar=1.0,
                                           in1=ps[:, cols], op0=ALU.add, op1=ALU.mult).then_inc(s[name], 1)
                    if g == XQZ:
                        wait(dve, s["gqT_ps"], n.done(lag=1))
                        v.tensor_scalar(xq[:], ps[:, 0:XA_W], unscale[:, g:g + 1], None, ALU.mult)\
                            .then_inc(s["xq_out"], 1)

            def tile_cos_sin(n):
                wait(dve, s["rope_t_s"], n.done(4, lag=1))
                v.tensor_scalar(cs[:], cos_sin[:, bass.ds(n.index(), 1)], 1.0, None, ALU.mult)\
                    .then_inc(s["cs_s"], 1)

            def pad_keys(n):
                dve.wait_ge(s["rope_s"], n.done(2))
                dve.wait_ge(s["misc_set"], 10)
                wait(dve, s["kT_ps"], n.done(lag=1))
                k = qkv[:, n.p, SWA_W:SWA_W + SWA_KVW].rearrange("p (h d) -> p h d", d=HD)
                v.tensor_copy(k_win[:, n.p, :, 1, :], k).then_inc(s["k_win_s"], 1)
                v.tensor_copy(k_win[0:CHUNK, n.p, :, 0, :], k[0:CHUNK]).then_inc(s["k_win_s"], 1)
                v.tensor_copy(k_win[CHUNK:P, 1 - n.p, :, 0, :], k[CHUNK:P]).then_inc(s["k_win_s"], 1)

            def pad_values(n):
                wait(dve, s["os_ps"], n.done(lag=1))
                dve.wait_ge(s["kvl_out"], n.done())
                dve.wait_ge(s["misc_set"], 10)
                val = qkv[:, n.p, SWA_W + SWA_KVW:SWA_W + 2 * SWA_KVW]
                v.tensor_copy(v_win[0:CHUNK, n.p, :], val[0:CHUNK]).then_inc(s["v_win_s"], 1)
                v.tensor_copy(v_win[CHUNK:P, 1 - n.p, :], val[CHUNK:P]).then_inc(s["v_win_s"], 1)

            def out_scale():
                dve.wait_ge(s["w_sum_s"], NG + KM // WO_SUM)
                step(v.tensor_reduce(w_max1, w_max[:, 0:KM // WO_SUM], AX, ALU.add))
                v.tensor_scalar(w_max1, w_max1, 1e-20, None, ALU.add).then_inc(s["wmax1"], 1)
                power_scale(NG + 1)
                v.tensor_scalar(w_scale[:, 0:KM], minus_half[:, 0:1].to_broadcast([P, KM]), w_rec, -2.0 * W_UP,
                                ALU.mult, ALU.mult).then_inc(s["wo_cols"], 1)
                dve.wait_ge(s["wo_cols"], 1)
                v.tensor_scalar(w_scale[:, 0:GLA_H], w_scale[:, 0:GLA_H], gg, None, ALU.mult)\
                    .then_inc(s["wo_cols"], 1)
                step(v.tensor_scalar(w_out_un, w_pow, 1.0 / W_UP / M_UP, None, ALU.mult))
                dve.wait_ge(s["wo_cols"], 2)

            def out_low(k0, k1):
                for k in range(k0, k1):
                    dve.wait_ge(s["w_hi_s"], HIGH_A * NG + k + 1)
                    v.scalar_tensor_tensor(out=wo_lo[:, k, :], in0=wo_raw[:, k, :], scalar=w_scale[:, k:k + 1],
                                           in1=wo_hi[:, k, :], op0=ALU.mult, op1=ALU.subtract).then_inc(s["w_lo_s"], 1)

            def mix_low(b):
                dve.wait_ge(m_in_s[b.p], b.done_alike())
                wait(dve, s["b_hi"], b.done(lag=1))
                wait(dve, s["b_lo"], b.done(lag=1))
                v.tensor_reduce(m_amax, m_in[b.p], AX, ALU.max, apply_absolute_value=True).then_inc(s["b_chain"], 1)
                dve.wait_ge(s["b_chain"], b.done(4) - 3)
                v.tensor_scalar(m_amax, m_amax, 1e-20, None, ALU.max).then_inc(s["b_chain"], 1)
                dve.wait_ge(s["b_chain"], b.done(4) - 2)
                v.tensor_scalar(m_pow.bitcast(I32), m_amax.bitcast(I32), EXPONENT, None, ALU.bitwise_and)\
                    .then_inc(s["b_chain"], 1)
                dve.wait_ge(s["b_chain"], b.done(4) - 1)
                v.reciprocal(m_rec, m_pow).then_inc(s["b_chain"], 1)
                dve.wait_ge(s["b_chain"], b.done(4))
                v.tensor_scalar(m_scale, m_rec, M_UP, None, ALU.mult).then_inc(s["b_scale"], 1)
                wait(dve, s["b_un_now"], b.done(lag=2))
                v.tensor_scalar(m_un[:, b.p:b.p + 1], m_pow, w_out_un, None, ALU.mult).then_inc(s["b_un"], 1)
                dve.wait_ge(s["b_hi"], b.done())
                wait(dve, s["bT_lo"], b.done(lag=1))
                v.scalar_tensor_tensor(out=m_lo, in0=m_in[b.p], scalar=m_scale, in1=m_hi, op0=ALU.mult,
                                       op1=ALU.subtract).then_inc(s["b_lo"], 1)

            def mixT_low(b):
                dve.wait_ge(s["bT_lo"], b.done())
                wait(dve, s["y_ps1"], b.done(lag=2))
                v.tensor_copy(mT_lo[b.p][:, 0:D], score[0][:].bitcast(F16)).then_inc(s["bT_lo_s"], 1)
                v.tensor_copy(mT_lo[b.p][:, D:D_MIX], score[1][:].bitcast(F16)[:, 0:D_MIX - D])\
                    .then_inc(s["bT_lo_s"], 1)

            def body(n, project, attend, first=False, last=False):
                t = n.moved(-1)
                tp = t.p
                if not attend:
                    for g in range(NG):
                        split_low(g)
                        if g == KVL:
                            memory_turned()
                        if g == SQ:
                            dve.wait_ge(s["cos_done"], 1)
                            tile_cos_sin(n)
                        if g == GQK:
                            x_mean(n.moved(1))
                        if g == GZ:
                            dve.wait_ge(s["memv_out"], MB)
                            v.tensor_reduce(w_max1, mem_v[:].rearrange("p b c -> p (b c)"), AX, ALU.max,
                                            apply_absolute_value=True).then_inc(s["wmax1"], 1)
                        if g == SZ:
                            split_memory_values()
                        if g >= 2:
                            project_out(g - 2, n)
                            if g - 2 == GQK:
                                pad_keys(n)
                                x_low(n.moved(1))
                    project_out(NG - 2, n)
                    project_out(NG - 1, n)
                    hT_low(n.moved(1))
                    pad_values(n)
                    return
                more = project and not (last and project)
                ending, ended = last and project, last and not project
                if project:
                    tile_cos_sin(n)
                dve.wait_ge(s["kT_ps"], t.done())
                wait(dve, s["s_ps"], t.done(lag=1))
                v.tensor_copy(kT[:].rearrange("p a b -> p (a b)"), turn[0][:, 0:2 * P]).then_inc(s["kT_s"], 1)
                wait(dve, s["lr_ps"], t.done(lag=1))
                v.tensor_copy(lrT[0:GLA_LR, :], turn[0][0:GLA_LR, 2 * P:3 * P]).then_inc(s["lrT_s"], 1)
                if project:
                    project_out(SQ, n)
                dve.wait_ge(s["gqT_ps"], t.done())
                wait(dve, s["og_ps"], t.done(lag=1))
                v.tensor_scalar(gqT.rearrange("p j t -> p (j t)"), turn[1][:, 0:2 * P], GLA_DK ** -0.5, None, ALU.mult)\
                    .then_inc(s["gqT_s"], 1)
                wait(dve, s["x_ps"], t.done(lag=1))
                v.tensor_copy(xqT[:].rearrange("p a b -> p (a b)"), turn[1][:, 2 * P:4 * P]).then_inc(s["xqT_s"], 1)
                if ended:
                    out_low(4, 8)
                if more:
                    x_mean(n.moved(1))
                dve.wait_ge(s["la_ln"], t.done())
                wait(dve, s["decay_cum"], t.done(lag=1))
                v.scalar_tensor_tensor(out=la[:], in0=decay_ps[:, 0:GLA_KW], scalar=0.0, in1=la_e[:], op0=ALU.min,
                                       op1=ALU.subtract).then_inc(s["la_s"], 1)
                if project:
                    pad_keys(n)
                dve.wait_ge(s["s_ps"], t.done())
                if first:
                    for b in range(2):
                        v.memset(score[b][0:CHUNK, :].rearrange("p (h k) -> p h k", h=4)[:, :, CHUNK:P], NEG)\
                            .then_inc(s["state0"], 1)
                    dve.wait_ge(s["state0"], 2)
                for b in range(2):
                    v.tensor_reduce(s_mx[:, 4 * b:4 * b + 4], score[b][:].rearrange("p (h k) -> p h k", h=4), AX,
                                    ALU.max).then_inc(s["s_mx_s"], 1)
                dve.wait_ge(s["s_mx_s"], t.done(2))
                v.scalar_tensor_tensor(out=s_m, in0=s_mx, scalar=SCALE, in1=sink_b[:], op0=ALU.mult, op1=ALU.max)\
                    .then_inc(s["s_m_s"], 1)
                dve.wait_ge(s["s_m_s"], t.done())
                wait(dve, s["pTa_ps"], t.done(lag=1))
                wait(dve, s["pTb_ps"], t.done(lag=1))
                for b in range(2):
                    v.scalar_tensor_tensor(out=probs[:, 4 * b:4 * b + 4, :],
                                           in0=score[b][:].rearrange("p (h k) -> p h k", h=4), scalar=SCALE,
                                           in1=s_m[:, 4 * b:4 * b + 4].unsqueeze(2).to_broadcast([P, 4, P]),
                                           op0=ALU.mult, op1=ALU.subtract).then_inc(s["s_d_s"], 1)
                wait(dve, s["s_sink_s"], t.done(lag=1))
                v.tensor_tensor(s_diff, sink_b[:], s_m, ALU.subtract).then_inc(s["s_diff_s"], 1)
                if ended:
                    out_low(8, KM)
                if more:
                    x_low(n.moved(1))
                dve.wait_ge(s["s_exp_s"], t.done())
                wait(dve, s["s_gate_s"], t.done(lag=1))
                v.tensor_reduce(s_den2, probs, AX, ALU.add).then_inc(s["s_den_s"], 1)
                dve.wait_ge(s["s_den_s"], t.done())
                dve.wait_ge(s["s_sink_s"], t.done())
                v.tensor_tensor(s_den2, s_den2, s_sink, ALU.add).then_inc(s["s_den2_s"], 1)
                dve.wait_ge(s["s_den2_s"], t.done())
                if project:
                    project_out(XQZ, n)
                if more:
                    hT_low(n.moved(1))
                dve.wait_ge(s["decay_s"], t.done())
                dve.wait_ge(s["gqk_out"], t.done())
                wait(dve, s["kv_done"], t.done(lag=1))
                v.tensor_tensor(k_dec, gqk[:, tp, GLA_KW:2 * GLA_KW], decay[:], ALU.mult).then_inc(s["k_dec_s"], 1)
                dve.wait_ge(s["x_ps"], t.done())
                for b in range(2):
                    v.tensor_reduce(c_mx[:, 2 * b:2 * b + 2], score[b][:].rearrange("p (h k) -> p h k", h=2), AX,
                                    ALU.max).then_inc(s["x_mx_s"], 1)
                dve.wait_ge(s["x_mx_s"], t.done(2))
                wait(dve, s["xTa_ps"], t.done(lag=1))
                wait(dve, s["xTb_ps"], t.done(lag=1))
                for b in range(2):
                    v.tensor_tensor(xprobs[:, 2 * b:2 * b + 2, :], score[b][:].rearrange("p (h k) -> p h k", h=2),
                                    c_mx[:, 2 * b:2 * b + 2].unsqueeze(2).to_broadcast([P, 2, MEM]),
                                    ALU.subtract).then_inc(s["x_d_s"], 1)
                v.reciprocal(s_rden, s_den2).then_inc(s["s_rden_s"], 1)
                dve.wait_ge(s["pTb_ps"], t.done())
                wait(dve, s["os_ps"], t.done(lag=1))
                v.tensor_copy(probsT[:, 4:8, :].rearrange("p a b -> p (a b)"), turn[1][:]).then_inc(s["pTb_s"], 1)
                dve.wait_ge(s["kv_done"], t.done())
                dve.wait_ge(s["g_end_s"], t.done())
                wait(dve, s["og_ps"], t.done(lag=1))
                for c in range(2):
                    for j in range(2):
                        if c or not first:
                            dve.wait_ge(s["state_s"], (t.done(4) - 2) if c else t.done(4, lag=1))
                        v.scalar_tensor_tensor(out=state[:, c, j, :], in0=state[:, 1 - c, j, :],
                                               scalar=g_end[:, 2 * j + c:2 * j + c + 1],
                                               in1=kv_banks[c][:, j * GLA_DV:(j + 1) * GLA_DV],
                                               op0=ALU.mult, op1=ALU.add).then_inc(s["state_s"], 1)
                dve.wait_ge(s["x_exp_s"], t.done())
                wait(dve, s["x_gate_s"], t.done(lag=1))
                v.tensor_reduce(c_mx, xprobs, AX, ALU.add).then_inc(s["x_den_s"], 1)
                dve.wait_ge(s["x_den_s"], t.done())
                v.reciprocal(c_rden, c_mx).then_inc(s["x_rden_s"], 1)
                if project:
                    project_out(GZ, n)
                wait(dve, s["ox_ps"], t.done(lag=1))
                for half in range(2):
                    dve.wait_ge(s["xT_hi_out"], t.done(2) - 1 + half)
                    cols = slice(4 * half, 4 * half + 4)
                    v.scalar_tensor_tensor(out=xprobsT_lo[:, cols, :].rearrange("p a b -> p (a b)"), in0=turn[half][:],
                                           scalar=PROB_UP, in1=xprobsT_hi[:, cols, :].rearrange("p a b -> p (a b)"),
                                           op0=ALU.mult, op1=ALU.subtract)\
                        .then_inc(s[("xTa_s", "xTb_s")[half]], 1)
                if ending:
                    out_scale()
                    out_low(0, 4)
                if ended:
                    mix_low(Tile(0, 0))
                if project:
                    project_out(SZ, n)
                wait(dve, s["mix_out"], t.done(16, lag=1))
                dve.wait_ge(s["os_ps"], t.done())
                dve.wait_ge(s["s_gate_s"], t.done())
                v.tensor_tensor(mix[:, GLA_W:GLA_W + SWA_W], score[1][:], gates[:, tp, GLA_W:GLA_W + SWA_W],
                                ALU.mult).then_inc(s["mix_s"], 1)
                dve.wait_ge(s["o_ss_s"], t.done(4))
                wait(dve, s["o_rs_s"], t.done(lag=1))
                v.tensor_scalar(o_ms, o_ss, 1.0 / GLA_DV, EPS, ALU.mult, ALU.add).then_inc(s["o_ms_s"], 1)
                dve.wait_ge(s["ox_ps"], t.done())
                dve.wait_ge(s["x_gate_s"], t.done())
                v.tensor_tensor(mix[:, GLA_W + SWA_W:D_MIX], decay_ps[:, 0:XA_W], gates[:, tp, GLA_W + SWA_W:D_MIX],
                                ALU.mult).then_inc(s["mix_s"], 1)
                dve.wait_ge(s["o_rc_s"], t.done())
                for h in range(GLA_H):
                    cols = slice(h * GLA_DV, (h + 1) * GLA_DV)
                    v.scalar_tensor_tensor(out=mix[:, cols], in0=gla_out(h), scalar=o_rc[:, h:h + 1],
                                           in1=gates[:, tp, cols], op0=ALU.mult, op1=ALU.mult)\
                        .then_inc(s["mix_s"], 1)
                if project:
                    pad_values(n)

            iterations(dve, body)

            mixT_low(Tile(0, 0))
            mix_low(Tile(0, 1))

            def out_body(b, more):
                un = m_un_now[:, b.p:b.p + 1]
                dve.wait_ge(s["b_un"], b.done())
                v.tensor_copy(un, m_un[:, b.p:b.p + 1]).then_inc(s["b_un_now"], 1)
                dve.wait_ge(s["b_un_now"], b.done())
                dve.wait_ge(xr_in_s[b.p], b.done_alike())
                wait(dve, s["y_out"], b.done(16, lag=1))
                for h in range(2):
                    dve.wait_ge(s[f"y_ps{h}"], b.done())
                    ps = (proj if h == 0 else (decay_ps, kv_ps))[b.p]
                    cols = slice(h * 512, (h + 1) * 512)
                    v.scalar_tensor_tensor(out=y[:, cols], in0=ps[:], scalar=un, in1=x_in[:, b.p, cols],
                                           op0=ALU.mult, op1=ALU.add).then_inc(s[f"y_res{h}"], 1)
                    if more and h == 0:
                        mixT_low(b.moved(1))
                    if more == 2 and h == 0:
                        mix_low(b.moved(2))
                dve.wait_ge(s["y_ss"], b.done())
                v.tensor_scalar(x_ms, x_ss, 1.0 / D, EPS, ALU.mult, ALU.add).then_inc(s["y_ms"], 1)
                dve.wait_ge(s["y_rs"], b.done())
                if not isinstance(b.m, int) or b.index() < 2:
                    dve.wait_ge(s["gfin_in"], 16)
                v.scalar_tensor_tensor(out=y, in0=y, scalar=x_rs, in1=g_fin, op0=ALU.mult, op1=ALU.mult)\
                    .then_inc(s["y_fin"], 1)

            out_iterations(dve, out_body)

        @block.tensor
        def _(pe):
            t_ = nc.tensor

            def mm(o, l, r, first, last):
                return t_.matmul(o, lhsT=l, rhs=r, start=first, stop=last)

            def x_turn(t):
                for half, bk, ready, done in ((x_hi, turn[0], "x_hi_s", "xT_hi_ps"), (x_lo, turn[1], "x_lo_s", "xT_lo_ps")):
                    pe.wait_ge(s[ready], t.done())
                    for k in range(KD):
                        i = t_.transpose(bk[:].bitcast(F16)[:, k * P:(k + 1) * P], half[:, k * P:(k + 1) * P], ident16[:])
                    i.then_inc(s[done], 1)

            def project(g, n):
                pe.wait_ge(s["hT_hi_s"], n.done())
                pe.wait_ge(s["hT_lo_s"], n.done())
                ps = proj_bank(n, g)[:, 0:GCOLS[g]]
                two_back = (g - 2) % NG
                wait(pe, s[last_reader[two_back]], n.done(lag=1 if g < 2 else 0))
                for k in range(KD):
                    hi = hT_hi[:, n.p, k * P:(k + 1) * P]
                    lo = hT_lo[:, n.p, k * P:(k + 1) * P]
                    mm(ps, hi, w_hi(g)[:, k, :], k == 0, False)
                    mm(ps, hi, w_lo(g)[:, k, :], False, False)
                    i = mm(ps, lo, w_hi(g)[:, k, :], False, k == KD - 1)
                i.then_inc(proj_ps[g], 1)

            pe.wait_ge(s["id_set"], 2)
            x_turn(Tile(0, 0))
            pe.wait_ge(s["mem_scaled"], 2)
            for k in range(KD):
                for b in range(MB):
                    ins = t_.transpose(mem_banks[k // 2][:, ((k % 2) * MB + b) * P:((k % 2) * MB + b + 1) * P],
                                       mem_in[:, b, k * P:(k + 1) * P], ident[:])
                if k % 2:
                    ins.then_inc(s["mem_T"], 1)

            def memory_keys():
                pe.wait_ge(s["mem_T_out"], KD)
                pe.wait_ge(s["memw_in"], 16)
                for j in range(2):
                    for k in range(KD):
                        ins = mm(score[j][:, 0:MEM], mem_w[:, k, j * P:(j + 1) * P], memT[:, k, :], k == 0, k == KD - 1)
                    ins.then_inc(s["memk_ps"], 1)

            def memory_values():
                pe.wait_ge(s["memk_out"], 2)
                for b in range(MB):
                    for k in range(KD):
                        ins = mm(score[b][:, 256:256 + XA_W], memT[:, k, b * P:(b + 1) * P],
                                 mem_w[:, k, XA_W:2 * XA_W], k == 0, k == KD - 1)
                    ins.then_inc(s["memv_ps"], 1)

            def body(n, project_, attend, first=False, last=False):
                t = n.moved(-1)
                tp = t.p
                more = project_ and not (last and project_)
                if not attend:
                    for g in range(NG):
                        split_through(pe, g)
                        project(g, n)
                        if g == KVL:
                            memory_keys()
                            memory_values()
                        if g == GV:
                            x_turn(n.moved(1))
                    return
                if project_:
                    project(KVL, n)
                if first:
                    pe.wait_ge(s["hT_hi_s"], 2)
                    pe.wait_ge(s["hT_lo_s"], 2)
                    pe.wait_ge(s["v_split_s"], 2)
                pe.wait_ge(s["k_win_s"], t.done(3))
                pe.wait_ge(s["kvl_out"], t.done())
                wait(pe, s["xTa_s"], t.done(lag=1))
                for h in range(SWA_KV):
                    i = t_.transpose(turn[0][:, h * P:(h + 1) * P],
                                     k_win[:, tp, h].rearrange("p a b -> p (a b)"), ident[:])
                i = t_.transpose(turn[0][0:GLA_LR, 2 * P:3 * P], qkv[:, tp, SWA_W + 2 * SWA_KVW:], ident[:])
                i.then_inc(s["kT_ps"], 1)
                pe.wait_ge(s["q_pad_s"], t.done(2))
                wait(pe, s["xTb_s"], t.done(lag=1))
                for h in range(4):
                    i = t_.transpose(turn[1][:, h * P:(h + 1) * P], q_pad[:, h].rearrange("p a b -> p (a b)"), ident[:])
                i.then_inc(s["qTa_ps"], 1)
                if project_:
                    project(SQ, n)
                pe.wait_ge(s["kT_s"], t.done())
                pe.wait_ge(s["lrT_s"], t.done())
                for h in range(4):
                    i = t_.transpose(turn[0][:, h * P:(h + 1) * P], q_pad[:, 4 + h].rearrange("p a b -> p (a b)"),
                                     ident[:])
                i.then_inc(s["qTb_ps"], 1)
                pe.wait_ge(s["qTa_s"], t.done())
                pe.wait_ge(s["gqk_out"], t.done())
                pe.wait_ge(s["xq_out"], t.done())
                for j in range(2):
                    t_.transpose(turn[1][:, j * P:(j + 1) * P], gqk[:, tp, j * P:(j + 1) * P], ident[:])
                for j in range(2):
                    i = t_.transpose(turn[1][:, (2 + j) * P:(3 + j) * P], xq[:, j * P:(j + 1) * P], ident[:])
                i.then_inc(s["gqT_ps"], 1)
                wait(pe, s["mix_s"], t.done(6, lag=1))
                mm(decay_ps[:, 0:GLA_KW], lrT[0:GLA_LR + 1, :], wa2[0:GLA_LR + 1, :], True, True)\
                    .then_inc(s["lr_ps"], 1)
                if project_:
                    project(GQK, n)
                pe.wait_ge(s["qTb_s"], t.done())
                for h in range(SWA_H):
                    i = mm(score[h // 4][:, (h % 4) * P:(h % 4 + 1) * P], qT_pad[:, h, :],
                           kT[:, h // (SWA_H // SWA_KV), :], True, True)
                i.then_inc(s["s_ps"], 1)
                if project_:
                    project(XQZ, n)
                pe.wait_ge(s["la_s"], t.done())
                mm(decay_ps[:, 0:GLA_KW], later[:], la[:], True, True)
                for j in range(2):
                    i = mm(kv_ps[:, GLA_KW + 2 * j:GLA_KW + 2 * j + 2], la[:, j * P:(j + 1) * P], halves[:],
                           True, True)
                i.then_inc(s["decay_cum"], 1)
                pe.wait_ge(s["s_d_s"], t.done(2))
                pe.wait_ge(s["xqT_s"], t.done())
                for h in range(XA_H):
                    rows = slice((h % 2) * HD, (h % 2 + 1) * HD)
                    i = mm(score[h % 2][:, (h // 2) * MEM:(h // 2 + 1) * MEM], xqT[rows, h // 2, :],
                           memT_k[rows, h // 2, :], True, True)
                i.then_inc(s["x_ps"], 1)
                if more:
                    pe.wait_ge(s["gqT_s"], t.done())
                    x_turn(n.moved(1))
                if project_:
                    project(GV, n)
                if more:
                    pe.wait_ge(s["hT_hi_s"], n.done(lag=-1))
                    pe.wait_ge(s["hT_lo_s"], n.done(lag=-1))
                pe.wait_ge(s["gqT_s"], t.done())
                pe.wait_ge(s["s_exp_s"], t.done())
                for half, done in ((0, "pTa_ps"), (1, "pTb_ps")):
                    if half:
                        pe.wait_ge(s["k_dec_s"], t.done())
                        if not project_ or first:
                            pe.wait_ge(s["gv_out"], t.done())
                        pe.wait_ge(s["g_end_s"], t.done())
                        wait(pe, s["state_s"], t.done(4, lag=1))
                    for h in range(4):
                        i = t_.transpose(turn[half][:, h * P:(h + 1) * P], probs[:, 4 * half + h, :], ident[:])
                    i.then_inc(s[done], 1)
                for j in range(2):
                    for b in range(2):
                        for c in range(2):
                            h, frames = 2 * j + b, slice(c * CHUNK, (c + 1) * CHUNK)
                            i = mm(kv_banks[c][b * GLA_DK:(b + 1) * GLA_DK, j * GLA_DV:(j + 1) * GLA_DV],
                                   k_dec[frames, h * GLA_DK:(h + 1) * GLA_DK],
                                   gv[frames, h * GLA_DV:(h + 1) * GLA_DV], True, True)
                i.then_inc(s["kv_done"], 1)
                if project_:
                    project(GZ, n)
                pe.wait_ge(s["x_exp_s"], t.done())
                pe.wait_ge(s["pTa_s"], t.done())
                pe.wait_ge(s["pTb_s"], t.done())
                for half, done in ((0, "xTa_ps"), (1, "xTb_ps")):
                    for i4 in range(4):
                        h, b = 2 * half + i4 // MB, i4 % MB
                        i = t_.transpose(turn[half][:, i4 * P:(i4 + 1) * P], xprobs[:, h, b * P:(b + 1) * P], ident[:])
                    i.then_inc(s[done], 1)
                pe.wait_ge(s["v_win_s"], t.done(2))
                for h in range(SWA_H):
                    kv = slice((h // 4) * HD, (h // 4 + 1) * HD)
                    mm(score[1][0:CHUNK, h * HD:(h + 1) * HD], probsT[:, h, 0:CHUNK], v_win[:, tp, kv], True, True)
                    i = mm(score[1][CHUNK:P, h * HD:(h + 1) * HD], probsT[:, h, CHUNK:P],
                           qkv[:, tp, SWA_W + SWA_KVW + kv.start:SWA_W + SWA_KVW + kv.stop], True, True)
                i.then_inc(s["os_ps"], 1)
                if project_:
                    project(SZ, n)
                pe.wait_ge(s["xTa_s"], t.done())
                pe.wait_ge(s["xTb_s"], t.done())
                pe.wait_ge(s["g_end_s"], t.done())
                pe.wait_ge(s["state_s"], t.done(4))
                for slot, h in enumerate(xa_order):
                    cols = slice(h * HD, (h + 1) * HD)
                    for b in range(MB):
                        hi, lo = xprobsT_hi[:, slot * MB + b, :], xprobsT_lo[:, slot * MB + b, :]
                        mm(decay_ps[:, cols], hi, mem_v_hi[:, b, cols], b == 0, False)
                        mm(decay_ps[:, cols], hi, mem_v_lo[:, b, cols], False, False)
                        i = mm(decay_ps[:, cols], lo, mem_v_hi[:, b, cols], False, b == MB - 1)
                i.then_inc(s["ox_ps"], 1)
                for j in range(2):
                    for c in range(2):
                        for b in range(2):
                            rows, frames = slice(b * GLA_DK, (b + 1) * GLA_DK), slice(c * CHUNK, (c + 1) * CHUNK)
                            i = mm(gla_out(2 * j + b)[frames], gqT[rows, j, frames], state[rows, c, j, :], True, True)
                i.then_inc(s["og_ps"], 1)

            iterations(pe, lambda n, project, attend, first=False, last=False:
                       body(n, project, attend, first, last))

            def mix_turn(b):
                for half, banks, ready, done, free in ((m_hi, turn, "b_hi", "bT_hi", "bT_hi_s"),
                                                       (m_lo, score, "b_lo", "bT_lo", "bT_lo_s")):
                    if isinstance(b.m, int) and b.index() == 0 and half is m_lo:
                        pe.wait_ge(s["mix_s"], 6 * TILES)
                    pe.wait_ge(s[ready], b.done())
                    wait(pe, s[free], b.done(2, lag=1))
                    for k in range(KM):
                        i = t_.transpose(banks[k // 8][:].bitcast(F16)[:, (k % 8) * P:(k % 8 + 1) * P],
                                         half[:, k * P:(k + 1) * P], ident16[:])
                    i.then_inc(s[done], 1)

            mix_turn(Tile(0, 0))
            pe.wait_ge(s["w_hi_s"], HIGH_A * NG + KM)
            pe.wait_ge(s["w_lo_s"], KD * NG + KM)

            def out_body(b, more):
                pe.wait_ge(s["bT_hi_s"], b.done(2))
                pe.wait_ge(s["bT_lo_s"], b.done(2))
                for h in range(2):
                    ps = (proj if h == 0 else (decay_ps, kv_ps))[b.p]
                    wait(pe, s[f"y_res{h}"], b.done(lag=2))
                    cols = slice(h * 512, (h + 1) * 512)
                    for k in range(KM):
                        hi = mT_hi[b.p][:, k * P:(k + 1) * P]
                        lo = mT_lo[b.p][:, k * P:(k + 1) * P]
                        mm(ps[:], hi, wo_hi[:, k, cols], k == 0, False)
                        mm(ps[:], hi, wo_lo[:, k, cols], False, False)
                        i = mm(ps[:], lo, wo_hi[:, k, cols], False, k == KM - 1)
                    i.then_inc(s[f"y_ps{h}"], 1)
                    if h == 0 and more:
                        mix_turn(b.moved(1))

            out_iterations(pe, out_body)


_OUT = (1, SEQ, D)


def kernel(**inputs):
    import numpy as _np
    import concourse.bacc as _bacc
    from concourse import mybir as _mybir
    from concourse.bass_utils import run_bass_kernel_spmd as _run

    c = _np.ascontiguousarray
    rows = lambda a, k: c(_np.asarray(a).reshape(k, P, -1).transpose(1, 0, 2))
    w_in = _np.asarray(inputs["w_in"])[0]
    arrays = {
        "x": c(_np.asarray(inputs["x"])[0]),
        "mem": c(_np.asarray(inputs["mem"])[0]),
        "pos": c(_np.asarray(inputs["positions"])[0].reshape(TILES, P).T),
        "g_norm": c(_np.asarray(inputs["g_norm"]).reshape(KD, P).T),
        "w_a2": c(_np.asarray(inputs["w_a2"])[0]),
        "b_a": c(_np.asarray(inputs["b_a"])),
        "g_gla": c(_np.asarray(inputs["g_gla"]).reshape(GLA_DV, 1)),
        "sinks": c(_np.asarray(inputs["sinks"])[0]),
        "g_mem": c(_np.asarray(inputs["g_mem"]).reshape(KD, P).T),
        "w_mem": rows(inputs["w_mem_kv"], KD),
        "w_out": rows(inputs["w_out"], KM),
        "g_final": c(_np.asarray(inputs["g_final"])),
    }
    for i, names in enumerate(GROUPS):
        cols = _np.concatenate([w_in[:, _starts[n]:_starts[n] + _width[n]] for n in names], axis=1)
        arrays[f"w_group{i}"] = rows(cols, KD).reshape(P, -1)
    nc = _bacc.Bacc("TRN2", target_bir_lowering=False, num_devices=1, dynamic_dma_scratch_size=4096)
    args = {n: nc.dram_tensor(n, a.shape, _mybir.dt.from_np(a.dtype), kind="ExternalInput").ap()
            for n, a in arrays.items()}
    out = nc.dram_tensor("out", (SEQ, D), F32, kind="ExternalOutput").ap()
    build_kernel(nc, args["x"], args["mem"], args["pos"], args["g_norm"],
                 [args[f"w_group{i}"] for i in range(NG)], args["w_a2"], args["b_a"], args["g_gla"],
                 args["sinks"], args["g_mem"], args["w_mem"], args["w_out"], args["g_final"], out)
    r = _run(nc, [arrays], core_ids=[0])
    return r.results[0]["out"].reshape(_OUT)
```

```python
from contextlib import ExitStack

import numpy as np

import concourse.bass as bass
from concourse import mybir

F32 = mybir.dt.float32
F16 = mybir.dt.float16
I32 = mybir.dt.int32
ALU = mybir.AluOpType
ACT = mybir.ActivationFunctionType
AX = mybir.AxisListType.X

P = 128
SEQ = 4096
D = 1024
KD = D // P
MEM = 256
MB = MEM // P
CHUNK = 64
EPS = 1e-6
TILES = SEQ // P
NEG = -1e30

GLA_H, GLA_DK, GLA_DV, GLA_LR, GLA_TAU = 4, 64, 128, 16, 16.0
GLA_KW, GLA_W = GLA_H * GLA_DK, GLA_H * GLA_DV
SWA_H, SWA_KV, HD = 8, 2, 64
SWA_W, SWA_KVW = SWA_H * HD, SWA_KV * HD
XA_H = 4
XA_W = XA_H * HD
D_MIX = GLA_W + SWA_W + XA_W
KM = D_MIX // P
ROPE_HALF = HD // 8
ROPE_THETA = 500000.0
SCALE = HD ** -0.5

_names = ("gq", "gk", "gv", "gz", "lr", "sq", "sk", "sv", "sz", "xq", "xz")
_widths = (GLA_KW, GLA_KW, GLA_W, GLA_W, GLA_LR, SWA_W, SWA_KVW, SWA_KVW, SWA_W, XA_W, XA_W)
_starts = dict(zip(_names, np.cumsum((0,) + _widths[:-1]).tolist()))
_width = dict(zip(_names, _widths))
GROUPS = (("sk", "sv", "lr"), ("sq",), ("gq", "gk"), ("xq", "xz"), ("gv",), ("gz",), ("sz",))
KVL, SQ, GQK, XQZ, GV, GZ, SZ = range(len(GROUPS))
NG = len(GROUPS)
GCOLS = [sum(_width[n] for n in g) for g in GROUPS]
GOFF = [KD * c for c in np.cumsum([0] + GCOLS[:-1]).tolist()]
W_WORDS = KD * sum(GCOLS)

X_UP = 1024.0
W_UP = 2.0 ** 14
M_UP = 2.0 ** 14
PROB_UP, V_UP, K_UP, XQ_UP = (2.0 ** 14,) * 4
EXPONENT = 0x7F800000
LA_MIN = -30000.0
HIGH_A = 5


def two_pi_parts(scale, bits, count):
    left, parts = 2.0 * np.pi * scale, []
    for _ in range(count):
        lsb = 2.0 ** (np.floor(np.log2(left)) - bits + 1)
        parts.append(float(np.floor(left / lsb) * lsb))
        left -= parts[-1]
    return parts


class Tile:

    def __init__(self, m, p):
        self.m, self.p = m, p

    def moved(self, k):
        n = self.p + k
        return Tile(self.m + n // 2, n % 2)

    def index(self):
        return self.m * 2 + self.p

    def done(self, per=1, lag=0):
        return self.m * (2 * per) + per * (self.p + 1 - lag)

    def done_alike(self, per=16):
        return self.m * per + per


def wait(eng, sem, value):
    if isinstance(value, int) and value <= 0:
        return
    eng.wait_ge(sem, value)


def build_kernel(nc, x, mem, pos, g_norm, w_groups, w_a2, b_a, g_gla, sinks, g_mem, w_mem, w_out, g_final, out):
    ctx = ExitStack()
    with ctx:
        def sb(name, shape, dt=F32):
            return ctx.enter_context(nc.sbuf_tensor(name, shape, dt))

        def sem(name):
            return ctx.enter_context(nc.semaphore(name))

        mix_dram = nc.dram_tensor("mix_rows", [SEQ, D_MIX], F32, kind="Internal").ap()

        W = sb("W", [P, W_WORDS])
        scratch = sb("scratch", [P, 8448])
        x_in = sb("x_in", [P, 2, D])
        x_hi = sb("x_hi", [P, D], F16)
        x_lo = sb("x_lo", [P, D], F16)
        hT_hi = sb("hT_hi", [P, 2, D], F16)
        hT_lo = sb("hT_lo", [P, 2, D], F16)
        qkv = sb("qkv", [P, 2, SWA_W + 2 * SWA_KVW + GLA_LR])
        k_twice = sb("k_twice", [P, SWA_KV, 2, HD])
        v_win = sb("v_win", [P, 2, SWA_KVW])
        kT = sb("kT", [P, SWA_KV, P])
        kT_first = sb("kT_first", [P, 2, SWA_KV, P])
        gqk = sb("gqk", [P, 2, 2 * GLA_KW])
        xq = sb("xq", [P, 2, XA_W], F16)
        xqT = sb("xqT", [P, 2, XA_H // 2, P], F16)
        gv = sb("gv", [P, GLA_W])
        gates = sb("gates", [P, 2, D_MIX])
        tanh_z = sb("tanh_z", [P, 512])
        lrT = sb("lrT", [32, P])
        wa2 = sb("wa2", [32, GLA_KW])
        la = sb("la", [P, GLA_KW])
        la_hi = sb("la_hi", [P, GLA_KW], F16)
        la_lo = sb("la_lo", [P, GLA_KW], F16)
        la_e = sb("la_e", [P, GLA_KW])
        decay = sb("decay", [P, GLA_KW])
        state = sb("state", [P, 2, 2, GLA_DV])
        memT_k = sb("memT_k", [P, XA_H // 2, MEM])
        memT_k_hi = sb("memT_k_hi", [P, XA_H // 2, MEM], F16)
        memT_k_lo = sb("memT_k_lo", [P, XA_H // 2, MEM], F16)
        mem_v = sb("mem_v", [P, MB, XA_W])
        mem_v_hi = sb("mem_v_hi", [P, MB, XA_W], F16)
        mem_v_lo = sb("mem_v_lo", [P, MB, XA_W], F16)
        ident = sb("ident", [P, P])
        ident16 = sb("ident16", [P, P], F16)
        later = sb("later", [P, P])
        later16 = sb("later16", [P, P], F16)
        halves = sb("halves", [P, 2], F16)
        rope_t = sb("rope_t", [P, 4, SWA_H + SWA_KV, ROPE_HALF])
        cos_sin = sb("cos_sin", [P, TILES, 2, ROPE_HALF])
        cs = sb("cs", [P, 2, ROPE_HALF])
        small = sb("small", [P, 224])

        used = [0]

        def column(n):
            used[0] += n
            assert used[0] <= 224
            return small[:, used[0] - n:used[0]]

        gn, gm, gg = column(KD), column(KD), column(1)
        minus_half = column(4)
        unscale, unscale_half = column(NG), column(NG)
        w_max, w_max1, w_pow, w_rec = column(KM), column(1), column(1), column(1)
        g_top, tiny, w_sum, w_bound, w_all = column(1), column(1), column(NG), column(NG), column(NG + 3)
        w_scale = column(2 * KD)
        x_ss, x_ms, x_rs = column(1), column(1), column(1)
        s_mx, s_m, s_diff, s_sink, s_den, s_den2, s_rden = (column(SWA_H) for _ in range(7))
        c_mx, c_den, c_rden = (column(XA_H) for _ in range(3))
        g_end = column(4)
        o_ss, o_ms, o_rs, o_rc = (column(GLA_H) for _ in range(4))
        m_amax, m_pow, m_rec, m_scale = (column(1) for _ in range(4))
        m_un, m_un_now = column(2), column(2)
        w_out_un = column(1)
        v_scale, v_unscale, xa_unscale, k_scale, xq_unscale, x_factor, xq_re = (column(1) for _ in range(7))
        xq_un = column(2)
        sink_b = sb("sink_b", [P, SWA_H])

        def room(at, n, *shape):
            v = scratch[:, at:at + n]
            names = "abcd"[:len(shape)]
            return v.rearrange(f"p ({' '.join(names)}) -> p {' '.join(names)}", **dict(zip(names, shape)))

        probs = room(0, 1024, SWA_H, P)
        probsT = room(1024, 1024, SWA_H, P)
        xprobs = room(2048, 1024, XA_H, MEM)
        xprobsT_hi, xprobsT_lo = (scratch[:, at:at + 512].bitcast(F16).rearrange("p (a b) -> p a b", b=P)
                                  for at in (3072, 3584))
        k_dec = scratch[:, 4096:4096 + GLA_KW]
        qT = room(5120, SWA_W, SWA_H // 2, P)
        gqT = room(6144, GLA_KW, 2, P)
        mix = scratch[:, 7168:8448]
        raw_rooms = (scratch[:, 0:4096], scratch[:, 4096:8192], W[:, GOFF[GV]:GOFF[GV] + 4096],
                     W[:, GOFF[SZ]:GOFF[SZ] + 4096])
        RAW = {KVL: (0, 1), SQ: (1, 1), GQK: (2, 1), XQZ: (0, 2), GV: (1, 2), GZ: (3, 1), SZ: (0, 3)}

        def raw(g):
            return raw_rooms[RAW[g][0]][:, 0:KD * GCOLS[g]].rearrange("p (k c) -> p k c", k=KD)

        def block_scale(g, k):
            return w_scale[:, (g % 2) * KD + k:(g % 2) * KD + k + 1]

        def wait_raw(eng, g):
            eng.wait_ge(w_raw_in[RAW[g][0]], 16 * RAW[g][1])

        def gla_out(h):
            return gla_banks[h % 2][:, (h // 2) * GLA_DV:(h // 2 + 1) * GLA_DV]

        def w_hi(g):
            n = KD * GCOLS[g]
            return W[:, GOFF[g]:GOFF[g] + n // 2].bitcast(F16).rearrange("p (k c) -> p k c", k=KD)

        def w_lo(g):
            n = KD * GCOLS[g]
            return W[:, GOFF[g] + n // 2:GOFF[g] + n].bitcast(F16).rearrange("p (k c) -> p k c", k=KD)

        mem_w = W[:, GOFF[SZ]:GOFF[SZ] + KD * 2 * XA_W].rearrange("p (k c) -> p k c", k=KD)
        mem_in = W[:, GOFF[GZ]:GOFF[GZ] + 2 * D].rearrange("p (b d) -> p b d", b=MB)
        memT = W[:, GOFF[GZ] + 2 * D:GOFF[GZ] + 4 * D].rearrange("p (k m) -> p k m", k=KD)
        wo_raw = W[:, GOFF[SQ]:GOFF[SQ] + KM * D].rearrange("p (k c) -> p k c", k=KM)
        wo_halves = W[:, GOFF[GV]:GOFF[GV] + KM * D].bitcast(F16).rearrange("p (k a c) -> p k a c", k=KM, a=2)
        wo_hi, wo_lo = wo_halves[:, :, 0, :], wo_halves[:, :, 1, :]
        assert GOFF[SQ] + KM * D + 3 * D_MIX // 2 <= GOFF[GV] and GOFF[GV] + KM * D + 3 * D_MIX // 2 <= W_WORDS

        def words(buffer, at, n=D_MIX // 2):
            return buffer[:, at:at + n]

        left_a, left_b = GOFF[SQ] + KM * D, GOFF[GV] + KM * D
        m_in = [words(W, left_b, D_MIX), words(W, GOFF[KVL], D_MIX)]
        m_hi = words(W, left_b + D_MIX).bitcast(F16)
        m_lo = words(W, left_a).bitcast(F16)
        mT_hi = [words(W, left_a + D_MIX // 2).bitcast(F16), words(scratch, 0).bitcast(F16)]
        mT_lo = [words(W, left_a + D_MIX).bitcast(F16), words(scratch, D_MIX // 2).bitcast(F16)]
        y = words(scratch, D_MIX, D)
        g_fin = words(scratch, D_MIX + D, D)
        WO_SUM = 2
        wo_junk = W[:, GOFF[KVL]:GOFF[KVL] + WO_SUM * D].rearrange("p (k c) -> p k c", k=WO_SUM)
        WO_ROOMS = ((SQ, 0, 4), (GQK, 4, 8), (XQZ, 8, KM))

        def bank(name):
            return ctx.enter_context(nc.psum_tensor(name, [P, 512], F32))

        proj = [bank("proj0"), bank("proj1")]
        turn = [bank("turn0"), bank("turn1")]
        score = [bank("score0"), bank("score1")]
        decay_ps = bank("decay_ps")
        kv_ps = bank("kv_ps")

        gla_banks = (score[0], kv_ps)
        kv_banks = (kv_ps[:, 0:2 * GLA_DV], decay_ps[:, 2 * GLA_DV:4 * GLA_DV])
        def even_first(heads):
            return [h for b in range(2) for h in range(b, heads, 2)]

        XQ_STEPS = 5

        def read_out(name, n, lag=0):
            return n.done(XQ_STEPS if name == "xq_out" else 1, lag)

        def low_banks(b):
            return proj if isinstance(b.m, int) and b.index() == 0 else score

        mem_banks = (score[0], score[1], decay_ps, kv_ps)

        sem_names = """
            mem_in_s memw_in gfin_in small_in
            set_up_steps b_chain b_un_now id_set misc_set pads_set
            ang_done ang_abs cos_done
            mem_sq mem_ms mem_rs mem_scaled mem_T mem_T_out memk_ps memk_out memv_ps memv_out v_split_s
            g_top_s w_sum_s w_bound_s wmax1 wall_s wscale2_s w_hi_s w_hi2_s w_lo_s unscale_s
            x_ss_s x_ms_s x_rs_s x_hi_s x_lo_s xT_hi_ps xT_lo_ps hT_hi_s hT_lo_s
            kvl_out sq_out gqk_out tanh_s xz_out xq_out gv_out gz_out sz_out
            cs_s rope_t_s rope_s k_twice_s v_win_s
            kT_ps qT_ps gqT_ps kT_s lrT_s qT_s gqT_s xqT_s
            lr_ps la_abs la_exp la_ln la_s decay_cum decay_s g_end_s k_dec_s
            s_ps s_mx_s s_m_s s_d_s s_diff_s s_exp_s s_sink_s s_den_s s_den2_s s_rden_s s_rdc_s s_gate_s
            x_ps x_mx_s x_d_s x_exp_s x_den_s x_rden_s x_rdc_s x_gate_s
            pTa_ps pTb_ps pTa_s pTb_s xTa_ps xTb_ps xTa_s xTb_s xT_hi_out
            kv_done state_s os_ps og_ps ox_ps o_ss_s o_ms_s o_rs_s o_rc_s mix_s mix_out
            wo_cols b_scale b_un b_hi b_lo bT_hi bT_lo bT_hi_s bT_lo_s
            y_ps0 y_ps1 y_res0 y_res1 y_ss y_ms y_rs y_fin y_out first_masked"""
        s = {n: sem(n) for n in sem_names.split()}
        assert len(s) == len(sem_names.split())
        w_raw_in = [sem(f"w_raw_in{r}") for r in range(4)]
        x_in_s = [sem("x_in_even"), sem("x_in_odd")]
        xr_in_s = [sem("xr_in_even"), sem("xr_in_odd")]
        m_in_s = [sem("m_in_even"), sem("m_in_odd")]
        wout_in = [sem(f"wout_in{part}") for part in range(3)]
        proj_ps = [sem(f"proj_ps{g}") for g in range(NG)]

        def split_through(eng, g):
            eng.wait_ge(s["w_lo_s"], KD * (g + 1))

        block = ctx.enter_context(nc.Block())

        def iterations(eng, body):
            body(Tile(0, 0), project=True, attend=False)
            body(Tile(0, 1), project=True, attend=True, first=True)
            with eng.Fori(1, TILES // 2 - 1) as m:
                body(Tile(m, 0), project=True, attend=True)
                body(Tile(m, 1), project=True, attend=True)
            body(Tile(TILES // 2 - 1, 0), project=True, attend=True)
            body(Tile(TILES // 2 - 1, 1), project=True, attend=True, last=True)
            body(Tile(TILES // 2, 0), project=False, attend=True, last=True)

        def out_iterations(eng, body):
            body(Tile(0, 0), 2)
            body(Tile(0, 1), 2)
            with eng.Fori(1, TILES // 2 - 1) as m:
                body(Tile(m, 0), 2)
                body(Tile(m, 1), 2)
            body(Tile(TILES // 2 - 1, 0), 1)
            body(Tile(TILES // 2 - 1, 1), 0)

        last_reader = {KVL: "kvl_out", SQ: "sq_out", GQK: "gqk_out", XQZ: "xq_out", GV: "gv_out", GZ: "gz_out",
                       SZ: "sz_out"}

        def proj_bank(t, g):
            return proj[(t.p + g) % 2]

        @block.sync
        def _(sp):
            def raw_load(g):
                sp.dma_start(raw_rooms[RAW[g][0]][:, 0:KD * GCOLS[g]], w_groups[g]).then_inc(w_raw_in[RAW[g][0]], 16)

            for dst, src in ((la_e[:, 0:TILES].bitcast(I32), pos), (gn, g_norm), (gm, g_mem), (gg, g_gla),
                             (wa2[0:GLA_LR, :], w_a2), (wa2[GLA_LR:GLA_LR + 1, :], b_a),
                             (sink_b[:], sinks.partition_broadcast(P))):
                sp.dma_start(dst, src).then_inc(s["small_in"], 16)
            sp.dma_start(x_in[:, 0, :], x[0:P, :]).then_inc(x_in_s[0], 16)
            raw_load(KVL)
            sp.dma_start(mem_in, mem.rearrange("(b p) d -> p b d", p=P)).then_inc(s["mem_in_s"], 16)
            raw_load(SQ)
            sp.dma_start(mem_w, w_mem).then_inc(s["memw_in"], 16)
            raw_load(GQK)
            sp.dma_start(x_in[:, 1, :], x[P:2 * P, :]).then_inc(x_in_s[1], 16)
            for g in (XQZ, GV):
                split_through(sp, g - 3)
                raw_load(g)
            sp.wait_ge(s["memv_ps"], MB)
            raw_load(GZ)
            split_through(sp, XQZ)
            raw_load(SZ)

            def body(n, project, attend, first=False, last=False):
                if project and not last:
                    nxt = n.moved(2)
                    row = sp.snap(nxt.index() * P) if not isinstance(n.m, int) else nxt.index() * P
                    if not (isinstance(n.m, int) and nxt.index() >= TILES):
                        wait(sp, s["x_hi_s"], n.done())
                        sp.wait_ge(s["x_lo_s"], n.done())
                        sp.dma_start(x_in[:, n.p, :], x[bass.ds(row, P), :]).then_inc(x_in_s[n.p], 16)
                if last and project:
                    for part, (g, k0, k1) in enumerate(WO_ROOMS):
                        sp.wait_ge(proj_ps[g], TILES)
                        sp.dma_start(wo_raw[:, k0:k1, :], w_out[:, k0:k1, :]).then_inc(wout_in[part], 16)
                    sp.wait_ge(s["mix_out"], 16 * 2)
                    sp.wait_ge(proj_ps[SZ], TILES)
                    sp.dma_start(m_in[0], mix_dram[0:P, :]).then_inc(m_in_s[0], 16)
                    sp.wait_ge(s["x_hi_s"], TILES)
                    sp.wait_ge(s["x_lo_s"], TILES)
                    sp.dma_start(x_in[:, 0, :], x[0:P, :]).then_inc(xr_in_s[0], 16)
                    sp.wait_ge(s["w_sum_s"], NG + KM // WO_SUM)
                    sp.dma_start(m_in[1], mix_dram[P:2 * P, :]).then_inc(m_in_s[1], 16)
                    sp.dma_start(x_in[:, 1, :], x[P:2 * P, :]).then_inc(xr_in_s[1], 16)
                if attend:
                    t = n.moved(-1)
                    row = sp.snap(t.index() * P) if not isinstance(n.m, int) else t.index() * P
                    sp.wait_ge(s["mix_s"], t.done(6))
                    sp.dma_start(mix_dram[bass.ds(row, P), :], mix).then_inc(s["mix_out"], 16)

            iterations(sp, body)

            sp.wait_ge(s["mix_out"], 16 * TILES)
            sp.dma_start(g_fin, g_final.partition_broadcast(P)).then_inc(s["gfin_in"], 16)

            def out_body(b, more):
                fixed = isinstance(b.m, int)
                nxt = b.moved(2)
                row = b.index() * P if fixed else sp.snap(b.index() * P)
                row2 = nxt.index() * P if fixed else sp.snap(nxt.index() * P)
                if not (fixed and nxt.index() >= TILES):
                    sp.wait_ge(s["b_hi"], b.done())
                    sp.wait_ge(s["b_lo"], b.done())
                    sp.dma_start(m_in[b.p], mix_dram[bass.ds(row2, P), :]).then_inc(m_in_s[b.p], 16)
                    sp.wait_ge(s["y_res0"], b.done())
                    sp.wait_ge(s["y_res1"], b.done())
                    sp.dma_start(x_in[:, b.p, :], x[bass.ds(row2, P), :]).then_inc(xr_in_s[b.p], 16)
                sp.wait_ge(s["y_fin"], b.done())
                sp.dma_start(out[bass.ds(row, P), :], y).then_inc(s["y_out"], 16)

            out_iterations(sp, out_body)
            sp.wait_ge(s["y_out"], 16 * TILES)

        @block.gpsimd
        def _(pool):
            g = nc.gpsimd
            g.memset(ident[:], 0.0).then_inc(s["misc_set"], 1)
            g.memset(later[:], 1.0 / GLA_TAU).then_inc(s["misc_set"], 1)
            g.memset(minus_half, -0.5).then_inc(s["misc_set"], 1)
            g.memset(tiny, 1e-20).then_inc(s["misc_set"], 1)
            g.memset(lrT[:], 1.0).then_inc(s["misc_set"], 1)
            g.memset(halves[:], 0.0).then_inc(s["misc_set"], 1)
            g.memset(kT_first[:], 0.0).then_inc(s["misc_set"], 1)
            g.memset(v_win[:], 0.0).then_inc(s["misc_set"], 1)
            g.memset(state[:], 0.0).then_inc(s["misc_set"], 1)
            pool.wait_ge(s["misc_set"], 9)
            g.memset(halves[0:CHUNK, 0:1], 1.0 / GLA_TAU).then_inc(s["pads_set"], 1)
            g.memset(halves[CHUNK:P, 1:2], 1.0 / GLA_TAU).then_inc(s["pads_set"], 1)
            pool.wait_ge(s["pads_set"], 2)
            g.affine_select(out=ident[:], in_=ident[:], compare_op=ALU.not_equal, fill=1.0, base=0,
                            pattern=[[-1, P]], channel_multiplier=1).then_inc(s["id_set"], 1)
            g.affine_select(out=later[:], in_=later[:], compare_op=ALU.is_gt, fill=0.0, base=0,
                            pattern=[[-1, P]], channel_multiplier=1).then_inc(s["pads_set"], 1)
            pool.wait_ge(s["pads_set"], 3)
            g.memset(later[CHUNK:P, 0:CHUNK], 0.0).then_inc(s["pads_set"], 1)
            pool.wait_ge(s["pads_set"], 4)
            pool.wait_ge(s["id_set"], 1)
            g.tensor_copy(ident16[:], ident[:]).then_inc(s["id_set"], 1)
            g.tensor_copy(later16[:], later[:]).then_inc(s["id_set"], 1)

            def memory_pow(b):
                pool.wait_ge(s["mem_ms"], b + 1)
                g.tensor_tensor(m_rec[:, :] if b else m_pow[:, :], m_scale[:, :] if b else m_amax[:, :],
                                minus_half[:, 0:1], ALU.pow).then_inc(s["mem_rs"], 1)

            def row_pow(t):
                pool.wait_ge(s["x_ms_s"], t.done())
                wait(pool, s["x_hi_s"], t.done(lag=1))
                wait(pool, s["x_lo_s"], t.done(lag=1))
                g.tensor_tensor(x_rs, x_ms, minus_half[:, 0:1], ALU.pow).then_inc(s["x_rs_s"], 1)

            def all_bound(k):
                pool.wait_ge(s["w_sum_s"], k + 1)
                pool.wait_ge(s["g_top_s"], 1)
                b = w_bound[:, k:k + 1]
                g.tensor_tensor(b, w_sum[:, k:k + 1], g_top, ALU.mult).then_inc(s["w_bound_s"], 1)
                pool.wait_ge(s["w_bound_s"], 2 * k + 1)
                g.tensor_tensor(b, b, tiny, ALU.add).then_inc(s["w_bound_s"], 1)
                pool.wait_ge(s["w_bound_s"], 2 * k + 2)
                g.partition_all_reduce(w_all[:, k:k + 1], b, P, bass.bass_isa.ReduceOp.max).then_inc(s["wall_s"], 1)

            def all_max(k):
                pool.wait_ge(s["wmax1"], k + 1)
                g.partition_all_reduce(w_all[:, NG + k:NG + k + 1], w_max1, P, bass.bass_isa.ReduceOp.max)\
                    .then_inc(s["wall_s"], 1)

            row_pow(Tile(0, 0))
            all_bound(0)
            for b in range(MB):
                memory_pow(b)

            def body(n, project, attend, first=False, last=False):
                t = n.moved(-1)
                tp = t.p
                if not attend:
                    for k in range(1, GZ + 1):
                        all_bound(k)
                if project:
                    heads = qkv[:, n.p, 0:SWA_W + SWA_KVW].rearrange("p (h d) -> p h d", d=HD)
                    x1, x2 = heads[:, :, 0:ROPE_HALF], heads[:, :, ROPE_HALF:2 * ROPE_HALF]
                    shape = [P, SWA_H + SWA_KV, ROPE_HALF]
                    c = cs[:, 0:1, :].to_broadcast(shape)
                    sn = cs[:, 1:2, :].to_broadcast(shape)
                    pool.wait_ge(s["cs_s"], n.done())
                    pool.wait_ge(s["kvl_out"], n.done())
                    pool.wait_ge(s["sq_out"], n.done())
                    for i, (a, b) in enumerate(((x1, c), (x2, sn), (x2, c), (x1, sn))):
                        g.tensor_tensor(rope_t[:, i], a, b, ALU.mult).then_inc(s["rope_t_s"], 1)
                    pool.wait_ge(s["rope_t_s"], n.done(4))
                    g.tensor_tensor(x1, rope_t[:, 0], rope_t[:, 1], ALU.subtract).then_inc(s["rope_s"], 1)
                    g.tensor_tensor(x2, rope_t[:, 2], rope_t[:, 3], ALU.add).then_inc(s["rope_s"], 1)
                    if not (last and project):
                        row_pow(n.moved(1))
                if not attend:
                    all_bound(SZ)
                    all_max(0)
                    all_max(1)
                if attend:
                    pool.wait_ge(s["s_rden_s"], t.done())
                    g.tensor_tensor(s_den, s_rden, unscale_half[:, SZ:SZ + 1].to_broadcast([P, SWA_H]), ALU.mult)\
                        .then_inc(s["s_rdc_s"], 1)
                    sg = gates[:, tp, GLA_W:GLA_W + SWA_W].rearrange("p (i b d) -> p b i d", b=2, d=HD)
                    by_head = s_den.rearrange("p (b i) -> p b i", b=2).unsqueeze(3)
                    pool.wait_ge(s["s_rdc_s"], t.done())
                    g.tensor_tensor(sg, sg, by_head.to_broadcast([P, 2, SWA_H // 2, HD]), ALU.mult)\
                        .then_inc(s["s_gate_s"], 1)
                    pool.wait_ge(s["x_rden_s"], t.done())
                    g.tensor_tensor(c_den, c_rden, xa_unscale.to_broadcast([P, XA_H]), ALU.mult)\
                        .then_inc(s["x_rdc_s"], 1)
                    xg = gates[:, tp, GLA_W + SWA_W:D_MIX].rearrange("p (j b d) -> p b j d", b=2, d=HD)
                    by_head = c_den.rearrange("p (b j) -> p b j", b=2).unsqueeze(3)
                    pool.wait_ge(s["x_rdc_s"], t.done())
                    g.tensor_tensor(xg, xg, by_head.to_broadcast([P, 2, XA_H // 2, HD]), ALU.mult)\
                        .then_inc(s["x_gate_s"], 1)
                    if last and project:
                        all_max(2)
                    pool.wait_ge(s["o_ms_s"], t.done())
                    g.tensor_tensor(o_rs, o_ms, minus_half, ALU.pow).then_inc(s["o_rs_s"], 1)
                    pool.wait_ge(s["o_rs_s"], t.done())
                    g.tensor_tensor(o_rc, o_rs, unscale_half[:, GZ:GZ + 1].to_broadcast([P, GLA_H]), ALU.mult)\
                        .then_inc(s["o_rc_s"], 1)

            iterations(pool, body)
            def out_body(b, more):
                pool.wait_ge(s["y_ms"], b.done())
                g.tensor_tensor(x_rs, x_ms, minus_half[:, 0:1], ALU.pow).then_inc(s["y_rs"], 1)

            out_iterations(pool, out_body)

        @block.scalar
        def _(act):
            a = nc.scalar
            def x_square(t):
                act.wait_ge(x_in_s[t.p], t.done_alike())
                wait(act, s["x_ms_s"], t.done(lag=1))
                wait(act, s["xT_hi_ps"], t.done(lag=1))
                a.activation(x_hi[:], x_in[:, t.p, :], ACT.Square, accum_out=x_ss).then_inc(s["x_ss_s"], 1)

            def x_high(t):
                act.wait_ge(s["x_rs_s"], t.done())
                act.wait_ge(s["x_ss_s"], t.done())
                a.activation(x_hi[:], x_in[:, t.p, :], ACT.Copy, scale=x_rs).then_inc(s["x_hi_s"], 1)

            def hT_high(t):
                act.wait_ge(s["xT_hi_ps"], t.done())
                wait(act, proj_ps[SZ], t.done(lag=2))
                a.activation(hT_hi[:, t.p, :], turn[0][:].bitcast(F16), ACT.Copy).then_inc(s["hT_hi_s"], 1)

            def memory_keys():
                for j in range(2):
                    act.wait_ge(s["memk_ps"], j + 1)
                    a.activation(memT_k[:, j, :], score[j][:, 0:MEM], ACT.Copy).then_inc(s["memk_out"], 1)

            def memory_values():
                for b in range(MB):
                    act.wait_ge(s["memv_ps"], b + 1)
                    a.activation(mem_v[:, b, :], score[b][:, 256:256 + XA_W], ACT.Copy).then_inc(s["memv_out"], 1)

            def magnitudes(g):
                wait_raw(act, g)
                if g < GV:
                    junk = W[:, GOFF[g]:GOFF[g] + KD * GCOLS[g]]
                elif g < SZ:
                    junk = W[:, GOFF[GZ]:GOFF[GZ] + KD * GCOLS[GZ]]
                    act.wait_ge(s["memv_ps"], MB)
                    act.wait_ge(s["w_sum_s"], g)
                else:
                    junk = raw_rooms[1]
                    split_through(act, GV)
                a.activation(junk[:, 0:KD * GCOLS[g]], raw_rooms[RAW[g][0]][:, 0:KD * GCOLS[g]], ACT.Abs,
                             accum_out=w_sum[:, g:g + 1]).then_inc(s["w_sum_s"], 1)

            def split_high(g):
                if XQZ <= g < GZ:
                    magnitudes(g + 1)
                act.wait_ge(s["wscale2_s"], g + 1)
                if g == SZ:
                    split_through(act, GZ)
                for k in range(HIGH_A):
                    a.activation(w_hi(g)[:, k, :], raw(g)[:, k, :], ACT.Copy, scale=block_scale(g, k))\
                        .then_inc(s["w_hi_s"], 1)
                if g == KVL:
                    hT_high(Tile(0, 0))
                if g < XQZ or g == GZ:
                    magnitudes(g + 1)

            x_square(Tile(0, 0))
            magnitudes(KVL)
            act.wait_ge(s["mem_in_s"], 16)
            for b in range(MB):
                a.activation((hT_hi, hT_lo)[b][:, 1, :], mem_in[:, b, :], ACT.Square,
                             accum_out=(s_mx if b == 0 else s_m)[:, 0:1]).then_inc(s["mem_sq"], 1)
            x_high(Tile(0, 0))

            def project_out(g, n):
                if g in (SQ,):
                    return
                act.wait_ge(proj_ps[g], n.done())
                ps = proj_bank(n, g)
                if g == KVL:
                    a.activation(qkv[:, n.p, SWA_W:], ps[:, 0:GCOLS[g]], ACT.Copy, scale=unscale[:, g:g + 1])\
                        .then_inc(s["kvl_out"], 1)
                elif g == GQK:
                    a.activation(gqk[:, n.p, :], ps[:], ACT.Copy, scale=unscale[:, g:g + 1])\
                        .then_inc(s["gqk_out"], 1)
                elif g == GV:
                    a.activation(gv[:], ps[:], ACT.Copy, scale=unscale[:, g:g + 1]).then_inc(s["gv_out"], 1)
                else:
                    cols = slice(XA_W, 2 * XA_W) if g == XQZ else slice(0, 512)
                    width = cols.stop - cols.start
                    before = {XQZ: ("sz_out", 1), GZ: ("xz_out", 0), SZ: ("gz_out", 0)}[g]
                    wait(act, s[before[0]], n.done(lag=before[1]))
                    if g == XQZ:
                        wait(act, s["o_ss_s"], n.done(4, lag=2))
                    a.activation(tanh_z[:, 0:width], ps[:, cols], ACT.Tanh, scale=unscale_half[:, g:g + 1])\
                        .then_inc(s["tanh_s"], 1)

            def out_sums(i):
                act.wait_ge(wout_in[i * WO_SUM // 4], 16)
                if i:
                    act.wait_ge(s["w_sum_s"], NG + i)
                a.activation(wo_junk, wo_raw[:, i * WO_SUM:(i + 1) * WO_SUM, :], ACT.Abs,
                             scale=gg if i * WO_SUM < GLA_H else 1.0, accum_out=w_max[:, i:i + 1])\
                    .then_inc(s["w_sum_s"], 1)

            def out_high(k0, k1):
                act.wait_ge(s["wo_cols"], 2)
                act.wait_ge(proj_ps[(GV, GZ, SZ)[k0 // 4]], TILES)
                for k in range(k0, k1):
                    a.activation(wo_hi[:, k, :], wo_raw[:, k, :], ACT.Copy, scale=w_scale[:, k:k + 1])\
                        .then_inc(s["w_hi_s"], 1)

            def mix_high(b):
                act.wait_ge(s["b_scale"], b.done())
                act.wait_ge(m_in_s[b.p], b.done_alike())
                wait(act, s["bT_hi"], b.done(lag=1))
                a.activation(m_hi, m_in[b.p], ACT.Copy, scale=m_scale).then_inc(s["b_hi"], 1)

            def mixT_high(b):
                act.wait_ge(s["bT_hi"], b.done())
                wait(act, s["y_ps1"], b.done(lag=2))
                a.activation(mT_hi[b.p][:, 0:D], turn[0][:].bitcast(F16), ACT.Copy).then_inc(s["bT_hi_s"], 1)
                a.activation(mT_hi[b.p][:, D:D_MIX], turn[1][:].bitcast(F16)[:, 0:D_MIX - D], ACT.Copy)\
                    .then_inc(s["bT_hi_s"], 1)

            def body(n, project, attend, first=False, last=False):
                t = n.moved(-1)
                lagged = project and not attend
                if lagged:
                    for g in range(NG):
                        split_high(g)
                        if g == KVL:
                            act.wait_ge(s["ang_done"], 1)
                            a.activation(cos_sin[:, :, 1, :], cos_sin[:, :, 1, :], ACT.Sin)
                            a.activation(cos_sin[:, :, 0, :], cos_sin[:, :, 0, :], ACT.Sin).then_inc(s["cos_done"], 1)
                        if g == SQ:
                            memory_keys()
                        if g == GQK:
                            x_square(n.moved(1))
                        if g == XQZ:
                            memory_values()
                        if g >= 2:
                            project_out(g - 2, n)
                            if g - 2 == GQK:
                                x_high(n.moved(1))
                    hT_high(n.moved(1))
                    project_out(NG - 2, n)
                    project_out(NG - 1, n)
                    return
                more = project and not (last and project)
                ending, ended = last and project, last and not project
                if project:
                    project_out(KVL, n)
                act.wait_ge(s["qT_ps"], t.done())
                wait(act, s["s_ps"], t.done(lag=1))
                if first:
                    split_through(act, NG - 1)
                a.activation(qT, turn[1][:], ACT.Copy).then_inc(s["qT_s"], 1)
                if ended:
                    out_high(2, 4)
                    out_high(4, 7)
                if more:
                    x_square(n.moved(1))
                if ended:
                    out_high(7, 8)
                act.wait_ge(s["lr_ps"], t.done())
                wait(act, s["la_s"], t.done(3, lag=1))
                a.activation(la_e[:], decay_ps[:, 0:GLA_KW], ACT.Abs).then_inc(s["la_abs"], 1)
                act.wait_ge(s["la_abs"], t.done())
                a.activation(la_e[:], la_e[:], ACT.Exp, scale=-1.0).then_inc(s["la_exp"], 1)
                act.wait_ge(s["la_exp"], t.done())
                a.activation(la_e[:], la_e[:], ACT.Ln, bias=1.0).then_inc(s["la_ln"], 1)
                if ended:
                    out_high(8, KM)
                if project:
                    project_out(GQK, n)
                if more:
                    x_high(n.moved(1))
                act.wait_ge(s["s_d_s"], t.done(2))
                a.activation(probs, probs, ACT.Exp).then_inc(s["s_exp_s"], 1)
                act.wait_ge(s["s_diff_s"], t.done())
                a.activation(s_sink, s_diff, ACT.Exp).then_inc(s["s_sink_s"], 1)
                if project:
                    project_out(XQZ, n)
                act.wait_ge(s["decay_cum"], t.done())
                wait(act, s["k_dec_s"], t.done(lag=1))
                a.activation(decay[:], decay_ps[:, 0:GLA_KW], ACT.Exp).then_inc(s["decay_s"], 1)
                wait(act, s["state_s"], t.done(4, lag=1))
                a.activation(g_end, kv_ps[:, GLA_KW:GLA_KW + 4], ACT.Exp).then_inc(s["g_end_s"], 1)
                if ended:
                    mix_high(Tile(0, 0))
                if ending:
                    out_sums(0)
                    out_sums(1)
                if more:
                    hT_high(n.moved(1))
                act.wait_ge(s["x_d_s"], t.done(2))
                a.activation(xprobs, xprobs, ACT.Exp, scale=x_factor).then_inc(s["x_exp_s"], 1)
                if project:
                    act.wait_ge(s["kv_done"], t.done())
                    project_out(GV, n)
                if ending:
                    out_sums(2)
                    out_sums(3)
                act.wait_ge(s["pTa_ps"], t.done())
                wait(act, s["os_ps"], t.done(lag=1))
                a.activation(probsT[:, 0:4, :], turn[0][:], ACT.Copy).then_inc(s["pTa_s"], 1)
                if project:
                    project_out(GZ, n)
                if ending:
                    out_sums(4)
                wait(act, s["ox_ps"], t.done(lag=1))
                for half in range(2):
                    act.wait_ge(s[("xTa_ps", "xTb_ps")[half]], t.done())
                    a.activation(xprobsT_hi[:, 4 * half:4 * half + 4, :], turn[half][:], ACT.Copy, scale=PROB_UP)\
                        .then_inc(s["xT_hi_out"], 1)
                if ending:
                    out_high(0, 2)
                if project:
                    project_out(SZ, n)
                act.wait_ge(s["og_ps"], t.done())
                wait(act, s["o_ms_s"], t.done(lag=1))
                act.wait_ge(s["sz_out"], n.done() if project else TILES)
                for h in range(GLA_H):
                    a.activation(tanh_z[:, h * GLA_DV:(h + 1) * GLA_DV], gla_out(h), ACT.Square,
                                 accum_out=o_ss[:, h:h + 1]).then_inc(s["o_ss_s"], 1)

            iterations(act, body)

            mixT_high(Tile(0, 0))
            mix_high(Tile(0, 1))

            def out_body(b, more):
                if more:
                    mixT_high(b.moved(1))
                if more == 2:
                    mix_high(b.moved(2))
                act.wait_ge(s["y_res0"], b.done())
                act.wait_ge(s["y_res1"], b.done())
                a.activation(gates[:, 0, 0:D], y, ACT.Square, accum_out=x_ss).then_inc(s["y_ss"], 1)

            out_iterations(act, out_body)

        @block.vector
        def _(dve):
            v = nc.vector

            def x_mean(t):
                dve.wait_ge(s["x_ss_s"], t.done())
                wait(dve, s["x_rs_s"], t.done(lag=1))
                v.tensor_scalar(x_ms, x_ss, 1.0 / D / X_UP ** 2, EPS / X_UP ** 2, ALU.mult, ALU.add)\
                    .then_inc(s["x_ms_s"], 1)

            dve.wait_ge(s["small_in"], 16 * 7)
            steps = [0]

            def step(ins):
                steps[0] += 1
                ins.then_inc(s["set_up_steps"], 1)
                dve.wait_ge(s["set_up_steps"], steps[0])

            posf = la[:, 0:TILES]
            ang = cos_sin[:, :, 1, :]
            turns_f = gates[:, 0, 0:TILES * ROPE_HALF].rearrange("p (t j) -> p t j", j=ROPE_HALF)
            turns_i = gates[:, 1, 0:TILES * ROPE_HALF].bitcast(I32).rearrange("p (t j) -> p t j", j=ROPE_HALF)
            step(v.tensor_copy(posf, la_e[:, 0:TILES].bitcast(I32)))
            inv = np.float32(1.0) / np.power(np.float32(ROPE_THETA),
                                             np.arange(ROPE_HALF, dtype=np.float32) / np.float32(ROPE_HALF))
            for j in range(ROPE_HALF):
                step(v.tensor_scalar(ang[:, :, j:j + 1], posf.unsqueeze(2), float(inv[j]), None, ALU.mult))
            step(v.tensor_reduce(w_max1, gn, AX, ALU.max, apply_absolute_value=True))
            v.tensor_copy(g_top, w_max1).then_inc(s["g_top_s"], 1)
            for scale, bits, count in ((4096.0, 7, 6), (1.0, 11, 4)):
                step(v.tensor_scalar(turns_i, ang, float(1.0 / (2.0 * np.pi * scale)), None, ALU.mult))
                step(v.tensor_copy(turns_f, turns_i))
                for part in two_pi_parts(scale, bits, count):
                    step(v.scalar_tensor_tensor(out=ang, in0=turns_f, scalar=-part, in1=ang, op0=ALU.mult,
                                                op1=ALU.add))
                if scale > 1.0:
                    x_mean(Tile(0, 0))
            step(v.tensor_scalar(ang, ang, float(np.float32(3.1415925)), float(np.float32(-3.1415925)),
                                 ALU.min, ALU.max))
            step(v.tensor_scalar(turns_f, ang, -1.0, None, ALU.mult))
            v.tensor_tensor(cos_sin[:, :, 0, :], turns_f, ang, ALU.max).then_inc(s["ang_abs"], 1)
            dve.wait_ge(s["ang_abs"], 1)
            v.tensor_scalar(cos_sin[:, :, 0, :], cos_sin[:, :, 0, :], -1.0, float(np.pi / 2), ALU.mult, ALU.add)\
                .then_inc(s["ang_abs"], 1)
            dve.wait_ge(s["ang_abs"], 2)
            v.tensor_copy(turns_f, ang).then_inc(s["ang_done"], 1)

            def x_low(t):
                dve.wait_ge(s["x_rs_s"], t.done())
                dve.wait_ge(s["x_hi_s"], t.done())
                wait(dve, s["xT_lo_ps"], t.done(lag=1))
                v.scalar_tensor_tensor(out=x_lo[:], in0=x_in[:, t.p, :], scalar=x_rs, in1=x_hi[:], op0=ALU.mult,
                                       op1=ALU.subtract).then_inc(s["x_lo_s"], 1)

            def hT_low(t):
                dve.wait_ge(s["xT_lo_ps"], t.done())
                wait(dve, proj_ps[SZ], t.done(lag=2))
                v.tensor_copy(hT_lo[:, t.p, :], turn[1][:].bitcast(F16)).then_inc(s["hT_lo_s"], 1)

            def power_scale(k):
                dve.wait_ge(s["wall_s"], k + 1)
                step(v.tensor_scalar(w_pow.bitcast(I32), w_all[:, k:k + 1].bitcast(I32), EXPONENT, None,
                                     ALU.bitwise_and))
                step(v.reciprocal(w_rec, w_pow))

            def group_scale(g):
                power_scale(g)
                v.tensor_scalar(w_scale[:, (g % 2) * KD:(g % 2 + 1) * KD], gn, w_rec, W_UP, ALU.mult, ALU.mult)\
                    .then_inc(s["wscale2_s"], 1)
                v.tensor_scalar(unscale[:, g:g + 1], w_pow, 1.0 / W_UP / X_UP, None, ALU.mult)\
                    .then_inc(s["unscale_s"], 1)
                v.tensor_scalar(unscale_half[:, g:g + 1], w_pow, 0.5 / W_UP / X_UP, None, ALU.mult)\
                    .then_inc(s["unscale_s"], 1)

            def split_low(g):
                dve.wait_ge(s["wscale2_s"], g + 1)
                dve.wait_ge(s["unscale_s"], 2 * (g + 1))
                wait_raw(dve, g)
                for k in range(HIGH_A, KD):
                    v.tensor_scalar(w_hi(g)[:, k, :], raw(g)[:, k, :], block_scale(g, k), None, ALU.mult)\
                        .then_inc(s["w_hi2_s"], 1)
                for k in range(KD):
                    if k < HIGH_A:
                        dve.wait_ge(s["w_hi_s"], HIGH_A * g + k + 1)
                    else:
                        dve.wait_ge(s["w_hi2_s"], (KD - HIGH_A) * g + k + 1 - HIGH_A)
                    v.scalar_tensor_tensor(out=w_lo(g)[:, k, :], in0=raw(g)[:, k, :], scalar=block_scale(g, k),
                                           in1=w_hi(g)[:, k, :], op0=ALU.mult, op1=ALU.subtract)\
                        .then_inc(s["w_lo_s"], 1)
                    if g + 1 < NG and k == (5 if XQZ <= g < GZ else KD - 1):
                        group_scale(g + 1)

            def memory_rows():
                for b in range(MB):
                    dve.wait_ge(s["mem_rs"], b + 1)
                    v.tensor_scalar(mem_in[:, b, :], mem_in[:, b, :], m_rec if b else m_pow, None, ALU.mult)\
                        .then_inc(s["mem_scaled"], 1)

            def split_memory():
                dve.wait_ge(s["wall_s"], NG + 1)
                v.tensor_reduce(w_max1, memT_k[:].rearrange("p b c -> p (b c)"), AX, ALU.max,
                                apply_absolute_value=True).then_inc(s["wmax1"], 1)
                step(v.tensor_scalar(w_all[:, NG:NG + 1], w_all[:, NG:NG + 1], 1e-20, None, ALU.max))
                power_scale(NG)
                step(v.tensor_scalar(v_scale, w_rec, V_UP, None, ALU.mult))
                step(v.tensor_scalar(v_unscale, w_pow, 1.0 / V_UP / PROB_UP, None, ALU.mult))
                step(v.tensor_scalar(xa_unscale, unscale_half[:, XQZ:XQZ + 1], v_unscale, None, ALU.mult))
                v.tensor_scalar(mem_v_hi[:], mem_v[:], v_scale, None, ALU.mult).then_inc(s["v_split_s"], 1)
                dve.wait_ge(s["v_split_s"], 1)
                v.scalar_tensor_tensor(out=mem_v_lo[:], in0=mem_v[:], scalar=v_scale, in1=mem_v_hi[:], op0=ALU.mult,
                                       op1=ALU.subtract).then_inc(s["v_split_s"], 1)
                dve.wait_ge(s["wall_s"], NG + 2)
                step(v.tensor_scalar(w_all[:, NG + 1:NG + 2], w_all[:, NG + 1:NG + 2], 1e-20, None, ALU.max))
                power_scale(NG + 1)
                step(v.tensor_scalar(k_scale, w_rec, K_UP, None, ALU.mult))
                step(v.tensor_scalar(xq_unscale, w_pow, unscale[:, XQZ:XQZ + 1], SCALE / K_UP, ALU.mult, ALU.mult))
                v.tensor_scalar(memT_k_hi[:], memT_k[:], k_scale, None, ALU.mult).then_inc(s["v_split_s"], 1)
                dve.wait_ge(s["v_split_s"], 3)
                v.scalar_tensor_tensor(out=memT_k_lo[:], in0=memT_k[:], scalar=k_scale, in1=memT_k_hi[:],
                                       op0=ALU.mult, op1=ALU.subtract).then_inc(s["v_split_s"], 1)

            def memory_turned():
                for k in range(KD):
                    dve.wait_ge(s["mem_T"], k // 2 + 1)
                    v.tensor_scalar(memT[:, k, :], mem_banks[k // 2][:, (k % 2) * MEM:(k % 2 + 1) * MEM],
                                    gm[:, k:k + 1], None, ALU.mult).then_inc(s["mem_T_out"], 1)

            group_scale(KVL)
            for b in range(MB):
                dve.wait_ge(s["mem_sq"], b + 1)
                v.tensor_scalar(m_scale if b else m_amax, (s_mx if b == 0 else s_m)[:, 0:1], 1.0 / D, EPS,
                                ALU.mult, ALU.add).then_inc(s["mem_ms"], 1)
            x_low(Tile(0, 0))
            hT_low(Tile(0, 0))
            memory_rows()

            def project_out(g, n):
                ps = proj_bank(n, g)
                if g == SQ:
                    dve.wait_ge(proj_ps[g], n.done())
                    v.tensor_scalar(qkv[:, n.p, 0:SWA_W], ps[:], unscale[:, g:g + 1], None, ALU.mult)\
                        .then_inc(s["sq_out"], 1)
                elif g in (XQZ, GZ, SZ):
                    dve.wait_ge(s["tanh_s"], n.done(3) - {XQZ: 2, GZ: 1, SZ: 0}[g])
                    cols, at, name = {XQZ: (slice(XA_W, 2 * XA_W), GLA_W + SWA_W, "xz_out"),
                                      GZ: (slice(0, 512), 0, "gz_out"), SZ: (slice(0, 512), GLA_W, "sz_out")}[g]
                    width = cols.stop - cols.start
                    v.scalar_tensor_tensor(out=gates[:, n.p, at:at + width], in0=tanh_z[:, 0:width], scalar=1.0,
                                           in1=ps[:, cols], op0=ALU.add, op1=ALU.mult).then_inc(s[name], 1)
                    if g == XQZ:
                        wait(dve, s["gqT_ps"], n.done(lag=1))
                        at = [n.done(XQ_STEPS) - XQ_STEPS]

                        def xq_step(ins):
                            ins.then_inc(s["xq_out"], 1)
                            at[0] = at[0] + 1

                        un = xq_un[:, n.p:n.p + 1]
                        xq_step(v.tensor_reduce(un, ps[:, 0:XA_W], AX, ALU.max, apply_absolute_value=True))
                        dve.wait_ge(s["xq_out"], at[0])
                        xq_step(v.tensor_scalar(un, un, 1e-20, 1.0 / XQ_UP, ALU.add, ALU.mult))
                        dve.wait_ge(s["xq_out"], at[0])
                        xq_step(v.reciprocal(xq_re, un))
                        dve.wait_ge(s["xq_out"], at[0])
                        xq_step(v.tensor_scalar(xq[:, 0, :], ps[:, 0:XA_W], xq_re, None, ALU.mult))
                        dve.wait_ge(s["xq_out"], at[0])
                        xq_step(v.scalar_tensor_tensor(out=xq[:, 1, :], in0=ps[:, 0:XA_W], scalar=xq_re,
                                                       in1=xq[:, 0, :], op0=ALU.mult, op1=ALU.subtract))

            def tile_cos_sin(n):
                wait(dve, s["rope_t_s"], n.done(4, lag=1))
                v.tensor_scalar(cs[:], cos_sin[:, bass.ds(n.index(), 1)], 1.0, None, ALU.mult)\
                    .then_inc(s["cs_s"], 1)

            def double_keys(n):
                dve.wait_ge(s["rope_s"], n.done(2))
                wait(dve, s["kT_ps"], n.done(lag=1))
                k = qkv[:, n.p, SWA_W:SWA_W + SWA_KVW].rearrange("p (h d) -> p h d", d=HD)
                v.tensor_copy(k_twice[:], k.unsqueeze(2).to_broadcast([P, SWA_KV, 2, HD])).then_inc(s["k_twice_s"], 1)

            def pad_values(n):
                wait(dve, s["os_ps"], n.done(lag=1))
                dve.wait_ge(s["kvl_out"], n.done())
                dve.wait_ge(s["misc_set"], 9)
                val = qkv[:, n.p, SWA_W + SWA_KVW:SWA_W + 2 * SWA_KVW]
                v.tensor_copy(v_win[0:CHUNK, n.p, :], val[0:CHUNK]).then_inc(s["v_win_s"], 1)
                v.tensor_copy(v_win[CHUNK:P, 1 - n.p, :], val[CHUNK:P]).then_inc(s["v_win_s"], 1)

            def out_scale():
                dve.wait_ge(s["w_sum_s"], NG + KM // WO_SUM)
                step(v.tensor_reduce(w_max1, w_max[:, 0:KM // WO_SUM], AX, ALU.add))
                v.tensor_scalar(w_max1, w_max1, 1e-20, None, ALU.add).then_inc(s["wmax1"], 1)
                power_scale(NG + 2)
                v.tensor_scalar(w_scale[:, 0:KM], minus_half[:, 0:1].to_broadcast([P, KM]), w_rec, -2.0 * W_UP,
                                ALU.mult, ALU.mult).then_inc(s["wo_cols"], 1)
                dve.wait_ge(s["wo_cols"], 1)
                v.tensor_scalar(w_scale[:, 0:GLA_H], w_scale[:, 0:GLA_H], gg, None, ALU.mult)\
                    .then_inc(s["wo_cols"], 1)
                step(v.tensor_scalar(w_out_un, w_pow, 1.0 / W_UP / M_UP, None, ALU.mult))
                dve.wait_ge(s["wo_cols"], 2)

            def out_low(k0, k1):
                for k in range(k0, k1):
                    dve.wait_ge(s["w_hi_s"], HIGH_A * NG + k + 1)
                    v.scalar_tensor_tensor(out=wo_lo[:, k, :], in0=wo_raw[:, k, :], scalar=w_scale[:, k:k + 1],
                                           in1=wo_hi[:, k, :], op0=ALU.mult, op1=ALU.subtract).then_inc(s["w_lo_s"], 1)

            def mix_scale(b):
                dve.wait_ge(m_in_s[b.p], b.done_alike())
                wait(dve, s["b_hi"], b.done(lag=1))
                wait(dve, s["b_lo"], b.done(lag=1))
                v.tensor_reduce(m_amax, m_in[b.p], AX, ALU.max, apply_absolute_value=True).then_inc(s["b_chain"], 1)
                dve.wait_ge(s["b_chain"], b.done(4) - 3)
                v.tensor_scalar(m_amax, m_amax, 1e-20, None, ALU.max).then_inc(s["b_chain"], 1)
                dve.wait_ge(s["b_chain"], b.done(4) - 2)
                v.tensor_scalar(m_pow.bitcast(I32), m_amax.bitcast(I32), EXPONENT, None, ALU.bitwise_and)\
                    .then_inc(s["b_chain"], 1)
                dve.wait_ge(s["b_chain"], b.done(4) - 1)
                v.reciprocal(m_rec, m_pow).then_inc(s["b_chain"], 1)
                dve.wait_ge(s["b_chain"], b.done(4))
                v.tensor_scalar(m_scale, m_rec, M_UP, None, ALU.mult).then_inc(s["b_scale"], 1)
                wait(dve, s["b_un_now"], b.done(lag=2))
                v.tensor_scalar(m_un[:, b.p:b.p + 1], m_pow, w_out_un, None, ALU.mult).then_inc(s["b_un"], 1)

            def mix_low(b):
                dve.wait_ge(s["b_hi"], b.done())
                wait(dve, s["bT_lo"], b.done(lag=1))
                v.scalar_tensor_tensor(out=m_lo, in0=m_in[b.p], scalar=m_scale, in1=m_hi, op0=ALU.mult,
                                       op1=ALU.subtract).then_inc(s["b_lo"], 1)

            def mixT_low(b):
                dve.wait_ge(s["bT_lo"], b.done())
                wait(dve, s["y_ps1"], b.done(lag=2))
                banks = low_banks(b)
                v.tensor_copy(mT_lo[b.p][:, 0:D], banks[0][:].bitcast(F16)).then_inc(s["bT_lo_s"], 1)
                v.tensor_copy(mT_lo[b.p][:, D:D_MIX], banks[1][:].bitcast(F16)[:, 0:D_MIX - D])\
                    .then_inc(s["bT_lo_s"], 1)

            def body(n, project, attend, first=False, last=False):
                t = n.moved(-1)
                tp = t.p
                if not attend:
                    for g in range(NG):
                        split_low(g)
                        if g == KVL:
                            memory_turned()
                        if g == SQ:
                            dve.wait_ge(s["cos_done"], 1)
                            tile_cos_sin(n)
                        if g == GQK:
                            x_mean(n.moved(1))
                        if g == GZ:
                            dve.wait_ge(s["memv_out"], MB)
                            v.tensor_reduce(w_max1, mem_v[:].rearrange("p b c -> p (b c)"), AX, ALU.max,
                                            apply_absolute_value=True).then_inc(s["wmax1"], 1)
                        if g == SZ:
                            split_memory()
                        if g >= 2:
                            project_out(g - 2, n)
                            if g - 2 == GQK:
                                double_keys(n)
                                x_low(n.moved(1))
                    hT_low(n.moved(1))
                    project_out(NG - 2, n)
                    project_out(NG - 1, n)
                    pad_values(n)
                    return
                more = project and not (last and project)
                ending, ended = last and project, last and not project
                if project:
                    tile_cos_sin(n)
                dve.wait_ge(s["kT_ps"], t.done())
                wait(dve, s["s_ps"], t.done(lag=1))
                new_keys = turn[0][:, 0:2 * P].rearrange("p (h t) -> p h t", h=SWA_KV)
                dve.wait_ge(s["misc_set"], 9)
                v.tensor_copy(kT[:], new_keys).then_inc(s["kT_s"], 1)
                v.tensor_copy(kT_first[:, tp, :, 0:CHUNK], new_keys[:, :, 0:CHUNK]).then_inc(s["kT_s"], 1)
                v.tensor_copy(kT_first[:, 1 - tp, :, CHUNK:P], new_keys[:, :, CHUNK:P]).then_inc(s["kT_s"], 1)
                wait(dve, s["lr_ps"], t.done(lag=1))
                v.tensor_copy(lrT[0:GLA_LR, :], turn[0][0:GLA_LR, 2 * P:3 * P]).then_inc(s["lrT_s"], 1)
                if ended:
                    out_low(2, 4)
                    mix_scale(Tile(0, 0))
                if project:
                    project_out(SQ, n)
                dve.wait_ge(s["gqT_ps"], t.done())
                wait(dve, s["og_ps"], t.done(lag=1))
                v.tensor_scalar(gqT.rearrange("p j t -> p (j t)"), turn[1][:, 0:2 * P], GLA_DK ** -0.5, None, ALU.mult)\
                    .then_inc(s["gqT_s"], 1)
                wait(dve, s["x_ps"], t.done(lag=1))
                v.tensor_copy(xqT[:].rearrange("p a j t -> p (a j t)"), turn[1][:].bitcast(F16)[:, 4 * P:8 * P])\
                    .then_inc(s["xqT_s"], 1)
                if ended:
                    out_low(4, 6)
                if more:
                    x_mean(n.moved(1))
                dve.wait_ge(s["la_ln"], t.done())
                wait(dve, s["decay_cum"], t.done(lag=1))
                v.scalar_tensor_tensor(out=la[:], in0=decay_ps[:, 0:GLA_KW], scalar=0.0, in1=la_e[:], op0=ALU.min,
                                       op1=ALU.subtract).then_inc(s["la_s"], 1)
                dve.wait_ge(s["la_s"], t.done(3) - 2)
                v.tensor_scalar(la_hi[:], la[:], LA_MIN, None, ALU.max).then_inc(s["la_s"], 1)
                dve.wait_ge(s["la_s"], t.done(3) - 1)
                v.scalar_tensor_tensor(out=la_lo[:], in0=la[:], scalar=LA_MIN, in1=la_hi[:], op0=ALU.max,
                                       op1=ALU.subtract).then_inc(s["la_s"], 1)
                if project:
                    double_keys(n)
                dve.wait_ge(s["s_ps"], t.done())
                if first:
                    for b in range(2):
                        v.memset(score[b][0:CHUNK, :].rearrange("p (h k) -> p h k", h=4)[:, :, CHUNK:P], NEG)\
                            .then_inc(s["first_masked"], 1)
                    dve.wait_ge(s["first_masked"], 2)
                for b in range(2):
                    v.tensor_reduce(s_mx[:, 4 * b:4 * b + 4], score[b][:].rearrange("p (h k) -> p h k", h=4), AX,
                                    ALU.max).then_inc(s["s_mx_s"], 1)
                dve.wait_ge(s["s_mx_s"], t.done(2))
                v.scalar_tensor_tensor(out=s_m, in0=s_mx, scalar=SCALE, in1=sink_b[:], op0=ALU.mult, op1=ALU.max)\
                    .then_inc(s["s_m_s"], 1)
                dve.wait_ge(s["s_m_s"], t.done())
                wait(dve, s["pTa_ps"], t.done(lag=1))
                wait(dve, s["pTb_ps"], t.done(lag=1))
                for b in range(2):
                    v.scalar_tensor_tensor(out=probs[:, 4 * b:4 * b + 4, :],
                                           in0=score[b][:].rearrange("p (h k) -> p h k", h=4), scalar=SCALE,
                                           in1=s_m[:, 4 * b:4 * b + 4].unsqueeze(2).to_broadcast([P, 4, P]),
                                           op0=ALU.mult, op1=ALU.subtract).then_inc(s["s_d_s"], 1)
                wait(dve, s["s_sink_s"], t.done(lag=1))
                v.tensor_tensor(s_diff, sink_b[:], s_m, ALU.subtract).then_inc(s["s_diff_s"], 1)
                if ended:
                    out_low(6, KM)
                if more:
                    x_low(n.moved(1))
                dve.wait_ge(s["s_exp_s"], t.done())
                wait(dve, s["s_gate_s"], t.done(lag=1))
                v.tensor_reduce(s_den2, probs, AX, ALU.add).then_inc(s["s_den_s"], 1)
                dve.wait_ge(s["s_den_s"], t.done())
                dve.wait_ge(s["s_sink_s"], t.done())
                v.tensor_tensor(s_den2, s_den2, s_sink, ALU.add).then_inc(s["s_den2_s"], 1)
                dve.wait_ge(s["s_den2_s"], t.done())
                if project:
                    project_out(XQZ, n)
                if more:
                    hT_low(n.moved(1))
                dve.wait_ge(s["decay_s"], t.done())
                dve.wait_ge(s["gqk_out"], t.done())
                wait(dve, s["kv_done"], t.done(lag=1))
                v.tensor_tensor(k_dec, gqk[:, tp, GLA_KW:2 * GLA_KW], decay[:], ALU.mult).then_inc(s["k_dec_s"], 1)
                dve.wait_ge(s["x_ps"], t.done())
                for b in range(2):
                    v.tensor_reduce(c_mx[:, 2 * b:2 * b + 2], score[b][:].rearrange("p (h k) -> p h k", h=2), AX,
                                    ALU.max).then_inc(s["x_mx_s"], 1)
                v.tensor_scalar(x_factor, xq_un[:, tp:tp + 1], xq_unscale, None, ALU.mult)
                dve.wait_ge(s["x_mx_s"], t.done(2))
                wait(dve, s["xTa_ps"], t.done(lag=1))
                wait(dve, s["xTb_ps"], t.done(lag=1))
                for b in range(2):
                    v.tensor_tensor(xprobs[:, 2 * b:2 * b + 2, :], score[b][:].rearrange("p (h k) -> p h k", h=2),
                                    c_mx[:, 2 * b:2 * b + 2].unsqueeze(2).to_broadcast([P, 2, MEM]),
                                    ALU.subtract).then_inc(s["x_d_s"], 1)
                v.reciprocal(s_rden, s_den2).then_inc(s["s_rden_s"], 1)
                dve.wait_ge(s["pTb_ps"], t.done())
                wait(dve, s["os_ps"], t.done(lag=1))
                v.tensor_copy(probsT[:, 4:8, :].rearrange("p a b -> p (a b)"), turn[1][:]).then_inc(s["pTb_s"], 1)
                dve.wait_ge(s["kv_done"], t.done())
                dve.wait_ge(s["g_end_s"], t.done())
                wait(dve, s["og_ps"], t.done(lag=1))
                for c in range(2):
                    for j in range(2):
                        if c or not first:
                            dve.wait_ge(s["state_s"], (t.done(4) - 2) if c else t.done(4, lag=1))
                        v.scalar_tensor_tensor(out=state[:, c, j, :], in0=state[:, 1 - c, j, :],
                                               scalar=g_end[:, 2 * j + c:2 * j + c + 1],
                                               in1=kv_banks[c][:, j * GLA_DV:(j + 1) * GLA_DV],
                                               op0=ALU.mult, op1=ALU.add).then_inc(s["state_s"], 1)
                dve.wait_ge(s["x_exp_s"], t.done())
                wait(dve, s["x_gate_s"], t.done(lag=1))
                v.tensor_reduce(c_mx, xprobs, AX, ALU.add).then_inc(s["x_den_s"], 1)
                dve.wait_ge(s["x_den_s"], t.done())
                v.reciprocal(c_rden, c_mx).then_inc(s["x_rden_s"], 1)
                if project:
                    project_out(GZ, n)
                wait(dve, s["ox_ps"], t.done(lag=1))
                for half in range(2):
                    dve.wait_ge(s["xT_hi_out"], t.done(2) - 1 + half)
                    cols = slice(4 * half, 4 * half + 4)
                    v.scalar_tensor_tensor(out=xprobsT_lo[:, cols, :].rearrange("p a b -> p (a b)"), in0=turn[half][:],
                                           scalar=PROB_UP, in1=xprobsT_hi[:, cols, :].rearrange("p a b -> p (a b)"),
                                           op0=ALU.mult, op1=ALU.subtract)\
                        .then_inc(s[("xTa_s", "xTb_s")[half]], 1)
                if ending:
                    out_scale()
                    out_low(0, 2)
                if ended:
                    mix_low(Tile(0, 0))
                if project:
                    project_out(SZ, n)
                wait(dve, s["mix_out"], t.done(16, lag=1))
                dve.wait_ge(s["os_ps"], t.done())
                dve.wait_ge(s["s_gate_s"], t.done())
                v.tensor_tensor(mix[:, GLA_W:GLA_W + SWA_W], score[1][:], gates[:, tp, GLA_W:GLA_W + SWA_W],
                                ALU.mult).then_inc(s["mix_s"], 1)
                dve.wait_ge(s["o_ss_s"], t.done(4))
                wait(dve, s["o_rs_s"], t.done(lag=1))
                v.tensor_scalar(o_ms, o_ss, 1.0 / GLA_DV, EPS, ALU.mult, ALU.add).then_inc(s["o_ms_s"], 1)
                dve.wait_ge(s["ox_ps"], t.done())
                dve.wait_ge(s["x_gate_s"], t.done())
                v.tensor_tensor(mix[:, GLA_W + SWA_W:D_MIX], decay_ps[:, 0:XA_W], gates[:, tp, GLA_W + SWA_W:D_MIX],
                                ALU.mult).then_inc(s["mix_s"], 1)
                if ended:
                    mixT_low(Tile(0, 0))
                dve.wait_ge(s["o_rc_s"], t.done())
                for h in range(GLA_H):
                    cols = slice(h * GLA_DV, (h + 1) * GLA_DV)
                    v.scalar_tensor_tensor(out=mix[:, cols], in0=gla_out(h), scalar=o_rc[:, h:h + 1],
                                           in1=gates[:, tp, cols], op0=ALU.mult, op1=ALU.mult)\
                        .then_inc(s["mix_s"], 1)
                if project:
                    pad_values(n)

            iterations(dve, body)

            mix_scale(Tile(0, 1))
            mix_low(Tile(0, 1))

            def out_body(b, more):
                un = m_un_now[:, b.p:b.p + 1]
                dve.wait_ge(s["b_un"], b.done())
                v.tensor_copy(un, m_un[:, b.p:b.p + 1]).then_inc(s["b_un_now"], 1)
                dve.wait_ge(s["b_un_now"], b.done())
                dve.wait_ge(xr_in_s[b.p], b.done_alike())
                wait(dve, s["y_out"], b.done(16, lag=1))
                for h in range(2):
                    dve.wait_ge(s[f"y_ps{h}"], b.done())
                    ps = (proj if h == 0 else (decay_ps, kv_ps))[b.p]
                    cols = slice(h * 512, (h + 1) * 512)
                    v.scalar_tensor_tensor(out=y[:, cols], in0=ps[:], scalar=un, in1=x_in[:, b.p, cols],
                                           op0=ALU.mult, op1=ALU.add).then_inc(s[f"y_res{h}"], 1)
                    if more and h == 0:
                        mixT_low(b.moved(1))
                    if more == 2 and h == 0:
                        mix_scale(b.moved(2))
                        mix_low(b.moved(2))
                dve.wait_ge(s["y_ss"], b.done())
                v.tensor_scalar(x_ms, x_ss, 1.0 / D, EPS, ALU.mult, ALU.add).then_inc(s["y_ms"], 1)
                dve.wait_ge(s["y_rs"], b.done())
                if not isinstance(b.m, int) or b.index() < 2:
                    dve.wait_ge(s["gfin_in"], 16)
                v.scalar_tensor_tensor(out=y, in0=y, scalar=x_rs, in1=g_fin, op0=ALU.mult, op1=ALU.mult)\
                    .then_inc(s["y_fin"], 1)

            out_iterations(dve, out_body)

        @block.tensor
        def _(pe):
            t_ = nc.tensor

            def mm(o, l, r, first, last):
                return t_.matmul(o, lhsT=l, rhs=r, start=first, stop=last)

            def x_turn(t):
                for half, bk, ready, done in ((x_hi, turn[0], "x_hi_s", "xT_hi_ps"),
                                              (x_lo, turn[1], "x_lo_s", "xT_lo_ps")):
                    pe.wait_ge(s[ready], t.done())
                    for k in range(KD):
                        cols = slice(k * P, (k + 1) * P)
                        i = t_.transpose(bk[:].bitcast(F16)[:, cols], half[:, cols], ident16[:])
                    i.then_inc(s[done], 1)

            def project(g, n):
                pe.wait_ge(s["hT_hi_s"], n.done())
                pe.wait_ge(s["hT_lo_s"], n.done())
                ps = proj_bank(n, g)[:, 0:GCOLS[g]]
                two_back = (g - 2) % NG
                wait(pe, s[last_reader[two_back]], read_out(last_reader[two_back], n, lag=1 if g < 2 else 0))
                for k in range(KD):
                    hi = hT_hi[:, n.p, k * P:(k + 1) * P]
                    lo = hT_lo[:, n.p, k * P:(k + 1) * P]
                    mm(ps, hi, w_hi(g)[:, k, :], k == 0, False)
                    mm(ps, hi, w_lo(g)[:, k, :], False, False)
                    i = mm(ps, lo, w_hi(g)[:, k, :], False, k == KD - 1)
                i.then_inc(proj_ps[g], 1)

            pe.wait_ge(s["id_set"], 3)
            x_turn(Tile(0, 0))
            pe.wait_ge(s["mem_scaled"], 2)
            for k in range(KD):
                for b in range(MB):
                    ins = t_.transpose(mem_banks[k // 2][:, ((k % 2) * MB + b) * P:((k % 2) * MB + b + 1) * P],
                                       mem_in[:, b, k * P:(k + 1) * P], ident[:])
                if k % 2:
                    ins.then_inc(s["mem_T"], 1)

            def memory_keys():
                pe.wait_ge(s["mem_T_out"], KD)
                pe.wait_ge(s["memw_in"], 16)
                for j in range(2):
                    for k in range(KD):
                        ins = mm(score[j][:, 0:MEM], mem_w[:, k, j * P:(j + 1) * P], memT[:, k, :], k == 0, k == KD - 1)
                    ins.then_inc(s["memk_ps"], 1)

            def memory_values():
                pe.wait_ge(s["memk_out"], 2)
                for b in range(MB):
                    for k in range(KD):
                        ins = mm(score[b][:, 256:256 + XA_W], memT[:, k, b * P:(b + 1) * P],
                                 mem_w[:, k, XA_W:2 * XA_W], k == 0, k == KD - 1)
                    ins.then_inc(s["memv_ps"], 1)

            def body(n, project_, attend, first=False, last=False):
                t = n.moved(-1)
                tp = t.p
                more = project_ and not (last and project_)
                if not attend:
                    for g in range(NG):
                        split_through(pe, g)
                        project(g, n)
                        if g == KVL:
                            memory_keys()
                            memory_values()
                        if g == GV:
                            x_turn(n.moved(1))
                    return
                if project_:
                    project(KVL, n)
                if first:
                    pe.wait_ge(s["hT_hi_s"], 2)
                    pe.wait_ge(s["hT_lo_s"], 2)
                    pe.wait_ge(s["v_split_s"], 4)
                pe.wait_ge(s["k_twice_s"], t.done())
                pe.wait_ge(s["kvl_out"], t.done())
                wait(pe, s["xTa_s"], t.done(lag=1))
                for h in range(SWA_KV):
                    i = t_.transpose(turn[0][:, h * P:(h + 1) * P],
                                     k_twice[:, h].rearrange("p a b -> p (a b)"), ident[:])
                i = t_.transpose(turn[0][0:GLA_LR, 2 * P:3 * P], qkv[:, tp, SWA_W + 2 * SWA_KVW:], ident[:])
                i.then_inc(s["kT_ps"], 1)
                pe.wait_ge(s["rope_s"], t.done(2))
                wait(pe, s["xTb_s"], t.done(lag=1))
                for i2 in range(SWA_H // 2):
                    i = t_.transpose(turn[1][:, i2 * P:(i2 + 1) * P], qkv[:, tp, i2 * P:(i2 + 1) * P], ident[:])
                i.then_inc(s["qT_ps"], 1)
                if project_:
                    project(SQ, n)
                pe.wait_ge(s["kT_s"], t.done(3))
                pe.wait_ge(s["lrT_s"], t.done())
                pe.wait_ge(s["qT_s"], t.done())
                pe.wait_ge(s["gqk_out"], t.done())
                pe.wait_ge(s["xq_out"], t.done(XQ_STEPS))
                for j in range(2):
                    t_.transpose(turn[1][:, j * P:(j + 1) * P], gqk[:, tp, j * P:(j + 1) * P], ident[:])
                for j in range(2):
                    for a in range(2):
                        at = (4 + 2 * a + j) * P
                        i = t_.transpose(turn[1][:].bitcast(F16)[:, at:at + P], xq[:, a, j * P:(j + 1) * P], ident16[:])
                i.then_inc(s["gqT_ps"], 1)
                wait(pe, s["mix_s"], t.done(6, lag=1))
                mm(decay_ps[:, 0:GLA_KW], lrT[0:GLA_LR + 1, :], wa2[0:GLA_LR + 1, :], True, True)\
                    .then_inc(s["lr_ps"], 1)
                if project_:
                    project(GQK, n)
                for i2 in range(SWA_H // 2):
                    for c in range(2):
                        for b in range(2):
                            rows, frames = slice(b * HD, (b + 1) * HD), slice(c * CHUNK, (c + 1) * CHUNK)
                            keys = (kT if c else kT_first[:, tp])[rows, (2 * i2 + b) // (SWA_H // SWA_KV)]
                            i = mm(score[b][frames, i2 * P:(i2 + 1) * P], qT[rows, i2, frames], keys, True, True)
                i.then_inc(s["s_ps"], 1)
                if project_:
                    project(XQZ, n)
                pe.wait_ge(s["la_s"], t.done(3))
                mm(decay_ps[:, 0:GLA_KW], later16[:], la_hi[:], True, False)
                mm(decay_ps[:, 0:GLA_KW], later16[:], la_lo[:], False, True)
                for j in range(2):
                    ends, dims = kv_ps[:, GLA_KW + 2 * j:GLA_KW + 2 * j + 2], slice(j * P, (j + 1) * P)
                    mm(ends, la_hi[:, dims], halves[:], True, False)
                    i = mm(ends, la_lo[:, dims], halves[:], False, True)
                i.then_inc(s["decay_cum"], 1)
                pe.wait_ge(s["s_d_s"], t.done(2))
                pe.wait_ge(s["xqT_s"], t.done())
                for j in range(XA_H // 2):
                    for a, k_half in ((0, memT_k_hi), (0, memT_k_lo), (1, memT_k_hi)):
                        for b in range(2):
                            rows = slice(b * HD, (b + 1) * HD)
                            i = mm(score[b][:, j * MEM:(j + 1) * MEM], xqT[rows, a, j, :], k_half[rows, j, :],
                                   a == 0 and k_half is memT_k_hi, a == 1)
                i.then_inc(s["x_ps"], 1)
                if more:
                    pe.wait_ge(s["gqT_s"], t.done())
                    x_turn(n.moved(1))
                if project_:
                    project(GV, n)
                if more:
                    pe.wait_ge(s["hT_hi_s"], n.done(lag=-1))
                    pe.wait_ge(s["hT_lo_s"], n.done(lag=-1))
                pe.wait_ge(s["gqT_s"], t.done())
                pe.wait_ge(s["s_exp_s"], t.done())
                for half, done in ((0, "pTa_ps"), (1, "pTb_ps")):
                    if half:
                        pe.wait_ge(s["k_dec_s"], t.done())
                        if not project_ or first:
                            pe.wait_ge(s["gv_out"], t.done())
                        pe.wait_ge(s["g_end_s"], t.done())
                        wait(pe, s["state_s"], t.done(4, lag=1))
                    for h in range(4):
                        i = t_.transpose(turn[half][:, h * P:(h + 1) * P], probs[:, 4 * half + h, :], ident[:])
                    i.then_inc(s[done], 1)
                for j in range(2):
                    for b in range(2):
                        for c in range(2):
                            h, frames = 2 * j + b, slice(c * CHUNK, (c + 1) * CHUNK)
                            i = mm(kv_banks[c][b * GLA_DK:(b + 1) * GLA_DK, j * GLA_DV:(j + 1) * GLA_DV],
                                   k_dec[frames, h * GLA_DK:(h + 1) * GLA_DK],
                                   gv[frames, h * GLA_DV:(h + 1) * GLA_DV], True, True)
                i.then_inc(s["kv_done"], 1)
                if project_:
                    project(GZ, n)
                pe.wait_ge(s["x_exp_s"], t.done())
                pe.wait_ge(s["pTa_s"], t.done())
                pe.wait_ge(s["pTb_s"], t.done())
                for half, done in ((0, "xTa_ps"), (1, "xTb_ps")):
                    for i4 in range(4):
                        h, b = 2 * half + i4 // MB, i4 % MB
                        i = t_.transpose(turn[half][:, i4 * P:(i4 + 1) * P], xprobs[:, h, b * P:(b + 1) * P], ident[:])
                    i.then_inc(s[done], 1)
                pe.wait_ge(s["v_win_s"], t.done(2))
                for slot, h in enumerate(even_first(SWA_H)):
                    kv = slice((h // 4) * HD, (h // 4 + 1) * HD)
                    mm(score[1][0:CHUNK, h * HD:(h + 1) * HD], probsT[:, slot, 0:CHUNK], v_win[:, tp, kv], True, True)
                    i = mm(score[1][CHUNK:P, h * HD:(h + 1) * HD], probsT[:, slot, CHUNK:P],
                           qkv[:, tp, SWA_W + SWA_KVW + kv.start:SWA_W + SWA_KVW + kv.stop], True, True)
                i.then_inc(s["os_ps"], 1)
                if project_:
                    project(SZ, n)
                pe.wait_ge(s["xTa_s"], t.done())
                pe.wait_ge(s["xTb_s"], t.done())
                pe.wait_ge(s["g_end_s"], t.done())
                pe.wait_ge(s["state_s"], t.done(4))
                for slot, h in enumerate(even_first(XA_H)):
                    cols = slice(h * HD, (h + 1) * HD)
                    for b in range(MB):
                        hi, lo = xprobsT_hi[:, slot * MB + b, :], xprobsT_lo[:, slot * MB + b, :]
                        mm(decay_ps[:, cols], hi, mem_v_hi[:, b, cols], b == 0, False)
                        mm(decay_ps[:, cols], hi, mem_v_lo[:, b, cols], False, False)
                        i = mm(decay_ps[:, cols], lo, mem_v_hi[:, b, cols], False, b == MB - 1)
                i.then_inc(s["ox_ps"], 1)
                for j in range(2):
                    for c in range(2):
                        for b in range(2):
                            rows, frames = slice(b * GLA_DK, (b + 1) * GLA_DK), slice(c * CHUNK, (c + 1) * CHUNK)
                            i = mm(gla_out(2 * j + b)[frames], gqT[rows, j, frames], state[rows, c, j, :], True, True)
                i.then_inc(s["og_ps"], 1)

            iterations(pe, lambda n, project, attend, first=False, last=False:
                       body(n, project, attend, first, last))

            def mix_turn(b):
                for half, banks, ready, done, free in ((m_hi, turn, "b_hi", "bT_hi", "bT_hi_s"),
                                                       (m_lo, low_banks(b), "b_lo", "bT_lo", "bT_lo_s")):
                    pe.wait_ge(s[ready], b.done())
                    wait(pe, s[free], b.done(2, lag=1))
                    for k in range(KM):
                        i = t_.transpose(banks[k // 8][:].bitcast(F16)[:, (k % 8) * P:(k % 8 + 1) * P],
                                         half[:, k * P:(k + 1) * P], ident16[:])
                    i.then_inc(s[done], 1)

            pe.wait_ge(s["sz_out"], TILES)
            mix_turn(Tile(0, 0))
            pe.wait_ge(s["w_hi_s"], HIGH_A * NG + KM)
            pe.wait_ge(s["w_lo_s"], KD * NG + KM)

            def out_body(b, more):
                pe.wait_ge(s["bT_hi_s"], b.done(2))
                pe.wait_ge(s["bT_lo_s"], b.done(2))
                for h in range(2):
                    ps = (proj if h == 0 else (decay_ps, kv_ps))[b.p]
                    wait(pe, s[f"y_res{h}"], b.done(lag=2))
                    cols = slice(h * 512, (h + 1) * 512)
                    for k in range(KM):
                        hi = mT_hi[b.p][:, k * P:(k + 1) * P]
                        lo = mT_lo[b.p][:, k * P:(k + 1) * P]
                        mm(ps[:], hi, wo_hi[:, k, cols], k == 0, False)
                        mm(ps[:], hi, wo_lo[:, k, cols], False, False)
                        i = mm(ps[:], lo, wo_hi[:, k, cols], False, k == KM - 1)
                    i.then_inc(s[f"y_ps{h}"], 1)
                    if h == 0 and isinstance(b.m, int) and b.index() == 0:
                        pe.wait_ge(s["mix_s"], 6 * TILES)
                    if h == 0 and more:
                        mix_turn(b.moved(1))

            out_iterations(pe, out_body)


_OUT = (1, SEQ, D)


def kernel(**inputs):
    import numpy as _np
    import concourse.bacc as _bacc
    from concourse import mybir as _mybir
    from concourse.bass_utils import run_bass_kernel_spmd as _run

    c = _np.ascontiguousarray
    rows = lambda a, k: c(_np.asarray(a).reshape(k, P, -1).transpose(1, 0, 2))
    w_in = _np.asarray(inputs["w_in"])[0]
    arrays = {
        "x": c(_np.asarray(inputs["x"])[0]),
        "mem": c(_np.asarray(inputs["mem"])[0]),
        "pos": c(_np.asarray(inputs["positions"])[0].reshape(TILES, P).T),
        "g_norm": c(_np.asarray(inputs["g_norm"]).reshape(KD, P).T),
        "w_a2": c(_np.asarray(inputs["w_a2"])[0]),
        "b_a": c(_np.asarray(inputs["b_a"])),
        "g_gla": c(_np.asarray(inputs["g_gla"]).reshape(GLA_DV, 1)),
        "sinks": c(_np.asarray(inputs["sinks"])[0].reshape(SWA_H // 2, 2).T.reshape(SWA_H)),
        "g_mem": c(_np.asarray(inputs["g_mem"]).reshape(KD, P).T),
        "w_mem": rows(inputs["w_mem_kv"], KD),
        "w_out": rows(inputs["w_out"], KM),
        "g_final": c(_np.asarray(inputs["g_final"])),
    }
    for i, names in enumerate(GROUPS):
        cols = _np.concatenate([w_in[:, _starts[n]:_starts[n] + _width[n]] for n in names], axis=1)
        arrays[f"w_group{i}"] = rows(cols, KD).reshape(P, -1)
    nc = _bacc.Bacc("TRN2", target_bir_lowering=False, num_devices=1, dynamic_dma_scratch_size=4096)
    args = {n: nc.dram_tensor(n, a.shape, _mybir.dt.from_np(a.dtype), kind="ExternalInput").ap()
            for n, a in arrays.items()}
    out = nc.dram_tensor("out", (SEQ, D), F32, kind="ExternalOutput").ap()
    build_kernel(nc, args["x"], args["mem"], args["pos"], args["g_norm"],
                 [args[f"w_group{i}"] for i in range(NG)], args["w_a2"], args["b_a"], args["g_gla"],
                 args["sinks"], args["g_mem"], args["w_mem"], args["w_out"], args["g_final"], out)
    r = _run(nc, [arrays], core_ids=[0])
    return r.results[0]["out"].reshape(_OUT)
```
